# Optimizing a Trainium2 kernel written in Bass

```python
import math
import jax, jax.numpy as jnp
from jax import lax
import numpy as np

D_MODEL = 1024
BATCH = 1
SEQ = 2048
DEPTH = 1
DEC_BATCH = 8
DEC_SEQ = 4
PAST_LEN = 512
PAGE_SIZE = 128

H_A = 4
DH_A = 64
DV_A = 2 * DH_A
W_A = H_A * DV_A
H_B = 8
DH_B = 64
W_B = H_B * DH_B
Q_BLOCK = 128
EPS = 1e-6
NEG_INF = -1e30
FORGET_BIAS = 3.0
_SIZES = (2 * H_A * DH_A, 2 * H_A * DH_A, W_A, W_A, W_B, W_B, W_B, H_B, W_B, D_MODEL, D_MODEL)
D_IN = sum(_SIZES)

kernel_name = 'diff_fox_gated_hybrid_step'

def _rms(x):
    xf = x.astype(jnp.float32)
    return (xf * lax.rsqrt(jnp.mean(xf * xf, axis=-1, keepdims=True) + EPS)).astype(x.dtype)

def _alibi_slopes():
    return jnp.asarray(2.0 ** (-8.0 * np.arange(1, H_A + 1) / H_A), jnp.float32)

def _lambda_init(layer):
    return 0.8 - 0.6 * math.exp(-0.3 * layer)

def _layer_inputs(x, c, w_ada, b_ada, w_in, b_f, g_q_a, g_k_a, g_q_b, g_k_b):
    B, T, _ = x.shape
    shift, scale, gate_res = jnp.split(jax.nn.silu(c) @ w_ada + b_ada, 3, axis=-1)
    h = _rms(x) * (1 + scale[:, None, :]) + shift[:, None, :]
    z = h @ w_in
    q_a, k_a, v_a, gate_a, q_b, k_b, v_b, f_b, gate_b, m_a, m_b = jnp.split(
        z, np.cumsum(_SIZES)[:-1].tolist(), axis=-1)
    q_a = _rms(q_a.reshape(B, T, 2, H_A, DH_A)) * g_q_a
    k_a = _rms(k_a.reshape(B, T, 2, H_A, DH_A)) * g_k_a
    v_a = v_a.reshape(B, T, H_A, DV_A)
    q_b = _rms(q_b.reshape(B, T, H_B, DH_B)) * g_q_b
    k_b = _rms(k_b.reshape(B, T, H_B, DH_B)) * g_k_b
    v_b = v_b.reshape(B, T, H_B, DH_B)
    logf = jax.nn.log_sigmoid((f_b + b_f).astype(jnp.float32))
    return q_a, k_a, v_a, gate_a, q_b, k_b, v_b, logf, gate_b, m_a, m_b, gate_res

def _diff_attn(q, k, v, q_pos, k_pos, slopes, lam):
    s = jnp.einsum('bqmhd,bkmhd->bmhqk', q, k, preferred_element_type=jnp.float32) * (DH_A ** -0.5)
    dist = (q_pos[:, None] - k_pos[None, :]).astype(jnp.float32)
    s = jnp.where(dist >= 0, s - slopes[:, None, None] * dist, NEG_INF)
    p = jax.nn.softmax(s, axis=-1)
    p = p[:, 0] - lam * p[:, 1]
    return jnp.einsum('bhqk,bkhd->bqhd', p.astype(v.dtype), v)

def _forgetting_attn(q, k, v, F_q, F_k, q_pos, k_pos):
    s = jnp.einsum('bqhd,bkhd->bhqk', q, k, preferred_element_type=jnp.float32) * (DH_B ** -0.5)
    s = s + jnp.swapaxes(F_q, 1, 2)[..., :, None] - jnp.swapaxes(F_k, 1, 2)[..., None, :]
    s = jnp.where(q_pos[:, None] >= k_pos[None, :], s, NEG_INF)
    p = jax.nn.softmax(s, axis=-1)
    return jnp.einsum('bhqk,bkhd->bqhd', p.astype(v.dtype), v)

def _prompt_mix(q_a, k_a, v_a, q_b, k_b, v_b, logf, slopes, lam):
    B, T = q_a.shape[:2]
    F = jnp.cumsum(logf, axis=1)
    k_pos = jnp.arange(T, dtype=jnp.int32)

    def block(i):
        start = i * Q_BLOCK
        q_pos = start + jnp.arange(Q_BLOCK, dtype=jnp.int32)
        qa = lax.dynamic_slice_in_dim(q_a, start, Q_BLOCK, axis=1)
        qb = lax.dynamic_slice_in_dim(q_b, start, Q_BLOCK, axis=1)
        Fq = lax.dynamic_slice_in_dim(F, start, Q_BLOCK, axis=1)
        return (_diff_attn(qa, k_a, v_a, q_pos, k_pos, slopes, lam),
                _forgetting_attn(qb, k_b, v_b, Fq, F, q_pos, k_pos))

    o_a, o_b = lax.map(block, jnp.arange(T // Q_BLOCK, dtype=jnp.int32))
    o_a = jnp.moveaxis(o_a, 0, 1).reshape(B, T, H_A, DV_A)
    o_b = jnp.moveaxis(o_b, 0, 1).reshape(B, T, H_B, DH_B)
    return o_a, o_b

def _gather_pages(pool, page_table):
    g = pool[page_table]
    return g.reshape(g.shape[0], g.shape[1] * g.shape[2], *g.shape[3:])

def _sample_mix(q_a, k_a, v_a, q_b, k_b, v_b, logf, pool_a_k, pool_a_v, pool_b_k, pool_b_v,
                pool_b_logf, page_table, slopes, lam):
    T = q_a.shape[1]
    ka = jnp.concatenate([_gather_pages(pool_a_k, page_table), k_a], axis=1)
    va = jnp.concatenate([_gather_pages(pool_a_v, page_table), v_a], axis=1)
    kb = jnp.concatenate([_gather_pages(pool_b_k, page_table), k_b], axis=1)
    vb = jnp.concatenate([_gather_pages(pool_b_v, page_table), v_b], axis=1)
    F_past = jnp.cumsum(_gather_pages(pool_b_logf, page_table).astype(jnp.float32), axis=1)
    F_new = F_past[:, -1:, :] + jnp.cumsum(logf, axis=1)
    F_k = jnp.concatenate([F_past, F_new], axis=1)
    past = ka.shape[1] - T
    q_pos = past + jnp.arange(T, dtype=jnp.int32)
    k_pos = jnp.arange(past + T, dtype=jnp.int32)
    o_a = _diff_attn(q_a, ka, va, q_pos, k_pos, slopes, lam)
    o_b = _forgetting_attn(q_b, kb, vb, F_new, F_k, q_pos, k_pos)
    return o_a, o_b

def _merge(x, o_a, o_b, gate_a, gate_b, m_a, m_b, gate_res, g_sub_a, w_out_a, w_out_b, w_o, lam_init):
    B, T = x.shape[:2]
    o_a = _rms(o_a) * g_sub_a * (1.0 - lam_init)
    y_a = (o_a.reshape(B, T, W_A) * jax.nn.silu(gate_a)) @ w_out_a
    y_b = (o_b.reshape(B, T, W_B) * jax.nn.silu(gate_b)) @ w_out_b
    y = (jax.nn.sigmoid(m_a) * y_a + jax.nn.sigmoid(m_b) * y_b) @ w_o
    return x + gate_res[:, None, :] * y

def setup_inputs(seed: int = 0) -> dict:
    key = jax.random.key(seed)
    ks = jax.random.split(key, 32)
    n_pages = PAST_LEN // PAGE_SIZE
    n_used = DEC_BATCH * n_pages
    n_pool = n_used + (n_used + 3) // 4

    def nrm(k, shape, s=1.0):
        return s * jax.random.normal(k, shape, jnp.float32)

    return {
        'x_prompt': nrm(ks[0], (BATCH, SEQ, D_MODEL)),
        'x_sample': nrm(ks[1], (DEC_BATCH, DEC_SEQ, D_MODEL)),
        'cache_a_k': nrm(ks[2], (DEPTH, n_pool, PAGE_SIZE, 2, H_A, DH_A)),
        'cache_a_v': nrm(ks[3], (DEPTH, n_pool, PAGE_SIZE, H_A, DV_A)),
        'cache_b_k': nrm(ks[4], (DEPTH, n_pool, PAGE_SIZE, H_B, DH_B)),
        'cache_b_v': nrm(ks[5], (DEPTH, n_pool, PAGE_SIZE, H_B, DH_B)),
        'cache_b_logf': jax.nn.log_sigmoid(FORGET_BIAS + nrm(ks[6], (DEPTH, n_pool, PAGE_SIZE, H_B))),
        'page_table': jax.random.permutation(ks[7], n_pool)[:n_used].reshape(DEC_BATCH, n_pages).astype(jnp.int32),
        'c_prompt': nrm(ks[8], (BATCH, D_MODEL)),
        'c_sample': nrm(ks[9], (DEC_BATCH, D_MODEL)),
        'w_ada': nrm(ks[10], (DEPTH, D_MODEL, 3 * D_MODEL), D_MODEL ** -0.5),
        'b_ada': nrm(ks[11], (DEPTH, 3 * D_MODEL), 0.1),
        'w_in': nrm(ks[12], (DEPTH, D_MODEL, D_IN), D_MODEL ** -0.5),
        'b_f': FORGET_BIAS + nrm(ks[13], (DEPTH, H_B), 0.5),
        'g_q_a': 1.0 + nrm(ks[14], (DEPTH, DH_A), 0.02),
        'g_k_a': 1.0 + nrm(ks[15], (DEPTH, DH_A), 0.02),
        'g_q_b': 1.0 + nrm(ks[16], (DEPTH, DH_B), 0.02),
        'g_k_b': 1.0 + nrm(ks[17], (DEPTH, DH_B), 0.02),
        'lambda_q1': nrm(ks[18], (DEPTH, DH_A), 0.1),
        'lambda_k1': nrm(ks[19], (DEPTH, DH_A), 0.1),
        'lambda_q2': nrm(ks[20], (DEPTH, DH_A), 0.1),
        'lambda_k2': nrm(ks[21], (DEPTH, DH_A), 0.1),
        'g_sub_a': 1.0 + nrm(ks[22], (DEPTH, DV_A), 0.02),
        'w_out_a': nrm(ks[23], (DEPTH, W_A, D_MODEL), W_A ** -0.5),
        'w_out_b': nrm(ks[24], (DEPTH, W_B, D_MODEL), W_B ** -0.5),
        'w_o': nrm(ks[25], (DEPTH, D_MODEL, D_MODEL), D_MODEL ** -0.5),
    }

def reference(x_prompt, x_sample, cache_a_k, cache_a_v, cache_b_k, cache_b_v, cache_b_logf, page_table,
              c_prompt, c_sample, w_ada, b_ada, w_in, b_f, g_q_a, g_k_a, g_q_b, g_k_b,
              lambda_q1, lambda_k1, lambda_q2, lambda_k2, g_sub_a, w_out_a, w_out_b, w_o):
    slopes = _alibi_slopes()
    xp, xs = x_prompt, x_sample
    st = {n: [] for n in ('kap', 'vap', 'kbp', 'vbp', 'lfp', 'kas', 'vas', 'kbs', 'vbs', 'lfs')}
    for l in range(DEPTH):
        lam_init = _lambda_init(l)
        lam = (jnp.exp(jnp.sum(lambda_q1[l].astype(jnp.float32) * lambda_k1[l].astype(jnp.float32)))
               - jnp.exp(jnp.sum(lambda_q2[l].astype(jnp.float32) * lambda_k2[l].astype(jnp.float32)))
               + lam_init)
        proj = (w_ada[l], b_ada[l], w_in[l], b_f[l], g_q_a[l], g_k_a[l], g_q_b[l], g_k_b[l])
        out = (g_sub_a[l], w_out_a[l], w_out_b[l], w_o[l], lam_init)

        q_a, k_a, v_a, ga, q_b, k_b, v_b, lf, gb, ma, mb, gr = _layer_inputs(xp, c_prompt, *proj)
        o_a, o_b = _prompt_mix(q_a, k_a, v_a, q_b, k_b, v_b, lf, slopes, lam)
        xp = _merge(xp, o_a, o_b, ga, gb, ma, mb, gr, *out)
        st['kap'].append(k_a); st['vap'].append(v_a); st['kbp'].append(k_b)
        st['vbp'].append(v_b); st['lfp'].append(lf)

        q_a, k_a, v_a, ga, q_b, k_b, v_b, lf, gb, ma, mb, gr = _layer_inputs(xs, c_sample, *proj)
        o_a, o_b = _sample_mix(q_a, k_a, v_a, q_b, k_b, v_b, lf, cache_a_k[l], cache_a_v[l], cache_b_k[l],
                               cache_b_v[l], cache_b_logf[l], page_table, slopes, lam)
        xs = _merge(xs, o_a, o_b, ga, gb, ma, mb, gr, *out)
        st['kas'].append(k_a); st['vas'].append(v_a); st['kbs'].append(k_b)
        st['vbs'].append(v_b); st['lfs'].append(lf)
    return (xp, xs,
            jnp.stack(st['kap']), jnp.stack(st['vap']), jnp.stack(st['kbp']), jnp.stack(st['vbp']), jnp.stack(st['lfp']),
            jnp.stack(st['kas']), jnp.stack(st['vas']), jnp.stack(st['kbs']), jnp.stack(st['vbs']), jnp.stack(st['lfs']))


_drawn_inputs = setup_inputs


def setup_inputs(seed=0):
    import zlib

    import numpy as np

    out = dict(_drawn_inputs(seed))
    spreads = {}
    factors = {'cache_b_logf': 4.401,
     'g_q_a': 8.0,
     'g_k_a': 3.031,
     'g_q_b': 8.0,
     'g_k_b': 2.83,
     'lambda_q2': 5.886,
     'lambda_k2': 4.073,
     'g_sub_a': 8.0}
    for name, (base, spread) in spreads.items():
        noise = np.random.default_rng([zlib.crc32(name.encode()), seed]).standard_normal(out[name].shape)
        drawn = base * np.exp(spread * noise) if base else spread * noise
        out[name] = __import__('jax').numpy.asarray(drawn.astype(out[name].dtype))
    for name, factor in factors.items():
        out[name] = (out[name] * factor).astype(out[name].dtype)
    return out
```

```python
from contextlib import ExitStack

import numpy as np

import concourse.bass as bass
from concourse import mybir

P = 128
F32 = mybir.dt.float32
F32R = mybir.dt.float32r
BF16 = mybir.dt.bfloat16
I32 = mybir.dt.int32
ALU = mybir.AluOpType
ACT = mybir.ActivationFunctionType
AX = mybir.AxisListType
ds = bass.ds

D = 1024
KD = D // P
SEQ = 2048
NB, NT = 8, 4
SR = NB * NT
HA, HB, DH, DVA = 4, 8, 64, 128
W = 512
NPG, PG = 4, 128
PAST = NPG * PG
TILES = SEQ // P
HALF = TILES // 2
GROUP = 4
NU = 2 * HA + HB
EPS = 1e-6
NEG = -1e30
LAM_INIT = 0.8 - 0.6
SLOPES = [2.0 ** (-8.0 * (h + 1) / HA) for h in range(HA)]
C_QA, C_KA, C_VA, C_GA = 0, W, 2 * W, 3 * W
C_QB, C_KB, C_VB, C_F = 4 * W, 5 * W, 6 * W, 7 * W
C_GB = C_F + HB
C_M = C_GB + W


class Tally:

    def __init__(self, sem, base=0):
        self.sem, self.base, self.n = sem, base, 0

    def inc(self, ins):
        self.n += 1
        ins.then_inc(self.sem, 1)

    def wait(self, eng):
        eng.wait_ge(self.sem, self.base + self.n)


class Store:
    pass


def program(nc, t):
    with ExitStack() as ctx:
        k = Store()
        k.nc, k.t, k.ctx = nc, t, ctx
        persistent(k)
        constants(k)
        modulation(k)
        for half in range(2):
            with ExitStack() as c2:
                rows = HALF * P + (SR if half else 0)
                k.h_hi = c2.enter_context(nc.sbuf_tensor(f"h_hi{half}", [P, KD, rows], F32R))
                k.h_lo = c2.enter_context(nc.sbuf_tensor(f"h_lo{half}", [P, KD, rows], F32R))
                normalise(k, half)
                project(k, half)
        forget(k)
        maxima(k)
        attention(k, "a")
        attention(k, "b")
        recycle(k)
        sample(k)
        merge(k)


def tools(k, ctx, tag):
    nc = k.nc

    def sb(name, shape, dt=F32):
        return ctx.enter_context(nc.sbuf_tensor(f"{tag}_{name}", shape, dt))

    def ps(name, shape, dt=F32):
        return ctx.enter_context(nc.psum_tensor(f"{tag}_{name}", shape, dt))

    def sem(name):
        k.sems.append(nc.alloc_semaphore(f"{tag}_{name}"))
        return k.sems[-1]

    return sb, ps, sem


def recycle(k):
    with k.nc.Block() as block:
        @block.gpsimd
        def _(pool):
            k.nc.clear_and_free_semaphores(k.sems)
    k.sems = []


def persistent(k):
    k.sems = []
    nc = k.nc
    sb, _, _ = tools(k, k.ctx, "keep")

    def dram(name, shape, dt=F32):
        return nc.dram_tensor(f"scratch_{name}", shape, dt, kind="Internal").ap()

    k.q_hi, k.q_lo = dram("q_hi", [NU // 2, P, SEQ]), dram("q_lo", [NU // 2, P, SEQ])
    k.k_hi, k.k_lo = dram("k_hi", [NU // 2, P, SEQ]), dram("k_lo", [NU // 2, P, SEQ])
    k.gates = dram("gates", [SEQ + SR, 2 * W])
    k.mixes = dram("mixes", [SEQ + SR, 2 * D])
    k.ada_gate = dram("ada_gate", [SR + 1, D])
    k.bias_row = dram("bias_row", [2, NU * TILES, P])
    k.bias_col = dram("bias_col", [NU, P, TILES])
    k.neg_max = dram("neg_max", [2, NU * TILES, P])
    k.o_a, k.o_b = dram("o_a", [SEQ + SR, W]), dram("o_b", [SEQ + SR, W])

    k.ident = sb("ident", [P, P])
    k.ident_b = sb("ident_b", [P, P], BF16)
    k.mask_k = sb("mask_k", [P, P], BF16)
    k.mask_q = sb("mask_q", [P, P], BF16)
    k.neg_half = sb("neg_half", [P, 8])
    k.neg_lam = sb("neg_lam", [P, 1])
    k.shiftT = sb("shiftT", [P, KD, SR + 1])
    k.scaleT = sb("scaleT", [P, KD, SR + 1])
    k.logf = sb("logf", [P, TILES + 1, HB])
    k.max_shift = sb("max_shift", [P, NU, TILES])
    k.qT_s = sb("qT_s", [P, 2, 4, SR])
    k.kT_s = sb("kT_s", [P, 2, 4, SR])
    k.v_s = sb("v_s", [SR, 2, W])


def constants(k):
    nc, t = k.nc, k.t
    with ExitStack() as ctx:
        sb, ps, sem = tools(k, ctx, "const")
        lam_in = sb("lam_in", [P, 4, DH])
        prod = sb("prod", [P, 2, DH])
        dots = sb("dots", [P, 2])
        exps = sb("exps", [P, 2])
        loaded, filled, dots_done, exps_done = (sem(n) for n in ("loaded", "filled", "dots", "exps"))
        steps = sem("steps")
        with nc.Block() as block:
            @block.sync
            def _(sp):
                for n, name in enumerate(("lambda_q1", "lambda_k1", "lambda_q2", "lambda_k2")):
                    sp.dma_start(lam_in[:, n, :], t[name].to_broadcast([P, DH])).then_inc(loaded, 16)

            @block.gpsimd
            def _(pool):
                nc.gpsimd.memset(k.neg_half[:], -0.5)
                nc.gpsimd.memset(k.logf[:], 0.0)
                nc.gpsimd.memset(k.ident[:], 0.0).then_inc(filled, 1)
                nc.gpsimd.memset(k.ident_b[:], 0.0).then_inc(filled, 1)
                nc.gpsimd.memset(k.mask_k[:], 0.0).then_inc(filled, 1)
                nc.gpsimd.memset(k.mask_q[:], 0.0).then_inc(filled, 1)
                pool.wait_ge(filled, 4)
                for m in (k.ident, k.ident_b):
                    nc.gpsimd.affine_select(out=m[:], in_=m[:], compare_op=ALU.not_equal, fill=1.0,
                                            base=0, pattern=[[-1, P]], channel_multiplier=1)
                nc.gpsimd.affine_select(out=k.mask_k[:], in_=k.mask_k[:], compare_op=ALU.is_ge, fill=NEG,
                                        base=0, pattern=[[-1, P]], channel_multiplier=1)
                nc.gpsimd.affine_select(out=k.mask_q[:], in_=k.mask_q[:], compare_op=ALU.is_ge, fill=NEG,
                                        base=0, pattern=[[1, P]], channel_multiplier=-1)

            @block.vector
            def _(dve):
                step = Tally(steps)
                dve.wait_ge(loaded, 64)
                pairs = lam_in[:].rearrange("p (n two) d -> p n two d", two=2)
                step.inc(nc.vector.tensor_tensor(prod[:], pairs[:, :, 0, :], pairs[:, :, 1, :], ALU.mult))
                step.wait(dve)
                nc.vector.reduce_sum(dots[:], prod[:], AX.X).then_inc(dots_done, 1)
                dve.wait_ge(exps_done, 1)
                step.inc(nc.vector.tensor_tensor(k.neg_lam[:], exps[:, 1:2], exps[:, 0:1], ALU.subtract))
                step.wait(dve)
                nc.vector.tensor_scalar(k.neg_lam[:], k.neg_lam[:], -LAM_INIT, None, ALU.add)

            @block.scalar
            def _(act):
                act.wait_ge(dots_done, 1)
                nc.scalar.activation(exps[:], dots[:], ACT.Exp).then_inc(exps_done, 1)


def modulation(k):
    nc, t = k.nc, k.t
    RING = 3
    NC = 3 * D // 512
    R = SR + 1
    with ExitStack() as ctx:
        sb, ps, sem = tools(k, ctx, "ada")
        c_in = sb("c_in", [R, D])
        c_silu = sb("c_silu", [R, D])
        cT = sb("cT", [P, KD, R])
        w = sb("w", [P, RING, 3 * D])
        bias = sb("bias", [R, 3 * D])
        ada = sb("ada", [R, 3 * D])
        acc = ps("acc", [R, NC, 512])
        ps_t = ps("ps_t", [P, 2, 512])
        c_loaded, b_loaded, stored = sem("c_loaded"), sem("b_loaded"), sem("stored")
        w_loaded = [sem(f"w_loaded{i}") for i in range(RING)]
        sig_done, silu_done, cT_ready, cT_copied = (sem(n) for n in ("sig", "silu", "cT_ready", "cT_copied"))
        w_used, ada_done, turned = (sem(n) for n in ("w_used", "ada_done", "turned"))
        with nc.Block() as block:
            @block.sync
            def _(sp):
                for s in range(NT):
                    sp.dma_start(c_in[s:SR:NT, :], t["c_sample"]).then_inc(c_loaded, 16)
                sp.dma_start(c_in[SR:R, :], t["c_prompt"]).then_inc(c_loaded, 16)
                for kt in range(KD):
                    if kt >= RING:
                        sp.wait_ge(w_used, kt - RING + 1)
                    sp.dma_start(w[:, kt % RING, :], t["w_ada"][0, kt * P:(kt + 1) * P, :]).then_inc(w_loaded[kt % RING], 16)
                    if kt == 1:
                        sp.dma_start(bias[:], t["b_ada"].to_broadcast([R, 3 * D])).then_inc(b_loaded, 16)
                sp.wait_ge(ada_done, 2)
                sp.dma_start(k.ada_gate, ada[:, 2 * D:3 * D]).then_inc(stored, 16)
                sp.wait_ge(stored, 16)

            @block.scalar
            def _(act):
                act.wait_ge(c_loaded, 80)
                nc.scalar.activation(c_silu[:], c_in[:], ACT.Sigmoid).then_inc(sig_done, 1)

            @block.vector
            def _(dve):
                dve.wait_ge(sig_done, 1)
                nc.vector.tensor_tensor(c_silu[:], c_silu[:], c_in[:], ALU.mult).then_inc(silu_done, 1)
                dve.wait_ge(cT_ready, 1)
                nc.vector.tensor_copy(cT[:].rearrange("p a b -> p (a b)"), ps_t[:, 0, 0:KD * R]).then_inc(cT_copied, 1)
                dve.wait_ge(b_loaded, 16)
                dve.wait_ge(w_used, KD)
                nc.vector.tensor_tensor(ada[:], acc[:].rearrange("p a b -> p (a b)"), bias[:], ALU.add).then_inc(ada_done, 1)
                dve.wait_ge(ada_done, 1)
                nc.vector.tensor_scalar(ada[:, D:2 * D], ada[:, D:2 * D], 1.0, None, ALU.add).then_inc(ada_done, 1)
                for n, out in enumerate((k.shiftT, k.scaleT)):
                    dve.wait_ge(turned, n + 1)
                    nc.vector.tensor_copy(out[:].rearrange("p a b -> p (a b)"), ps_t[:, n, 0:KD * R])

            @block.tensor
            def _(pe):
                pe.wait_ge(silu_done, 1)
                for kt in range(KD):
                    last = nc.tensor.transpose(ps_t[:, 0, kt * R:(kt + 1) * R], c_silu[:, kt * P:(kt + 1) * P], k.ident[0:R, 0:R])
                last.then_inc(cT_ready, 1)
                pe.wait_ge(cT_copied, 1)
                for kt in range(KD):
                    pe.wait_ge(w_loaded[kt % RING], 16 * (kt // RING + 1))
                    for n in range(NC):
                        last = nc.tensor.matmul(acc[:, n, :], cT[:, kt, :], w[:, kt % RING, n * 512:(n + 1) * 512],
                                                start=(kt == 0), stop=(kt == KD - 1))
                    last.then_inc(w_used, 1)
                pe.wait_ge(ada_done, 2)
                for n in range(2):
                    for kt in range(KD):
                        c = n * D + kt * P
                        last = nc.tensor.transpose(ps_t[:, n, kt * R:(kt + 1) * R], ada[:, c:c + P], k.ident[0:R, 0:R])
                    last.then_inc(turned, 1)


def normalise(k, half):
    nc, t = k.nc, k.t
    NG = HALF // GROUP
    x_v = t["x_prompt"][0].rearrange("(g t p) d -> g p t d", t=GROUP, p=P)
    xs_v = t["x_sample"].rearrange("b t d -> (b t) d")
    groups = [(g, P, GROUP) for g in range(NG)] + ([(NG, SR, 1)] if half else [])
    with ExitStack() as ctx:
        sb, ps, sem = tools(k, ctx, f"norm{half}")
        x_in = sb("x_in", [P, 2, GROUP, D])
        xn = sb("xn", [P, GROUP, D])
        junk = sb("junk", [P, 2, D])
        ss = sb("ss", [P, 2, GROUP])
        rstd = sb("rstd", [P, 2, GROUP])
        hf = sb("hf", [P, 2, 512])
        ps_t = ps("ps_t", [P, 4, 512])
        loaded = [sem("loaded0"), sem("loaded1")]
        ss_done, rstd_done, xn_done, turned, hf_done, lo_done = (
            sem(n) for n in ("ss_done", "rstd_done", "xn_done", "turned", "hf_done", "lo_done"))
        with nc.Block() as block:
            @block.sync
            def _(sp):
                for g, pn, tn in groups:
                    if g >= 2:
                        sp.wait_ge(xn_done, g - 1)
                    src = x_v[half * NG + g] if tn == GROUP else xs_v
                    dst = x_in[0:pn, g % 2, :, :] if tn == GROUP else x_in[0:pn, g % 2, 0, :]
                    sp.dma_start(dst, src).then_inc(loaded[g % 2], 16)

            @block.gpsimd
            def _(pool):
                for g, pn, tn in groups:
                    pool.wait_ge(rstd_done, 2 * g + 1)
                    nc.gpsimd.tensor_tensor(rstd[0:pn, g % 2, 0:tn], rstd[0:pn, g % 2, 0:tn], k.neg_half[0:pn, 0:tn], ALU.pow).then_inc(rstd_done, 1)

            @block.scalar
            def _(act):
                n = 0
                for g, pn, tn in groups:
                    act.wait_ge(loaded[g % 2], 16 * (g // 2 + 1))
                    if g >= 2:
                        act.wait_ge(rstd_done, 2 * (g - 2) + 1)
                    for j in range(tn):
                        q = g * GROUP + j
                        if q >= 2:
                            act.wait_ge(ss_done, q - 1)
                        nc.scalar.activation(junk[0:pn, q % 2, :], x_in[0:pn, g % 2, j, :], ACT.Square,
                                             accum_out=ss[0:pn, g % 2, j:j + 1]).then_inc(ss_done, 1)
                    if tn == GROUP:
                        for kt in range(KD):
                            act.wait_ge(turned, n + 1)
                            if n >= 2:
                                act.wait_ge(lo_done, n - 1)
                            hi = k.h_hi[:, kt, g * 512:(g + 1) * 512]
                            src = ps_t[:, n % 4, :]
                            sc, sh = k.scaleT[:, kt, SR:SR + 1], k.shiftT[:, kt, SR:SR + 1]
                            nc.scalar.activation(hf[:, n % 2, :], src, ACT.Identity, scale=sc, bias=sh).then_inc(hf_done, 1)
                            nc.scalar.activation(hi, src, ACT.Identity, scale=sc, bias=sh).then_inc(hf_done, 1)
                            n += 1

            @block.vector
            def _(dve):
                n, m, seen = 0, 0, 0
                for g, pn, tn in groups:
                    seen += tn
                    dve.wait_ge(ss_done, seen)
                    nc.vector.tensor_scalar(rstd[0:pn, g % 2, 0:tn], ss[0:pn, g % 2, 0:tn], 1.0 / D, EPS, ALU.mult, ALU.add).then_inc(rstd_done, 1)
                    dve.wait_ge(rstd_done, 2 * g + 2)
                    if g >= 1:
                        dve.wait_ge(turned, n)
                    for j in range(tn):
                        last = nc.vector.tensor_scalar(xn[0:pn, j, :], x_in[0:pn, g % 2, j, :],
                                                       rstd[0:pn, g % 2, j:j + 1], None, ALU.mult)
                    last.then_inc(xn_done, 1)
                    for kt in range(KD):
                        cols = slice(g * 512, g * 512 + pn * tn)
                        if tn == GROUP:
                            m += 2
                            dve.wait_ge(hf_done, m)
                        else:
                            dve.wait_ge(turned, n + 1)
                            nc.vector.tensor_tensor(hf[:, n % 2, 0:SR], ps_t[:, n % 4, 0:SR], k.scaleT[:, kt, 0:SR], ALU.mult).then_inc(hf_done, 1)
                            m += 1
                            dve.wait_ge(hf_done, m)
                            nc.vector.tensor_tensor(hf[:, n % 2, 0:SR], hf[:, n % 2, 0:SR], k.shiftT[:, kt, 0:SR], ALU.add).then_inc(hf_done, 1)
                            m += 1
                            dve.wait_ge(hf_done, m)
                            nc.vector.tensor_copy(k.h_hi[:, kt, cols], hf[:, n % 2, 0:SR]).then_inc(hf_done, 1)
                            m += 1
                            dve.wait_ge(hf_done, m)
                        nc.vector.tensor_tensor(k.h_lo[:, kt, cols], hf[:, n % 2, 0:pn * tn],
                                                k.h_hi[:, kt, cols].bitcast(F32), ALU.subtract).then_inc(lo_done, 1)
                        n += 1

            @block.tensor
            def _(pe):
                n = 0
                for g, pn, tn in groups:
                    pe.wait_ge(xn_done, g + 1)
                    for kt in range(KD):
                        if n >= 4:
                            pe.wait_ge(lo_done, n - 3)
                        for j in range(tn):
                            last = nc.tensor.transpose(ps_t[:, n % 4, j * P:j * P + pn], xn[0:pn, j, kt * P:(kt + 1) * P],
                                                       k.ident[0:pn, 0:pn])
                        last.then_inc(turned, 1)
                        n += 1


def split_product(nc, out, left, right, terms, first=True, last=True):
    for n, (lt, rt) in enumerate(terms):
        ins = nc.tensor.matmul(out, left(*lt), right(*rt), start=first and n == 0, stop=last and n == len(terms) - 1)
    return ins


HI, LO = 0, 1


def three_terms(kts):
    return [((lp, kt), (rp, kt)) for kt in kts for lp, rp in ((HI, HI), (HI, LO), (LO, HI))]


def project(k, half):
    nc, t = k.nc, k.t
    T = HALF + half
    R = 4 if T % 2 == 0 else 3
    row0 = half * HALF * P
    w_in = t["w_in"][0]
    g_names = ("g_q_a", "g_k_a", "g_q_b", "g_k_b")
    chunks = [("gate", 0, C_GA), ("gate", 1, C_GB), ("v", 0, C_VA), ("v", 1, C_VB),
              ("k", 0, C_KA), ("k", 1, C_KB), ("q", 0, C_QA), ("q", 1, C_QB)]
    NM = 4
    tiles = [(c, j, kind, b) for c, (kind, b, _) in enumerate(chunks) for j in range(T)]
    M0 = NM * T

    def rows_of(j):
        return P if j < HALF else SR

    def dram_rows(ap, j):
        r = row0 + j * P if j < HALF else SEQ
        return ap[r:r + rows_of(j)]

    def out_rows(name, j):
        if j < HALF:
            r = row0 + j * P
            return t[f"{name}_prompt"][r:r + P, :]
        return t[f"{name}_sample"]

    turned_tiles = [n for n, (_, _, kind, _) in enumerate(tiles) if kind in "qk"]
    turn_index = {n: i for i, n in enumerate(turned_tiles)}
    parts_index = {n: i for i, n in enumerate(x for x in turned_tiles if tiles[x][1] < HALF)}
    dve_tiles = [n for n, (_, _, kind, _) in enumerate(tiles) if kind != "v"]
    dve_before = {n: sum(x <= n for x in dve_tiles) for n in range(-2, len(tiles))}
    stored_before, seen = [], [NM * T // R + 1] * R
    for n, (_, _, kind, _) in enumerate(tiles):
        stored_before.append(list(seen))
        if kind != "q":
            seen[n % R] += 1
    assert M0 % R == 0

    with ExitStack() as ctx:
        sb, ps, sem = tools(k, ctx, f"proj{half}")
        w_raw = sb("w_raw", [P, KD, 512])
        w_parts = [sb("w_hi", [P, 2, KD, 512], F32R), sb("w_lo", [P, 2, KD, 512], F32R)]
        wf_raw = sb("wf_raw", [P, KD, HB])
        wf_parts = [sb("wf_hi", [P, KD, HB], F32R), sb("wf_lo", [P, KD, HB], F32R)]
        gains = sb("gains", [P, 4, DH])
        z_sb = sb("z_sb", [P, 2, 512])
        sq = sb("sq", [P, 2, 512])
        ss = sb("ss", [P, 8])
        rstd = sb("rstd", [P, 8])
        out = sb("out", [P, R, 512])
        turned_parts = [sb("t_hi", [P, 2, 4, P], F32R), sb("t_lo", [P, 2, 4, P], F32R)]
        z = ps("z", [P, R, 512])
        ps_t = ps("ps_t", [P, 2, 4, P])
        ps_f = ps("ps_f", [P, 512])
        w_loaded = [sem(f"w_loaded{i}") for i in range(KD)]
        g_loaded, wf_loaded = sem("g_loaded"), sem("wf_loaded")
        stored = [sem(f"stored{i}") for i in range(R)]
        parts_stored = [sem("parts_stored0"), sem("parts_stored1")]
        (w_split, z_done, z_read, norm_done, norm_steps, turned, t_hi_done, t_done, wf_split, f_done,
         mean_done, rstd_done) = (sem(n) for n in (
             "w_split", "z_done", "z_read", "norm_done", "norm_steps", "turned",
                             "t_hi_done", "t_done", "wf_split", "f_done", "mean_done", "rstd_done"))
        h_parts = [k.h_hi, k.h_lo]

        def hT(part, kt, j):
            return h_parts[part][:, kt, j * P:j * P + rows_of(j)]

        with nc.Block() as block:
            def store_parts(sp, n):
                _, j, kind, b = tiles[n]
                i, r = parts_index[n], row0 + j * P
                sp.wait_ge(t_done, turn_index[n] + 1)
                for part, dst in zip(turned_parts, (k.q_hi, k.q_lo) if kind == "q" else (k.k_hi, k.k_lo)):
                    sp.dma_start(dst[4 * b:4 * b + 4, :, r:r + P].rearrange("u p r -> p u r"),
                                 part[:, i % 2, :, :].bitcast(F32)).then_inc(parts_stored[i % 2], 16)

            def turned_high(act, n):
                i = parts_index[n]
                act.wait_ge(turned, turn_index[n] + 1)
                if i >= 2:
                    act.wait_ge(parts_stored[i % 2], 32 * (i // 2))
                nc.scalar.activation(turned_parts[HI][:, i % 2, :, :], ps_t[:, turn_index[n] % 2, :, :],
                                     ACT.Copy).then_inc(t_hi_done, 1)

            def turned_low(dve, n):
                _, j, kind, b = tiles[n]
                q = turn_index[n]
                if n in parts_index:
                    i = parts_index[n]
                    dve.wait_ge(t_hi_done, i + 1)
                    nc.vector.tensor_tensor(turned_parts[LO][:, i % 2, :, :], ps_t[:, q % 2, :, :],
                                            turned_parts[HI][:, i % 2, :, :].bitcast(F32), ALU.subtract).then_inc(t_done, 1)
                else:
                    dve.wait_ge(turned, q + 1)
                    dst = (k.qT_s if kind == "q" else k.kT_s)[:, b, :, :]
                    nc.vector.tensor_copy(dst, ps_t[:, q % 2, :, 0:SR]).then_inc(t_done, 1)

            @block.gpsimd
            def _(pool):
                for i, n in enumerate(turned_tiles):
                    pn = rows_of(tiles[n][1])
                    pool.wait_ge(mean_done, i + 1)
                    nc.gpsimd.tensor_tensor(rstd[0:pn, :], rstd[0:pn, :], k.neg_half[0:pn, :], ALU.pow).then_inc(rstd_done, 1)

            @block.sync
            def _(sp):
                for s in range(R):
                    sp.sem_inc(stored[s], 16)
                sp.dma_start(wf_raw[:], w_in[:, C_F:C_F + HB].rearrange("(a p) n -> p a n", p=P)).then_inc(wf_loaded, 16)
                for n, name in enumerate(g_names):
                    sp.dma_start(gains[:, n, :], t[name].to_broadcast([P, DH])).then_inc(g_loaded, 16)
                def load_w(c, kt, col):
                    if not isinstance(c, int) or c > 0:
                        sp.wait_ge(w_split, (c - 1) * KD + (kt + 1))
                    sp.dma_start(w_raw[:, kt, :], w_in[kt * P:(kt + 1) * P, col]).then_inc(w_loaded[kt], 16)

                for c in range(2):
                    for kt in range(KD):
                        load_w(c, kt, slice(C_M + c * 512, C_M + (c + 1) * 512))
                with sp.Fori(0, NM // 2) as i:
                    for c in range(2):
                        first, then = C_M + (c + 2) * 512, chunks[c][2]
                        for kt in range(KD):
                            load_w(i * 2 + (c + 2), kt, ds(first + i * (then - first), 512))
                        for j in range(T):
                            n = c * T + j
                            sp.wait_ge(z_read, i * (2 * T) + (n + 1 + R))
                            sp.dma_start(dram_rows(k.mixes, j)[:, ds(i * 1024 + c * 512, 512)],
                                         out[0:rows_of(j), n % R, :]).then_inc(stored[n % R], 16)
                for n, (c, j, kind, b) in enumerate(tiles):
                    pn = rows_of(j)
                    src = out[0:pn, n % R, :]
                    if kind == "v":
                        sp.wait_ge(z_read, M0 + n + 1 + R)
                        sp.dma_start(out_rows("v_ab"[0:2] + "ab"[b], j), src).then_inc(stored[n % R], 16)
                    else:
                        sp.wait_ge(norm_done, dve_before[n])
                        if kind == "gate":
                            sp.dma_start(dram_rows(k.gates, j)[:, b * W:(b + 1) * W], src).then_inc(stored[n % R], 16)
                        elif kind == "k":
                            sp.dma_start(out_rows("k_" + "ab"[b], j), src).then_inc(stored[n % R], 16)
                    if n - 1 in parts_index:
                        store_parts(sp, n - 1)
                    if c + 2 < len(chunks) and j < KD:
                        col = chunks[c + 2][2]
                        load_w(NM + c + 2, j, slice(col, col + 512))
                if len(tiles) - 1 in parts_index:
                    store_parts(sp, len(tiles) - 1)
                for s in range(R):
                    sp.wait_ge(stored[s], 16 * seen[s])
                for s in range(2):
                    sp.wait_ge(parts_stored[s], 32 * len(range(s, len(parts_index), 2)))

            @block.scalar
            def _(act):
                act.sem_inc(z_read, R)
                with act.Fori(0, NM // 2) as i:
                    for n in range(2 * T):
                        pn = rows_of(n % T)
                        act.wait_ge(z_done, i * (2 * T) + (n + 1))
                        act.wait_ge(stored[n % R], 16 * (i * (2 * T // R) + (n // R + 1)))
                        nc.scalar.activation(out[0:pn, n % R, :], z[0:pn, n % R, :], ACT.Sigmoid).then_inc(z_read, 1)
                for n, (c, j, kind, b) in enumerate(tiles):
                    pn = rows_of(j)
                    src = z[0:pn, n % R, :]
                    act.wait_ge(z_done, M0 + n + 1)
                    if kind == "v":
                        act.wait_ge(stored[n % R], 16 * stored_before[n][n % R])
                        if n >= R and tiles[n - R][2] != "v":
                            act.wait_ge(norm_done, dve_before[n - R])
                        if j == HALF:
                            nc.scalar.activation(k.v_s[:, b, :], src, ACT.Copy)
                        nc.scalar.activation(out[0:pn, n % R, :], src, ACT.Copy).then_inc(z_read, 1)
                    else:
                        if n >= 2 and dve_before[n - 2]:
                            act.wait_ge(norm_done, dve_before[n - 2])
                        nc.scalar.activation(z_sb[0:pn, n % 2, :], src, ACT.Copy)
                        func = ACT.Sigmoid if kind == "gate" else ACT.Square
                        nc.scalar.activation(sq[0:pn, n % 2, :], src, func).then_inc(z_read, 1)
                    if n - 1 in parts_index:
                        turned_high(act, n - 1)
                if len(tiles) - 1 in parts_index:
                    turned_high(act, len(tiles) - 1)

            @block.vector
            def _(dve):
                step = Tally(norm_steps)
                dve.wait_ge(wf_loaded, 16)
                nc.vector.tensor_copy(wf_parts[HI][:], wf_raw[:]).then_inc(wf_split, 1)
                dve.wait_ge(wf_split, 1)
                nc.vector.tensor_tensor(wf_parts[LO][:], wf_raw[:], wf_parts[HI][:].bitcast(F32), ALU.subtract).then_inc(wf_split, 1)

                def split(c, par, kt):
                    dve.wait_ge(w_loaded[kt], 16 * (c + 1))
                    step.inc(nc.vector.tensor_copy(w_parts[HI][:, par, kt, :], w_raw[:, kt, :]))
                    step.wait(dve)
                    nc.vector.tensor_tensor(w_parts[LO][:, par, kt, :], w_raw[:, kt, :],
                                            w_parts[HI][:, par, kt, :].bitcast(F32), ALU.subtract).then_inc(w_split, 1)

                for c in range(2):
                    for kt in range(KD):
                        split(c, c, kt)
                with dve.Fori(1, NM // 2) as i:
                    step = Tally(norm_steps, 2 * KD * i)
                    for c in range(2):
                        dve.wait_ge(z_done, i * (2 * T) + (c - 1) * T)
                        for kt in range(KD):
                            split(i * 2 + c, c, kt)
                step = Tally(norm_steps, NM * KD)
                dve.wait_ge(f_done, 1)
                nc.vector.tensor_copy(k.logf[:, half * HALF:(half + 1) * HALF, :].rearrange("p a b -> p (a b)"), ps_f[:, 0:HALF * HB])
                if half:
                    nc.vector.tensor_copy(k.logf[0:SR, TILES, :], ps_f[0:SR, HALF * HB:(HALF + 1) * HB])
                dve.wait_ge(z_done, (NM - 1) * T)
                for kt in range(KD):
                    split(NM, NM % 2, kt)
                dve.wait_ge(g_loaded, 64)
                for n in (0, 2):
                    nc.vector.tensor_scalar(gains[:, n, :], gains[:, n, :], DH ** -0.5, None, ALU.mult)
                for n, (c, j, kind, b) in enumerate(tiles):
                    pn = rows_of(j)
                    if kind != "v":
                        dve.wait_ge(z_read, M0 + n + 1 + R)
                        dve.wait_ge(stored[n % R], 16 * stored_before[n][n % R])
                        if n - R in turn_index:
                            dve.wait_ge(turned, turn_index[n - R] + 1)
                        dst = out[0:pn, n % R, :]
                        zi, si = z_sb[0:pn, n % 2, :], sq[0:pn, n % 2, :]
                    if kind == "gate":
                        nc.vector.tensor_tensor(dst, zi, si, ALU.mult).then_inc(norm_done, 1)
                    elif kind != "v":
                        step.inc(nc.vector.reduce_sum(ss[0:pn, :], si.rearrange("p (u d) -> p u d", d=DH), AX.X))
                        step.wait(dve)
                        nc.vector.tensor_scalar(rstd[0:pn, :], ss[0:pn, :], 1.0 / DH, EPS, ALU.mult, ALU.add).then_inc(mean_done, 1)
                    if n - 1 in turn_index:
                        turned_low(dve, n - 1)
                    if c + 1 < len(chunks) and j < KD:
                        if j == 0:
                            dve.wait_ge(z_done, M0 + c * T)
                        split(NM + c + 1, (NM + c + 1) % 2, j)
                    if kind in "qk":
                        z3 = zi.rearrange("p (u d) -> p u d", d=DH)
                        dve.wait_ge(rstd_done, turn_index[n] + 1)
                        step.inc(nc.vector.tensor_tensor(z3, z3, rstd[0:pn, :].unsqueeze(2).to_broadcast([pn, 8, DH]), ALU.mult))
                        step.wait(dve)
                        gain = gains[0:pn, 2 * b + (kind == "k"), :].unsqueeze(1).to_broadcast([pn, 8, DH])
                        nc.vector.tensor_tensor(dst.rearrange("p (u d) -> p u d", d=DH), z3, gain, ALU.mult).then_inc(norm_done, 1)
                if len(tiles) - 1 in turn_index:
                    turned_low(dve, len(tiles) - 1)

            @block.tensor
            def _(pe):
                pe.wait_ge(wf_split, 2)
                for j in range(T):
                    last = split_product(nc, ps_f[0:rows_of(j), j * HB:(j + 1) * HB], lambda part, kt: hT(part, kt, j),
                                         lambda part, kt: wf_parts[part][:, kt, :], three_terms(range(KD)))
                last.then_inc(f_done, 1)

                def tile(par, j, bank):
                    split_product(nc, z[0:rows_of(j), bank, :], lambda part, kt: hT(part, kt, j),
                                  lambda part, kt: w_parts[part][:, par, kt, :],
                                  three_terms(range(KD))).then_inc(z_done, 1)

                def turn(n):
                    pn = rows_of(tiles[n][1])
                    q = turn_index[n]
                    pe.wait_ge(norm_done, dve_before[n])
                    if q >= 2:
                        pe.wait_ge(t_done, q - 1)
                    for p in range(4):
                        last = nc.tensor.transpose(ps_t[:, q % 2, p, 0:pn], out[0:pn, n % R, p * P:(p + 1) * P],
                                                   k.ident[0:pn, 0:pn])
                    last.then_inc(turned, 1)

                with pe.Fori(0, NM // 2) as i:
                    for c in range(2):
                        pe.wait_ge(w_split, i * (2 * KD) + (c + 1) * KD)
                        for j in range(T):
                            n = c * T + j
                            pe.wait_ge(z_read, i * (2 * T) + (n + 1))
                            tile(c, j, n % R)
                for n, (c, j, kind, b) in enumerate(tiles):
                    if j == 0:
                        pe.wait_ge(w_split, (NM + c + 1) * KD)
                    pe.wait_ge(z_read, M0 + n + 1)
                    tile((NM + c) % 2, j, n % R)
                    if n - 1 in turn_index:
                        turn(n - 1)
                if len(tiles) - 1 in turn_index:
                    turn(len(tiles) - 1)


def forget(k):
    nc, t = k.nc, k.t
    ALL = TILES + 1
    with ExitStack() as ctx:
        sb, ps, sem = tools(k, ctx, "forget")
        bf = sb("bf", [P, HB])
        x = sb("x", [P, ALL, HB])
        ab = sb("ab", [P, ALL, HB])
        tri = sb("tri", [P, P])
        ones = sb("ones", [P, P])
        pos = sb("pos", [P, TILES], I32)
        group_pos = sb("group_pos", [P, TILES], I32)
        incl = sb("incl", [P, HB, TILES])
        before = sb("before", [P, HB, TILES])
        bias = sb("bias", [P, NU, TILES])
        bias_c = sb("bias_c", [P, NU, TILES])
        rows_hi = sb("rows_hi", [P, 2, P], F32R)
        rows_lo = sb("rows_lo", [P, 2, P], F32R)
        sums = ps("sums", [P, 2, 512])
        ps_t = ps("ps_t", [P, 2, 512])
        loaded, made, filled, act_step, dve_step = (sem(n) for n in ("loaded", "made", "filled", "act_step", "dve_step"))
        logf_done, summed, bias_done, turned, hi_done, lo_done, stored = (
            sem(n) for n in ("logf_done", "summed", "bias_done", "turned", "hi_done", "lo_done", "stored"))
        x_done = sem("x_done")
        with nc.Block() as block:
            @block.gpsimd
            def _(pool):
                nc.gpsimd.memset(ones[:], 1.0)
                nc.gpsimd.memset(tri[:], 1.0).then_inc(filled, 1)
                pool.wait_ge(filled, 1)
                nc.gpsimd.affine_select(out=tri[:], in_=tri[:], compare_op=ALU.is_ge, fill=0.0, base=0,
                                        pattern=[[1, P]], channel_multiplier=-1)
                nc.gpsimd.iota(pos[:], pattern=[[P, TILES]], base=0, channel_multiplier=1)
                nc.gpsimd.iota(group_pos[:], pattern=[[512, TILES // GROUP], [0, GROUP]], base=0,
                               channel_multiplier=0).then_inc(made, 1)

            @block.sync
            def _(sp):
                sp.dma_start(bf[:], t["b_f"].to_broadcast([P, HB])).then_inc(loaded, 16)
                sp.wait_ge(logf_done, 1)
                sp.dma_start(t["logf_prompt"].rearrange("(t p) h -> p t h", p=P), k.logf[:, 0:TILES, :]).then_inc(stored, 16)
                sp.dma_start(t["logf_sample"], k.logf[0:SR, TILES, :]).then_inc(stored, 16)
                sp.wait_ge(bias_done, 2)
                sp.dma_start(k.bias_col.rearrange("u p t -> p u t"), bias_c[:]).then_inc(stored, 16)
                sp.wait_ge(lo_done, 1)
                for part, rows in ((HI, rows_hi), (LO, rows_lo)):
                    sp.dma_start(k.bias_row[part].rearrange("(g r) p -> r g p", g=2), rows[:].bitcast(F32)).then_inc(stored, 16)
                sp.wait_ge(stored, 80)

            @block.scalar
            def _(act):
                step = Tally(act_step)
                act.wait_ge(x_done, 1)
                step.inc(nc.scalar.activation(ab[:], x[:], ACT.Abs))
                step.wait(act)
                step.inc(nc.scalar.activation(ab[:], ab[:], ACT.Exp, scale=-1.0))
                step.wait(act)
                step.inc(nc.scalar.activation(ab[:], ab[:], ACT.Ln, bias=1.0))
                act.wait_ge(turned, 1)
                nc.scalar.activation(rows_hi[:], ps_t[:, :, 0:P], ACT.Copy).then_inc(hi_done, 1)

            @block.vector
            def _(dve):
                step = Tally(dve_step)
                dve.wait_ge(loaded, 16)
                nc.vector.tensor_tensor(x[:], k.logf[:], bf[:].unsqueeze(1).to_broadcast([P, ALL, HB]), ALU.add).then_inc(x_done, 1)
                dve.wait_ge(act_step, 3)
                step.inc(nc.vector.tensor_scalar(x[:], x[:], 0.0, None, ALU.min))
                step.wait(dve)
                nc.vector.tensor_tensor(k.logf[:], x[:], ab[:], ALU.subtract).then_inc(logf_done, 1)
                dve.wait_ge(made, 1)
                for u in range(2 * HA):
                    slope = SLOPES[u % HA]
                    step.inc(nc.vector.tensor_scalar(bias[:, u, :], pos[:], slope, None, ALU.mult))
                    nc.vector.tensor_scalar(k.max_shift[:, u, :], group_pos[:], slope, None, ALU.mult)
                step.inc(nc.vector.memset(k.max_shift[:, 2 * HA:NU, :], 0.0))
                step.wait(dve)
                for u in range(2 * HA):
                    nc.vector.tensor_scalar(bias_c[:, u, :], bias[:, u, :], -SLOPES[u % HA] * (SEQ - 512), None, ALU.add)
                dve.wait_ge(summed, 2)
                within = sums[:, 0, 0:TILES * HB].rearrange("p (t h) -> p h t", h=HB)
                total = sums[:, 1, 0:TILES * HB].rearrange("p (t h) -> p h t", h=HB)
                for h in range(HB):
                    last = nc.vector.tensor_tensor_scan(incl[:, h, :], ones[:, 0:TILES], total[:, h, :], 0.0, ALU.mult, ALU.add)
                step.inc(last)
                step.wait(dve)
                step.inc(nc.vector.tensor_tensor(before[:], total, incl[:], ALU.subtract))
                step.wait(dve)
                nc.vector.tensor_tensor(bias[:, 2 * HA:NU, :], before[:], within, ALU.subtract).then_inc(bias_done, 1)
                dve.wait_ge(bias_done, 1)
                nc.vector.tensor_copy(bias_c[:, 2 * HA:NU, :], bias[:, 2 * HA:NU, :]).then_inc(bias_done, 1)
                dve.wait_ge(hi_done, 1)
                nc.vector.tensor_tensor(rows_lo[:], ps_t[:, :, 0:P], rows_hi[:].bitcast(F32), ALU.subtract).then_inc(lo_done, 1)

            @block.tensor
            def _(pe):
                pe.wait_ge(made, 1)
                pe.wait_ge(logf_done, 1)
                rhs = k.logf[:, 0:TILES, :].rearrange("p t h -> p (t h)")
                for n, m in enumerate((tri, ones)):
                    nc.tensor.matmul(sums[:, n, 0:TILES * HB], m[:], rhs, start=True, stop=True).then_inc(summed, 1)
                pe.wait_ge(bias_done, 1)
                flat = bias[:].rearrange("p u t -> p (u t)")
                for g in range(2):
                    last = nc.tensor.transpose(ps_t[:, g, 0:P], flat[:, g * P:(g + 1) * P], k.ident[:])
                last.then_inc(turned, 1)


def maxima(k):
    nc = k.nc
    A = DH + 2
    q_u = k.q_hi.rearrange("a (b d) s -> (a b) d s", b=2)
    k_u = k.k_hi.rearrange("a (b d) s -> (a b) d s", b=2)
    bias_u = k.bias_row.rearrange("c (u t) p -> u c (t p)", t=TILES)
    N = 2 * TILES
    with ExitStack() as ctx:
        sb, ps, sem = tools(k, ctx, "max")
        q = [sb(f"q{s}", [A, SEQ], F32R) for s in range(2)]
        kb = [sb(f"kb{s}", [A, SEQ], F32R) for s in range(2)]
        ones = sb("ones", [A, SEQ])
        top = sb("top", [P, NU, TILES])
        neg = sb("neg", [P, NU, TILES])
        rows = [sb("rows_hi", [P, 2, P], F32R), sb("rows_lo", [P, 2, P], F32R)]
        s_ps = ps("s_ps", [P, 2, 4 * 512])
        loaded = [sem("loaded0"), sem("loaded1")]
        ones_done, s_done, max_done, neg_done, turned, hi_done, lo_done, stored = (
            sem(n) for n in ("ones_done", "s_done", "max_done", "neg_done", "turned", "hi_done", "lo_done", "stored"))
        with nc.Block() as block:
            @block.sync
            def _(sp):
                def load(u, s):
                    sp.dma_start(q[s][0:DH, :].bitcast(F32).unsqueeze(1), q_u[ds(u, 1)].rearrange("u d s -> d u s")).then_inc(loaded[s], 16)
                    sp.dma_start(kb[s][0:DH, :].bitcast(F32).unsqueeze(1), k_u[ds(u, 1)].rearrange("u d s -> d u s")).then_inc(loaded[s], 16)
                    sp.dma_start(kb[s][DH:A, :].bitcast(F32).unsqueeze(1), bias_u[ds(u, 1)].rearrange("u c s -> c u s")).then_inc(loaded[s], 16)
                for s in range(2):
                    load(s, s)
                with sp.Fori(1, NU // 2) as i:
                    for s in range(2):
                        sp.wait_ge(s_done, i * N + ((s + 1) * TILES - N))
                        load(i * 2 + s, s)
                sp.wait_ge(lo_done, 1)
                for part in range(2):
                    sp.dma_start(k.neg_max[part].rearrange("(g r) p -> r g p", g=2), rows[part][:].bitcast(F32)).then_inc(stored, 16)
                sp.wait_ge(stored, 32)

            @block.gpsimd
            def _(pool):
                nc.gpsimd.memset(ones[DH:A, :], 1.0).then_inc(ones_done, 1)

            @block.scalar
            def _(act):
                act.wait_ge(ones_done, 1)
                for s in range(2):
                    nc.scalar.activation(q[s][DH:A, :], ones[DH:A, :], ACT.Copy).then_inc(ones_done, 1)
                act.wait_ge(turned, 1)
                nc.scalar.activation(rows[HI][:], s_ps[:, 0, 0:2 * P].rearrange("p (g c) -> p g c", g=2), ACT.Copy).then_inc(hi_done, 1)

            @block.vector
            def _(dve):
                dve.sem_inc(max_done, 1)
                with dve.Fori(0, NU // 2) as i:
                    for n in range(N):
                        s, qt = n // TILES, n % TILES
                        dve.wait_ge(s_done, i * N + (n + 1))
                        nc.vector.reduce_max(top[:, ds(i * 2 + s, 1), qt], s_ps[:, n % 2, 0:(qt + 1) * P], AX.X).then_inc(max_done, 1)
                dve.wait_ge(max_done, NU * TILES + 1)
                nc.vector.tensor_tensor(neg[:], k.max_shift[:], top[:], ALU.subtract).then_inc(neg_done, 1)
                dve.wait_ge(hi_done, 1)
                nc.vector.tensor_tensor(rows[LO][:], s_ps[:, 0, 0:2 * P].rearrange("p (g c) -> p g c", g=2),
                                        rows[HI][:].bitcast(F32), ALU.subtract).then_inc(lo_done, 1)

            @block.tensor
            def _(pe):
                pe.wait_ge(ones_done, 3)
                with pe.Fori(0, NU // 2) as i:
                    for n in range(N):
                        s, qt = n // TILES, n % TILES
                        if qt == 0:
                            pe.wait_ge(loaded[s], i * 48 + 48)
                        pe.wait_ge(max_done, i * N + max(n, 1))
                        cols = (qt + 1) * P
                        for c0 in range(0, cols, 512):
                            w = min(512, cols - c0)
                            diag = c0 + w == cols
                            last = nc.tensor.matmul(s_ps[:, n % 2, c0:c0 + w], q[s][:, qt * P:(qt + 1) * P], kb[s][:, c0:c0 + w],
                                                    start=True, stop=not diag)
                        last = nc.tensor.matmul(s_ps[:, n % 2, cols - P:cols], k.ident_b[:], k.mask_k[:], start=False, stop=True)
                        last.then_inc(s_done, 1)
                pe.wait_ge(neg_done, 1)
                flat = neg[:].rearrange("p u t -> p (u t)")
                for g in range(2):
                    last = nc.tensor.transpose(s_ps[:, 0, g * P:(g + 1) * P], flat[:, g * P:(g + 1) * P], k.ident[:])
                last.then_inc(turned, 1)


def attention(k, branch):
    nc, t = k.nc, k.t
    A = branch == "a"
    dv = DVA if A else DH
    VW = 2 + 2 * dv
    v_in = t[f"v_{branch}_prompt"].rearrange("(t p) c -> p t c", p=P)
    o_out = (k.o_a if A else k.o_b)[0:SEQ].rearrange("(t p) c -> p t c", p=P)
    first = [0, HA] if A else [2 * HA, 2 * HA + 1]
    stride = 1 if A else 2
    TURNS = 4
    unit = lambda ap: ap.rearrange("a (b d) s -> (a b) d s", b=2)
    q_hi, q_lo, k_hi, k_lo = (unit(x) for x in (k.q_hi, k.q_lo, k.k_hi, k.k_lo))
    nm_u = k.neg_max.rearrange("c (u t) p -> u c (t p)", t=TILES)
    NGR = TILES // GROUP
    steps = [(s, g, kt) for s in range(2) for g in range(NGR) for kt in range(4 * g + 4)]
    N, NS = len(steps), len(steps) // 2
    AHEAD = 2
    PR = 4
    AUG = DH + 2
    with ExitStack() as ctx:
        sb, ps, sem = tools(k, ctx, f"att_{branch}")
        q2 = [sb(f"q2_{s}", [P, SEQ], F32R) for s in range(2)]
        qm = [sb(f"qm_{s}", [AUG, SEQ], F32R) for s in range(2)]
        k2 = [sb(f"k2_{s}", [P, SEQ], F32R) for s in range(2)]
        km = [sb(f"km_{s}", [AUG, SEQ], F32R) for s in range(2)]
        ones = sb("ones", [P, SEQ // 2])
        zero = sb("zero", [P, TILES])
        bias = [sb(f"bias{s}", [P, TILES]) for s in range(2)]
        v_raw = [sb(f"v_raw{s}", [P, TILES, dv]) for s in range(2)]
        v = [sb(f"v{s}", [P, TILES, VW], F32R) for s in range(2)]
        pf = sb("pf", [P, PR, 512])
        parts = [sb("p_hi", [P, PR, 512], F32R), sb("p_lo", [P, PR, 512], F32R)]
        low = sb("low", [P, GROUP, dv])
        raw = sb("raw", [P, 2, GROUP, dv])
        recip = sb("recip", [P, GROUP])
        o0 = sb("o0", [P, TILES, dv]) if A else None
        o = sb("o", [P, 2, GROUP, dv])
        s_ps = ps("s_ps", [P, 4, 512])
        acc = ps("acc", [P, GROUP, 512])
        loaded = [sem("loaded0"), sem("loaded1")]
        ones_done, s_done, p_done, split_done, pv_done, v_done, dve_step, pool_step = (
            sem(n) for n in ("ones_done", "s_done", "p_done", "split_done", "pv_done", "v_done", "dve_step", "pool_step"))
        low_done, acc_read, o_done = sem("low_done"), sem("acc_read"), sem("o_done")
        stored = [sem("stored0"), sem("stored1")]
        LOADS = 9 * 16
        out_groups = [(s, g) for s in range(2) for g in range(NGR) if s or not A]
        NO = len(out_groups)

        with nc.Block() as block:
            @block.sync
            def _(sp):
                def load(i, s):
                    u = i * stride + first[s]
                    row = lambda ap: ap[ds(u, 1)].rearrange("u d s -> d u s")
                    to = lambda tile, a, b: tile[a:b, :].bitcast(F32).unsqueeze(1)
                    for dst, src in ((to(q2[s], 0, DH), row(q_hi)), (to(q2[s], DH, P), row(q_lo)),
                                     (to(qm[s], 0, DH), row(q_hi)), (to(qm[s], DH, AUG), row(nm_u)),
                                     (to(k2[s], 0, DH), row(k_hi)), (to(k2[s], DH, P), row(k_hi)),
                                     (to(km[s], 0, DH), row(k_lo)),
                                     (bias[s][:].unsqueeze(1), row(k.bias_col)),
                                     (v_raw[s][:], v_in[:, :, ds(i * (DVA if A else 2 * DH) + (0 if A else s * DH), dv)])):
                        sp.dma_start(dst, src).then_inc(loaded[s], 16)
                def store(i, s):
                    for g in range(NGR):
                        if (s, g) in out_groups:
                            n = out_groups.index((s, g))
                            sp.wait_ge(o_done, i * NO + (n + 1))
                            cols = ds(i * (DVA if A else 2 * DH) + (0 if A else s * DH), dv)
                            sp.dma_start(o_out[:, g * GROUP:(g + 1) * GROUP, cols], o[:, n % 2, :, :]).then_inc(stored[n % 2], 16)

                for s in range(2):
                    sp.sem_inc(stored[s], 16)
                    load(0, s)
                with sp.Fori(1, TURNS) as i:
                    for s in range(2):
                        store(i - 1, s)
                        sp.wait_ge(pv_done, i * N + ((s + 1) * NS - N))
                        load(i, s)
                for s in range(2):
                    store(TURNS - 1, s)
                for s in range(2):
                    sp.wait_ge(stored[s], 16 * TURNS * NO // 2 + 16)

            @block.gpsimd
            def _(pool):
                nc.gpsimd.memset(zero[:], 0.0)
                nc.gpsimd.memset(ones[:], 1.0).then_inc(ones_done, 1)
                pool.wait_ge(ones_done, 1)

                def split_v(i, s):
                    pool.wait_ge(loaded[s], i * LOADS + LOADS)
                    nc.gpsimd.tensor_tensor(v[s][:, :, 2:2 + dv], v_raw[s][:], zero[:].unsqueeze(2).to_broadcast([P, TILES, dv]),
                                            ALU.add).then_inc(pool_step, 1)
                    pool.wait_ge(pool_step, i * 2 + (s + 1))
                    nc.gpsimd.tensor_tensor(v[s][:, :, 2 + dv:VW], v_raw[s][:], v[s][:, :, 2:2 + dv].bitcast(F32),
                                            ALU.subtract).then_inc(v_done, 1)

                for s in range(2):
                    split_v(0, s)
                with pool.Fori(1, TURNS) as i:
                    for s in range(2):
                        split_v(i, s)

            @block.scalar
            def _(act):
                act.wait_ge(ones_done, 1)
                for s in range(2):
                    for c in range(2):
                        nc.scalar.activation(km[s][DH:AUG, c * (SEQ // 2):(c + 1) * (SEQ // 2)], ones[DH:AUG, :], ACT.Copy)
                    nc.scalar.activation(v[s][:, :, 0:2], ones[:, 0:2 * TILES].rearrange("p (t c) -> p t c", c=2), ACT.Copy).then_inc(ones_done, 1)
                with act.Fori(0, TURNS) as i:
                    def low_part(m):
                        s, g, kt = steps[m]
                        G = s * NGR + g
                        act.wait_ge(pv_done, i * N + (m + 1))
                        nc.scalar.activation(low[:], acc[:, :, 2 + dv:VW], ACT.Copy).then_inc(low_done, 1)

                    ends = [n for n in range(N) if n + 1 == N or steps[n + 1][1] != steps[n][1]]
                    for n, (s, g, kt) in enumerate(steps):
                        if n % NS == 0:
                            act.wait_ge(loaded[s], i * LOADS + LOADS)
                        act.wait_ge(s_done, i * N + (n + 1))
                        if n >= PR:
                            act.wait_ge(split_done, i * N + (n - PR + 1))
                        w = 512 - P * max(0, kt - 4 * g)
                        col = 12 + kt - 4 * g if A else kt
                        nc.scalar.activation(pf[:, n % PR, 0:w], s_ps[:, n % 4, 0:w], ACT.Exp,
                                             bias=bias[s][:, col:col + 1]).then_inc(p_done, 1)
                        if n - AHEAD in ends:
                            low_part(n - AHEAD)
                    low_part(N - 1)

            @block.vector
            def _(dve):
                dve.sem_inc(acc_read, 1)
                with dve.Fori(0, TURNS) as i:
                    ends = [n for n in range(N) if n + 1 == N or steps[n + 1][1] != steps[n][1]]
                    PER = N + 2 * NGR if not A else N + NGR * 2 + NGR * 3
                    step = Tally(dve_step, i * PER)

                    def finish(m):
                        s, g, kt = steps[m]
                        G = s * NGR + g
                        src = acc[:, :, 2:2 + dv]
                        dve.wait_ge(pv_done, i * N + (m + 1))
                        dve.wait_ge(low_done, i * (2 * NGR) + (G + 1))
                        step.inc(nc.vector.reciprocal(recip[:], acc[:, :, 0]))
                        nc.vector.tensor_tensor(raw[:, G % 2, :, :], src, low[:], ALU.add).then_inc(acc_read, 1)
                        step.wait(dve)
                        if A and s == 1:
                            step.inc(nc.vector.tensor_scalar(recip[:], recip[:], k.neg_lam[:], None, ALU.mult))
                            step.wait(dve)
                        dve.wait_ge(acc_read, i * (2 * NGR) + (G + 2))
                        scale = recip[:].unsqueeze(2).to_broadcast([P, GROUP, dv])
                        if (s, g) not in out_groups:
                            step.inc(nc.vector.tensor_tensor(o0[:, g * GROUP:(g + 1) * GROUP, :], raw[:, G % 2, :, :], scale, ALU.mult))
                            step.wait(dve)
                            return
                        n = out_groups.index((s, g))
                        dve.wait_ge(stored[n % 2], i * (8 * NO) + 16 * (n // 2 + 1))
                        if A:
                            step.inc(nc.vector.tensor_tensor(raw[:, G % 2, :, :], raw[:, G % 2, :, :], scale, ALU.mult))
                            step.wait(dve)
                            nc.vector.tensor_tensor(o[:, n % 2, :, :], raw[:, G % 2, :, :], o0[:, g * GROUP:(g + 1) * GROUP, :],
                                                    ALU.add).then_inc(o_done, 1)
                        else:
                            nc.vector.tensor_tensor(o[:, n % 2, :, :], raw[:, G % 2, :, :], scale, ALU.mult).then_inc(o_done, 1)
                        dve.wait_ge(o_done, i * NO + (n + 1))

                    for n, (s, g, kt) in enumerate(steps):
                        w = 512 - P * max(0, kt - 4 * g)
                        dve.wait_ge(p_done, i * N + (n + 1))
                        if n >= PR:
                            dve.wait_ge(pv_done, i * N + (n - PR + 1))
                        step.inc(nc.vector.tensor_copy(parts[HI][:, n % PR, 0:w], pf[:, n % PR, 0:w]))
                        step.wait(dve)
                        nc.vector.tensor_tensor(parts[LO][:, n % PR, 0:w], pf[:, n % PR, 0:w],
                                                parts[HI][:, n % PR, 0:w].bitcast(F32), ALU.subtract).then_inc(split_done, 1)
                        if n - AHEAD in ends:
                            finish(n - AHEAD)
                    finish(N - 1)
                    assert step.n == PER

            @block.tensor
            def _(pe):
                pe.wait_ge(ones_done, 3)
                with pe.Fori(0, TURNS) as i:
                    def scores(n):
                        s, g, kt = steps[n]
                        off = P * max(0, kt - 4 * g)
                        w = 512 - off
                        qs, ks = slice(g * 512 + off, (g + 1) * 512), slice(kt * P, (kt + 1) * P)
                        if n % NS == 0:
                            pe.wait_ge(loaded[s], i * LOADS + LOADS)
                        if n >= 4:
                            pe.wait_ge(p_done, i * N + (n - 3))
                        out = s_ps[:, n % 4, 0:w]
                        nc.tensor.matmul(out, k2[s][:, ks], q2[s][:, qs], start=True, stop=False)
                        last = nc.tensor.matmul(out, km[s][:, ks], qm[s][:, qs], start=False, stop=kt < 4 * g)
                        if kt >= 4 * g:
                            last = nc.tensor.matmul(s_ps[:, n % 4, 0:P], k.ident_b[:], k.mask_q[:], start=False, stop=True)
                        last.then_inc(s_done, 1)

                    for n in range(AHEAD):
                        scores(n)
                    for n, (s, g, kt) in enumerate(steps):
                        if n + AHEAD < N:
                            scores(n + AHEAD)
                        if n % NS == 0:
                            pe.wait_ge(v_done, i * 2 + (s + 1))
                        pe.wait_ge(split_done, i * N + (n + 1))
                        G = s * NGR + g
                        if kt == 0:
                            pe.wait_ge(acc_read, i * (2 * NGR) + (G + 1))
                        off = max(0, kt - 4 * g)
                        for j in range(off, GROUP):
                            stop = kt == 4 * g + j
                            lhs = slice((j - off) * P, (j - off + 1) * P)
                            nc.tensor.matmul(acc[:, j, 0:VW], parts[HI][:, n % PR, lhs], v[s][:, kt, :], start=kt == 0, stop=False)
                            last = nc.tensor.matmul(acc[:, j, 0:2 + dv], parts[LO][:, n % PR, lhs], v[s][:, kt, 0:2 + dv], start=False, stop=stop)
                        last.then_inc(pv_done, 1)


def sample(k):
    nc, t = k.nc, k.t
    ROWS = 4 * HB
    KEYS = PAST + SR
    caches = [t[n].rearrange(f"z n r {x} -> (z n) r ({x})") for n, x in (
        ("cache_a_k", "m h d"), ("cache_b_k", "h d"), ("cache_a_v", "h d"), ("cache_b_v", "h d"))]
    cache_f = t["cache_b_logf"].rearrange("z n r h -> (z n) r h")
    NPOOL = caches[0].shape[0]
    TURNS = NB // 2
    with ExitStack() as ctx:
        sb, ps, sem = tools(k, ctx, "smp")
        pages = sb("pages", [1, NB * NPG], I32)
        kv = [[sb(f"{n}{s}", [P, NPG, W]) for n in ("k_a", "k_b", "v_a", "v_b")] for s in range(2)]
        lf = sb("lf", [P, NPG, NB, HB])
        row_i, col_i, t_i = sb("row_i", [ROWS, 4], I32), sb("col_i", [ROWS, PAST], I32), sb("t_i", [ROWS, NB, NT], I32)
        row_q, map_i = sb("row_q", [ROWS, 1], I32), sb("map_i", [ROWS, 1], I32)
        row_qf, weight, slope = sb("row_qf", [ROWS, 1]), sb("weight", [ROWS, 1]), sb("slope", [ROWS, 1])
        past_bias = sb("past_bias", [ROWS, PAST])
        causal, causal_a = sb("causal", [ROWS, SR]), sb("causal_a", [ROWS, SR])
        new_bias = sb("new_bias", [ROWS, 2, NB, SR])
        own = sb("own", [ROWS, 2, W])
        match = sb("match", [ROWS, 2, SR])
        select = sb("select", [ROWS, 2, NB, SR])
        pick_f = sb("pick_f", [NB * HB, NB, ROWS])
        pick_h = sb("pick_h", [HB, ROWS])
        tri = sb("tri", [SR, SR])
        ones = sb("ones", [NB * HB, PAST])
        f_past = sb("f_past", [NB * HB, PAST])
        f_rel = sb("f_rel", [NB * HB, PAST])
        f_new = sb("f_new", [HB, SR])
        q_all = sb("q_all", [P, NB, 2, 4, ROWS])
        fence = sb("fence", [1, 2])
        q_blk = [sb(f"q_blk{s}", [P, 2, 4, ROWS]) for s in range(2)]
        sel_b = [sb(f"sel_b{s}", [ROWS, 2, SR]) for s in range(2)]
        pick_b = [sb(f"pick_b{s}", [NB * HB, ROWS]) for s in range(2)]
        kT = sb("kT", [P, 2, 4, PAST])
        sc = sb("sc", [ROWS, 2, KEYS])
        pr = sb("pr", [ROWS, 2, KEYS])
        neg_max, sums, recip = sb("neg_max", [ROWS, 2]), sb("sums", [ROWS, 2]), sb("recip", [ROWS, 2])
        pT = sb("pT", [P, 2, NPG, ROWS])
        pT_new = sb("pT_new", [SR, 2, ROWS])
        o_own = sb("o_own", [ROWS, 2, W])
        o_sum = sb("o_sum", [SR, 2, W])
        ps_t = ps("ps_t", [P, 2, 512])
        ps_f = ps_t[0:NB * HB, 0, :]
        ps_s = ps("ps_s", [ROWS, 2, 512])
        ps_n = ps("ps_n", [ROWS, 512])
        ps_p = ps("ps_p", [P, 512])
        ps_o = ps("ps_o", [ROWS, 2, 512])
        pages_in, lf_in, stored = sem("pages_in"), sem("lf_in"), sem("stored")
        kv_in = [[sem(f"kv_in{s}_{n}") for n in range(4)] for s in range(2)]
        names = ("pool_step", "filled", "made", "small", "consts", "dve_step", "lf_turned", "f_scanned", "f_ready",
                 "fn_ready", "fn_copied", "prepared", "turned", "kt_act", "kt_dve", "s_done", "past_b", "max_done",
                 "p_done", "pt_ready", "pt_copied", "pv_done", "own_done", "dve_recip", "picked", "added")
        S = {n: sem(n) for n in names}
        with nc.Block() as block:
            @block.sync
            def _(sp):
                sp.dma_start(pages[:], t["page_table"].rearrange("b n -> (b n)").unsqueeze(0)).then_inc(pages_in, 16)
                sp.wait_ge(pages_in, 16)

                def page(b, g):
                    return sp.value_load(pages[0:1, ds(b * NPG + g, 1)], min_val=0, max_val=NPOOL - 1)

                with sp.Fori(0, NB) as b:
                    for g in range(NPG):
                        sp.dma_start(lf[:, g, ds(b, 1), :], cache_f[ds(page(b, g), 1)].rearrange("n r h -> r n h")).then_inc(lf_in, 16)

                def load(b, s):
                    for g in range(NPG):
                        pg = page(b, g)
                        for n in range(4):
                            sp.dma_start(kv[s][n][:, g:g + 1, :], caches[n][ds(pg, 1)].rearrange("n r c -> r n c")).then_inc(kv_in[s][n], 16)
                load(0, 0)
                load(1, 1)
                with sp.Fori(1, TURNS) as i:
                    for s in range(2):
                        sp.wait_ge(S["pv_done"], i * 2 + (s - 1))
                        load(i * 2 + s, s)
                sp.wait_ge(S["added"], NB + 1)
                sp.dma_start(k.o_a[SEQ:SEQ + SR], o_sum[:, 0, :]).then_inc(stored, 16)
                sp.dma_start(k.o_b[SEQ:SEQ + SR], o_sum[:, 1, :]).then_inc(stored, 16)
                sp.wait_ge(stored, 32)

            @block.gpsimd
            def _(pool):
                g = nc.gpsimd
                g.iota(row_i[:], pattern=[[0, 4]], base=0, channel_multiplier=1)
                g.iota(col_i[:], pattern=[[1, PAST]], base=-PAST, channel_multiplier=0)
                g.iota(t_i[:], pattern=[[0, NB], [1, NT]], base=0, channel_multiplier=0)
                g.memset(slope[:], SLOPES[HA - 1])
                g.memset(own[:], 1.0)
                g.memset(pick_f[:], -1.0)
                g.memset(pick_h[:], -1.0)
                g.memset(tri[:], 1.0)
                g.memset(ones[:], 1.0)
                g.memset(q_all[:], 0.0).then_inc(S["filled"], 1)
                pool.wait_ge(S["filled"], 1)
                step = Tally(S["pool_step"])

                def select_(ap, pattern, cm, base, fill, op=ALU.is_ge):
                    step.inc(g.affine_select(out=ap, in_=ap, compare_op=op, fill=fill, base=base, pattern=pattern, channel_multiplier=cm))
                    step.wait(pool)
                for h in range(HA - 2, -1, -1):
                    select_(slope[:], [[0, 1]], 1, -8 * (h + 1), SLOPES[h])
                for b, (n, w, r) in enumerate(((HA, DVA, 2 * NT), (HB, DH, NT))):
                    select_(own[:, b, :], [[-r, n], [0, w]], 1, 0, 0.0)
                    select_(own[:, b, :], [[r, n], [0, w]], -1, r - 1, 0.0)
                select_(pick_f[:], [[-HB, NB], [-1, HB], [0, NT]], 1, 0, 0.0, ALU.is_equal)
                select_(pick_h[:], [[-1, HB], [0, NT]], 1, 0, 0.0, ALU.is_equal)
                select_(tri[:], [[NT, NB], [1, NT]], -1, 0, 0.0)
                select_(tri[:], [[-NT, NB], [0, NT]], 1, 0, 0.0)
                g.memset(fence[:], 0.0).then_inc(S["made"], 1)
                pool.wait_ge(S["small"], 1)
                for b in range(2):
                    select_(new_bias[:, b, :, :], [[-1, NB], [1, NB], [0, NT]], 0, 0, NEG, ALU.is_equal)
                    select_(select[:, b, :, :], [[-1, NB], [1, NB], [0, NT]], 0, 0, 0.0, ALU.is_equal)
                g.memset(fence[:], 0.0).then_inc(S["consts"], 1)

            def iteration(body):
                def run(eng):
                    with eng.Fori(0, TURNS - 1) as i:
                        for s in range(2):
                            body(i, s, True)
                    for s in range(2):
                        body(TURNS - 1, s, s == 0)
                return run

            @block.vector
            def _(dve):
                v = nc.vector
                step = Tally(S["dve_step"])

                def go(ins):
                    step.inc(ins)
                    step.wait(dve)
                dve.wait_ge(S["made"], 1)
                go(v.tensor_scalar(row_q[:], row_i[:, 0:1], 3, None, ALU.bitwise_and))
                go(v.tensor_scalar(map_i[:], row_i[:, 0:1], 4, None, ALU.bitwise_and))
                go(v.tensor_copy(row_qf[:], row_q[:]))
                go(v.tensor_scalar(weight[:], map_i[:], 0.25, None, ALU.mult))
                go(v.tensor_scalar(sums[:, 0:1], k.neg_lam[0:ROWS, :], -1.0, None, ALU.add))
                go(v.tensor_tensor(weight[:], weight[:], sums[:, 0:1], ALU.mult))
                go(v.tensor_scalar(weight[:], weight[:], 1.0, None, ALU.add))
                go(v.tensor_scalar(past_bias[:], col_i[:], slope[:], None, ALU.mult))
                tf = t_i[:].rearrange("p b t -> p (b t)")
                go(v.tensor_scalar(causal[:], tf, row_qf[:], NEG, ALU.is_gt, ALU.mult))
                go(v.tensor_scalar(causal_a[:], tf, slope[:], None, ALU.mult))
                go(v.tensor_tensor(causal_a[:], causal_a[:], causal[:], ALU.add))
                go(v.tensor_scalar(match[:, 1, :], tf, row_qf[:], None, ALU.is_equal))
                go(v.tensor_scalar(match[:, 0, :], match[:, 1, :], weight[:], None, ALU.mult))
                over = lambda ap: ap.unsqueeze(1).to_broadcast([ROWS, NB, SR])
                v.tensor_copy(new_bias[:, 0, :, :], over(causal_a[:]))
                v.tensor_copy(new_bias[:, 1, :, :], over(causal[:]))
                v.tensor_copy(select[:, 0, :, :], over(match[:, 0, :]))
                v.tensor_copy(select[:, 1, :, :], over(match[:, 1, :])).then_inc(S["small"], 1)
                for b in range(2):
                    for u in range(8):
                        p, half = u // 2, u % 2
                        c = 8 * (u % HA) + 4 * (u // HA) if b == 0 else 4 * u
                        r = slice(half * DH, (half + 1) * DH)
                        last = v.tensor_copy(q_all[r, :, b, p, c:c + NT], k.qT_s[r, b, p, :].rearrange("p (b t) -> p b t", t=NT))
                step.inc(last)
                dve.wait_ge(S["lf_turned"], 1)
                go(v.tensor_tensor_scan(f_past[:], ones[:], ps_f, 0.0, ALU.mult, ALU.add))
                v.tensor_scalar(f_rel[:], f_past[:], f_past[:, PAST - 1:PAST], None, ALU.subtract).then_inc(S["f_ready"], 1)
                dve.wait_ge(S["fn_ready"], 1)
                v.tensor_copy(f_new[:], ps_n[0:HB, 0:SR]).then_inc(S["fn_copied"], 1)
                go(v.memset(o_sum[:], 0.0))
                dve.wait_ge(S["consts"], 1)

                def prepare(b, s):
                    v.tensor_copy(q_blk[s][:].unsqueeze(1), q_all[:, ds(b, 1)])
                    v.tensor_copy(sel_b[s][:].unsqueeze(2), select[:, :, ds(b, 1), :])
                    v.tensor_copy(pick_b[s][:].unsqueeze(1), pick_f[:, ds(b, 1), :]).then_inc(S["prepared"], 1)

                def k_turned(b):
                    for n in range(0, 8, 2):
                        dve.wait_ge(S["turned"], b * 8 + (n + 1))
                        v.tensor_copy(kT[:, n // 4, n % 4, :], ps_t[:, 0, :]).then_inc(S["kt_dve"], 1)

                dve.sem_inc(S["added"], 1)
                prepare(0, 0)
                prepare(1, 1)
                k_turned(0)

                def body(i, s, more):
                    b = i * 2 + s
                    dve.wait_ge(S["s_done"], b + 1)
                    v.tensor_tensor(sc[:, 0, 0:PAST], ps_s[:, 0, :], past_bias[:], ALU.add)
                    v.tensor_tensor(sc[:, :, PAST:KEYS].unsqueeze(2), ps_n[:, 0:2 * SR].rearrange("p (c k) -> p c k", c=2).unsqueeze(2),
                                    new_bias[:, :, ds(b, 1), :], ALU.add).then_inc(S["max_done"], 1)
                    dve.wait_ge(S["past_b"], b + 1)
                    dve.wait_ge(S["max_done"], b * 2 + 1)
                    v.tensor_reduce(neg_max[:], sc[:], AX.X, ALU.max, negate=True).then_inc(S["max_done"], 1)
                    if more:
                        k_turned(b + 1)
                    dve.wait_ge(S["p_done"], b * 2 + 2)
                    v.reciprocal(recip[:], sums[:]).then_inc(S["dve_recip"], 1)
                    dve.wait_ge(S["pt_ready"], b + 1)
                    v.tensor_copy(pT[:], ps_p[:, 0:2 * NPG * ROWS].rearrange("p (c g r) -> p c g r", c=2, g=NPG))
                    v.tensor_copy(pT_new[:], ps_p[0:SR, 2 * NPG * ROWS:2 * (NPG + 1) * ROWS].rearrange("p (c r) -> p c r", c=2)).then_inc(S["pt_copied"], 1)
                    dve.wait_ge(S["pv_done"], b + 1)
                    dve.wait_ge(S["dve_recip"], b + 1)
                    for c in range(2):
                        last = v.scalar_tensor_tensor(o_own[:, c, :], ps_o[:, c, :], recip[:, c:c + 1], own[:, c, :], ALU.mult, ALU.mult)
                    last.then_inc(S["own_done"], 1)
                    dve.wait_ge(S["picked"], b + 1)
                    v.tensor_tensor(o_sum[:], ps_o[0:SR, :, :], o_sum[:], ALU.add).then_inc(S["added"], 1)
                    dve.wait_ge(S["added"], b + 2)
                    if not isinstance(i, int):
                        prepare(b + 2, s)

                iteration(body)(dve)

            @block.scalar
            def _(act):
                a = nc.scalar

                def k_turned(b):
                    for n in range(1, 8, 2):
                        act.wait_ge(S["turned"], b * 8 + (n + 1))
                        a.activation(kT[:, n // 4, n % 4, :], ps_t[:, 1, :], ACT.Copy).then_inc(S["kt_act"], 1)

                def body(i, s, more):
                    b = i * 2 + s
                    act.wait_ge(S["s_done"], b + 1)
                    a.activation(sc[:, 1, 0:PAST], ps_s[:, 1, :], ACT.Copy).then_inc(S["past_b"], 1)
                    act.wait_ge(S["max_done"], b * 2 + 2)
                    for c in range(2):
                        a.activation(pr[:, c, :], sc[:, c, :], ACT.Exp, bias=neg_max[:, c:c + 1],
                                     accum_out=sums[:, c:c + 1]).then_inc(S["p_done"], 1)
                    if more:
                        k_turned(b + 1)
                k_turned(0)
                iteration(body)(act)

            @block.tensor
            def _(pe):
                mm, tr = nc.tensor.matmul, nc.tensor.transpose
                pe.wait_ge(lf_in, 16 * NB * NPG)
                for g in range(NPG):
                    last = tr(ps_f[:, g * PG:(g + 1) * PG], lf[:, g, :, :].rearrange("p b h -> p (b h)"), k.ident[:])
                last.then_inc(S["lf_turned"], 1)
                pe.wait_ge(S["made"], 1)
                mm(ps_n[0:HB, 0:SR], k.logf[0:SR, TILES, :], tri[:], start=True, stop=True).then_inc(S["fn_ready"], 1)
                pe.wait_ge(S["fn_copied"], 1)
                pe.wait_ge(S["f_ready"], 1)

                def front(i, s):
                    b = i * 2 + s
                    for n in range(8):
                        c, p = n // 4, n % 4
                        if p == 0:
                            pe.wait_ge(kv_in[s][c], i * (16 * NPG) + 16 * NPG)
                        if n >= 2:
                            pe.wait_ge((S["kt_dve"], S["kt_act"])[n % 2], b * 4 + n // 2)
                        for g in range(NPG):
                            last = tr(ps_t[:, n % 2, g * PG:(g + 1) * PG], kv[s][c][:, g, p * P:(p + 1) * P], k.ident[:])
                        last.then_inc(S["turned"], 1)
                    pe.wait_ge(S["prepared"], b + 1)
                    pe.wait_ge(S["kt_dve"], b * 4 + 4)
                    pe.wait_ge(S["kt_act"], b * 4 + 4)
                    for c in range(2):
                        for p in range(4):
                            mm(ps_s[:, c, :], q_blk[s][:, c, p, :], kT[:, c, p, :], start=p == 0, stop=p == 3 and c == 0)
                    mm(ps_s[:, 1, :], pick_b[s][:], f_rel[:], start=False, stop=True)
                    for c in range(2):
                        for p in range(4):
                            mm(ps_n[:, c * SR:(c + 1) * SR], q_blk[s][:, c, p, :], k.kT_s[:, c, p, :], start=p == 0, stop=p == 3 and c == 0)
                    mm(ps_n[:, SR:2 * SR], pick_h[:], f_new[:], start=False, stop=True).then_inc(S["s_done"], 1)

                front(0, 0)

                def body(i, s, more):
                    b = i * 2 + s
                    if more:
                        pe.wait_ge(S["max_done"], b * 2 + 2)
                        front(*((i, 1) if s == 0 else (i + 1, 0)))
                    pe.wait_ge(S["made"], 1)
                    pe.wait_ge(S["p_done"], b * 2 + 2)
                    for c in range(2):
                        for g in range(NPG):
                            n = c * NPG + g
                            tr(ps_p[:, n * ROWS:(n + 1) * ROWS], pr[:, c, g * PG:(g + 1) * PG], k.ident[0:ROWS, 0:ROWS])
                    for c in range(2):
                        n = 2 * NPG + c
                        last = tr(ps_p[0:SR, n * ROWS:(n + 1) * ROWS], pr[:, c, PAST:KEYS], k.ident[0:ROWS, 0:ROWS])
                    last.then_inc(S["pt_ready"], 1)
                    pe.wait_ge(S["pt_copied"], b + 1)
                    pe.wait_ge(S["added"], b + 1)
                    for c in range(2):
                        pe.wait_ge(kv_in[s][2 + c], i * (16 * NPG) + 16 * NPG)
                        for g in range(NPG):
                            mm(ps_o[:, c, :], pT[:, c, g, :], kv[s][2 + c][:, g, :], start=g == 0, stop=False)
                        last = mm(ps_o[:, c, :], pT_new[:, c, :], k.v_s[:, c, :], start=False, stop=True)
                    last.then_inc(S["pv_done"], 1)
                    pe.wait_ge(S["made"], 1)
                    pe.wait_ge(S["own_done"], b + 1)
                    for c in range(2):
                        last = mm(ps_o[:, c, :], sel_b[s][:, c, :], o_own[:, c, :], start=True, stop=True)
                    last.then_inc(S["picked"], 1)
                iteration(body)(pe)


def merge(k):
    nc, t = k.nc, k.t
    KW = W // P
    KT = 2 * KW + KD
    weights = [t["w_out_a"][0]] * KW + [t["w_out_b"][0]] * KW + [t["w_o"][0]] * KD
    w_row = [kt % KW if kt < 2 * KW else kt - 2 * KW for kt in range(KT)]
    x_in = {P: t["x_prompt"][0], SR: t["x_sample"].rearrange("b t d -> (b t) d")}
    with ExitStack() as ctx:
        sb, ps, sem = tools(k, ctx, "mrg")
        w_raw = sb("w_raw", [P, 2, D])
        w = [sb("w_hi", [P, KT, D], F32R), sb("w_lo", [P, KT, D], F32R)]
        gain = sb("gain", [P, DVA])
        res = sb("res", [P, D])
        ob = sb("ob", [P, 2 * W])
        gates = sb("gates", [P, 2 * W])
        mix = sb("mix", [P, 2 * D])
        x = sb("x", [P, D])
        ms, rstd = sb("ms", [P, HA]), sb("rstd", [P, HA])
        u = sb("u", [P, 2 * W])
        uT = [sb("uT_hi", [P, 2 * KW, P], F32R), sb("uT_lo", [P, 2 * KW, P], F32R)]
        y, y2 = sb("y", [P, D]), sb("y2", [P, D])
        yT = [sb("yT_hi", [P, KD, P], F32R), sb("yT_lo", [P, KD, P], F32R)]
        out = sb("out", [P, D])
        ps_y = ps("ps_y", [P, 4, 512])
        ps_o = ps("ps_o", [P, 2, 512])
        ps_t = ps("ps_t", [P, 2, 512])
        names = ("gain_in", "res_in", "w_split", "w_step", "o_in", "g_in", "m_in", "x_in", "sq_done", "mean_done",
                 "rstd_done", "u_step", "u_done", "u_turned", "uT_hi_done", "uT_done", "y_ready", "y_step", "y_done",
                 "y_turned", "yT_hi_done", "yT_done", "o_ready", "scaled", "out_done", "stored")
        S = {n: sem(n) for n in names}
        w_in = [sem("w_in0"), sem("w_in1")]

        def where(tile, pn, ap):
            return ap[ds(tile * P, P)] if pn == P else ap[SEQ:SEQ + SR]

        with nc.Block() as block:
            @block.sync
            def _(sp):
                def load_o(tile, pn):
                    for n, src in enumerate((k.o_a, k.o_b)):
                        sp.dma_start(ob[0:pn, n * W:(n + 1) * W], where(tile, pn, src)).then_inc(S["o_in"], 16)
                    sp.dma_start(gates[0:pn, :], where(tile, pn, k.gates)).then_inc(S["g_in"], 16)

                def load_m(tile, pn):
                    sp.dma_start(mix[0:pn, :], where(tile, pn, k.mixes)).then_inc(S["m_in"], 16)

                def load_x(tile, pn):
                    src = x_in[P][ds(tile * P, P)] if pn == P else x_in[SR]
                    sp.dma_start(x[0:pn, :], src).then_inc(S["x_in"], 16)

                def store(tile, pn):
                    sp.wait_ge(S["out_done"], tile + 1)
                    dst = t["y_prompt"][ds(tile * P, P)] if pn == P else t["y_sample"]
                    sp.dma_start(dst, out[0:pn, :]).then_inc(S["stored"], 16)

                sp.sem_inc(S["stored"], 16)
                load_o(0, P)
                sp.dma_start(gain[:], t["g_sub_a"].to_broadcast([P, DVA])).then_inc(S["gain_in"], 16)
                for kt in range(KT):
                    if kt >= 2:
                        sp.wait_ge(S["w_split"], kt - 1)
                    r = w_row[kt] * P
                    sp.dma_start(w_raw[:, kt % 2, :], weights[kt][r:r + P, :]).then_inc(w_in[kt % 2], 16)
                    if kt == 2:
                        load_m(0, P)
                        load_x(0, P)
                        sp.dma_start(res[:], k.ada_gate[SR:SR + 1, :].to_broadcast([P, D])).then_inc(S["res_in"], 16)

                def turn(n, pn_next, first=False):
                    sp.wait_ge(S["u_done"], n + 1)
                    load_o(n + 1, pn_next)
                    sp.wait_ge(S["y_done"], n + 1)
                    load_m(n + 1, pn_next)
                    if not first:
                        sp.wait_ge(S["out_done"], n)
                        load_x(n, P)
                        store(n - 1, P)
                turn(0, P, first=True)
                with sp.Fori(1, TILES - 1) as n:
                    turn(n, P)
                turn(TILES - 1, SR)
                sp.wait_ge(S["out_done"], TILES)
                load_x(TILES, SR)
                store(TILES - 1, P)
                sp.wait_ge(S["scaled"], TILES + 1)
                sp.dma_start(res[0:SR, :], k.ada_gate[0:SR, :]).then_inc(S["res_in"], 16)
                store(TILES, SR)
                sp.wait_ge(S["stored"], 16 * (TILES + 2))

            @block.gpsimd
            def _(pool):
                def gate(n, pn):
                    pool.wait_ge(S["mean_done"], n + 1)
                    nc.gpsimd.tensor_tensor(rstd[0:pn, :], ms[0:pn, :], k.neg_half[0:pn, 0:HA], ALU.pow).then_inc(S["rstd_done"], 1)
                with pool.Fori(0, TILES) as n:
                    gate(n, P)
                gate(TILES, SR)

            @block.scalar
            def _(act):
                a = nc.scalar

                def square(n, pn, first=False):
                    act.wait_ge(S["o_in"], n * 32 + 32)
                    if not first:
                        act.wait_ge(S["u_turned"], n)
                    a.activation(u[0:pn, 0:W], ob[0:pn, 0:W], ACT.Square).then_inc(S["sq_done"], 1)

                def turn(n, pn, nxt):
                    if nxt:
                        square(n + 1, nxt)
                        act.wait_ge(S["u_turned"], n + 2)
                        act.wait_ge(S["y_ready"], n + 1)
                        evacuate(n + 1, nxt, uT[HI], S["uT_hi_done"])
                    act.wait_ge(S["y_turned"], n + 1)
                    act.wait_ge(S["o_ready"], n + 1)
                    evacuate(n, pn, yT[HI], S["yT_hi_done"])

                def evacuate(n, pn, hi, done):
                    for c in range(2):
                        last = a.activation(hi[:, 4 * c:4 * c + 4, 0:pn], ps_t[:, c, :].rearrange("p (a r) -> p a r", a=4)[:, :, 0:pn], ACT.Copy)
                    last.then_inc(done, 1)

                square(0, P, first=True)
                act.wait_ge(S["u_turned"], 1)
                evacuate(0, P, uT[HI], S["uT_hi_done"])
                with act.Fori(0, TILES - 1) as n:
                    turn(n, P, P)
                turn(TILES - 1, P, SR)
                turn(TILES, SR, 0)

            @block.vector
            def _(dve):
                v = nc.vector
                halves = lambda ap: ap.rearrange("p a b -> p (a b)")

                def gated(n, pn):
                    step = Tally(S["u_step"], n * 2)
                    heads = lambda ap: ap.rearrange("p (h d) -> p h d", h=HA)
                    dve.wait_ge(S["sq_done"], n + 1)
                    step.inc(v.reduce_sum(ms[0:pn, :], heads(u[0:pn, 0:W]), AX.X))
                    step.wait(dve)
                    v.tensor_scalar(ms[0:pn, :], ms[0:pn, :], 1.0 / DVA, EPS, ALU.mult, ALU.add).then_inc(S["mean_done"], 1)
                    dve.wait_ge(S["g_in"], n * 16 + 16)
                    step.inc(v.tensor_tensor(heads(gates[0:pn, 0:W]), heads(gates[0:pn, 0:W]),
                                             gain[0:pn, :].unsqueeze(1).to_broadcast([pn, HA, DVA]), ALU.mult))
                    v.tensor_tensor(u[0:pn, W:2 * W], ob[0:pn, W:2 * W], gates[0:pn, W:2 * W], ALU.mult)
                    step.wait(dve)
                    dve.wait_ge(S["rstd_done"], n + 1)
                    for h in range(HA):
                        c = slice(h * DVA, (h + 1) * DVA)
                        last = v.scalar_tensor_tensor(u[0:pn, c], ob[0:pn, c], rstd[0:pn, h:h + 1], gates[0:pn, c], ALU.mult, ALU.mult)
                    last.then_inc(S["u_done"], 1)

                def low(n, pn, hi_done, parts, done):
                    dve.wait_ge(hi_done, n + 1)
                    for c in range(2):
                        last = v.tensor_tensor(parts[LO][:, 4 * c:4 * c + 4, 0:pn], ps_t[:, c, :].rearrange("p (a r) -> p a r", a=4)[:, :, 0:pn],
                                               parts[HI][:, 4 * c:4 * c + 4, 0:pn].bitcast(F32), ALU.subtract)
                    last.then_inc(done, 1)

                def combine(n, pn, first):
                    dve.wait_ge(S["m_in"], n * 16 + 16)
                    dve.wait_ge(S["y_ready"], n + 1)
                    if not first:
                        dve.wait_ge(S["y_turned"], n)
                    v.tensor_tensor(y[0:pn, :], halves(ps_y[0:pn, 0:2, :]), mix[0:pn, 0:D], ALU.mult)
                    v.tensor_tensor(y2[0:pn, :], halves(ps_y[0:pn, 2:4, :]), mix[0:pn, D:2 * D], ALU.mult).then_inc(S["y_step"], 1)
                    dve.wait_ge(S["y_step"], n + 1)
                    v.tensor_tensor(y[0:pn, :], y[0:pn, :], y2[0:pn, :], ALU.add).then_inc(S["y_done"], 1)

                def finish(n, pn):
                    dve.wait_ge(S["o_ready"], n + 2)
                    dve.wait_ge(S["res_in"], 16 if pn == P else 32)
                    dve.wait_ge(S["x_in"], n * 16 + 16)
                    dve.wait_ge(S["stored"], n * 16 + 16)
                    v.tensor_tensor(out[0:pn, :], halves(ps_o[0:pn, :, :]), res[0:pn, :], ALU.mult).then_inc(S["scaled"], 1)
                    dve.wait_ge(S["scaled"], n + 2)
                    v.tensor_tensor(out[0:pn, :], out[0:pn, :], x[0:pn, :], ALU.add).then_inc(S["out_done"], 1)

                def turn(n, pn, nxt, first=False):
                    if nxt:
                        gated(n + 1, nxt)
                    combine(n, pn, first)
                    if nxt:
                        low(n + 1, nxt, S["uT_hi_done"], uT, S["uT_done"])
                    if not first:
                        finish(n - 1, P)
                    low(n, pn, S["yT_hi_done"], yT, S["yT_done"])

                dve.sem_inc(S["scaled"], 1)
                dve.wait_ge(S["gain_in"], 16)
                v.tensor_scalar(gain[:], gain[:], 1.0 - LAM_INIT, None, ALU.mult).then_inc(S["w_step"], 1)
                dve.wait_ge(S["w_step"], 1)
                gated(0, P)
                low(0, P, S["uT_hi_done"], uT, S["uT_done"])
                for kt in range(KT):
                    dve.wait_ge(w_in[kt % 2], 16 * (kt // 2 + 1))
                    v.tensor_copy(w[HI][:, kt, :], w_raw[:, kt % 2, :]).then_inc(S["w_step"], 1)
                    dve.wait_ge(S["w_step"], kt + 2)
                    v.tensor_tensor(w[LO][:, kt, :], w_raw[:, kt % 2, :], w[HI][:, kt, :].bitcast(F32), ALU.subtract).then_inc(S["w_split"], 1)
                turn(0, P, P, first=True)
                with dve.Fori(1, TILES - 1) as n:
                    turn(n, P, P)
                turn(TILES - 1, P, SR)
                turn(TILES, SR, 0)
                finish(TILES, SR)

            @block.tensor
            def _(pe):
                def turn_u(n, pn):
                    pe.wait_ge(S["u_done"], n + 1)
                    transpose(u, pn).then_inc(S["u_turned"], 1)

                def transpose(src, pn):
                    for c in range(8):
                        at = (c % 4) * P
                        last = nc.tensor.transpose(ps_t[:, c // 4, at:at + pn], src[0:pn, c * P:(c + 1) * P], k.ident[0:pn, 0:pn])
                    return last

                def products(n, pn, first=False):
                    pe.wait_ge(S["uT_done"], n + 1)
                    if not first:
                        pe.wait_ge(S["y_done"], n)
                    for b in range(2):
                        if first:
                            pe.wait_ge(S["w_split"], (b + 1) * KW)
                        for h in range(2):
                            last = split_product(nc, ps_y[0:pn, 2 * b + h, :], lambda part, kt: uT[part][:, kt, 0:pn],
                                                 lambda part, kt: w[part][:, kt, h * 512:(h + 1) * 512],
                                                 three_terms(range(b * KW, (b + 1) * KW)))
                    last.then_inc(S["y_ready"], 1)

                def project_out(n, pn):
                    pe.wait_ge(S["yT_done"], n + 1)
                    pe.wait_ge(S["scaled"], n + 1)
                    for h in range(2):
                        last = split_product(nc, ps_o[0:pn, h, :], lambda part, kt: yT[part][:, kt, 0:pn],
                                             lambda part, kt: w[part][:, 2 * KW + kt, h * 512:(h + 1) * 512],
                                             three_terms(range(KD)))
                    last.then_inc(S["o_ready"], 1)

                def turn(n, pn, nxt, first=False):
                    products(n, pn, first)
                    if not first:
                        project_out(n - 1, P)
                    if nxt:
                        turn_u(n + 1, nxt)
                        pe.wait_ge(S["uT_done"], n + 2)
                    pe.wait_ge(S["y_done"], n + 1)
                    transpose(y, pn).then_inc(S["y_turned"], 1)

                pe.sem_inc(S["o_ready"], 1)
                turn_u(0, P)
                turn(0, P, P, first=True)
                pe.wait_ge(S["w_split"], KT)
                with pe.Fori(1, TILES - 1) as n:
                    turn(n, P, P)
                turn(TILES - 1, P, SR)
                turn(TILES, SR, 0)
                project_out(TILES, SR)


INPUTS = ["x_prompt", "x_sample", "cache_a_k", "cache_a_v", "cache_b_k", "cache_b_v", "cache_b_logf", "page_table",
          "c_prompt", "c_sample", "w_ada", "b_ada", "w_in", "b_f", "g_q_a", "g_k_a", "g_q_b", "g_k_b",
          "lambda_q1", "lambda_k1", "lambda_q2", "lambda_k2", "g_sub_a", "w_out_a", "w_out_b", "w_o"]
OUTPUTS = [("y_prompt", (1, SEQ, D)), ("y_sample", (NB, NT, D)),
           ("k_a_prompt", (1, 1, SEQ, 2, HA, DH)), ("v_a_prompt", (1, 1, SEQ, HA, DVA)),
           ("k_b_prompt", (1, 1, SEQ, HB, DH)), ("v_b_prompt", (1, 1, SEQ, HB, DH)),
           ("logf_prompt", (1, 1, SEQ, HB)),
           ("k_a_sample", (1, NB, NT, 2, HA, DH)), ("v_a_sample", (1, NB, NT, HA, DVA)),
           ("k_b_sample", (1, NB, NT, HB, DH)), ("v_b_sample", (1, NB, NT, HB, DH)),
           ("logf_sample", (1, NB, NT, HB))]


def declare(nc, arrays):
    t = {n: nc.dram_tensor(f"in_{n}", a.shape, mybir.dt.from_np(a.dtype), kind="ExternalInput").ap()
         for n, a in arrays.items()}
    for name, shape in OUTPUTS:
        ap = nc.dram_tensor(f"out_{name}", shape, F32, kind="ExternalOutput").ap()
        rows = SEQ if name.endswith("prompt") else SR
        letters = "abcdef"[:len(shape)]
        lead = 2 if name[0] == "y" else 3
        t[name] = ap.rearrange(f"{' '.join(letters)} -> ({' '.join(letters[:lead])}) ({' '.join(letters[lead:])})")
        assert t[name].shape[0] == rows
    return t


def kernel(**inputs):
    import concourse.bacc as bacc
    from concourse.bass_utils import run_bass_kernel_spmd

    nc = bacc.Bacc("TRN2", target_bir_lowering=False, num_devices=1)
    arrays = {n: np.ascontiguousarray(inputs[n]) for n in INPUTS}
    program(nc, declare(nc, arrays))
    r = run_bass_kernel_spmd(nc, [{f"in_{n}": a for n, a in arrays.items()}], core_ids=[0])
    return tuple(r.results[0][f"out_{n}"] for n, _ in OUTPUTS)
```

```python
from contextlib import ExitStack

import numpy as np

import concourse.bass as bass
from concourse import mybir

P = 128
F32 = mybir.dt.float32
F32R = mybir.dt.float32r
BF16 = mybir.dt.bfloat16
I32 = mybir.dt.int32
ALU = mybir.AluOpType
ACT = mybir.ActivationFunctionType
AX = mybir.AxisListType
ds = bass.ds

D = 1024
KD = D // P
SEQ = 2048
NB, NT = 8, 4
SR = NB * NT
HA, HB, DH, DVA = 4, 8, 64, 128
W = 512
NPG, PG = 4, 128
PAST = NPG * PG
TILES = SEQ // P
HALF = TILES // 2
GROUP = 4
NU = 2 * HA + HB
EPS = 1e-6
NEG = -1e30
LAM_INIT = 0.8 - 0.6
SLOPES = [2.0 ** (-8.0 * (h + 1) / HA) for h in range(HA)]
C_QA, C_KA, C_VA, C_GA = 0, W, 2 * W, 3 * W
C_QB, C_KB, C_VB, C_F = 4 * W, 5 * W, 6 * W, 7 * W
C_GB = C_F + HB
C_M = C_GB + W


class Tally:

    def __init__(self, sem, base=0):
        self.sem, self.base, self.n = sem, base, 0

    def inc(self, ins):
        self.n += 1
        ins.then_inc(self.sem, 1)

    def wait(self, eng):
        eng.wait_ge(self.sem, self.base + self.n)


class Store:
    pass


def program(nc, t):
    with ExitStack() as ctx:
        k = Store()
        k.nc, k.t, k.ctx = nc, t, ctx
        persistent(k)
        constants(k)
        modulation(k)
        for half in range(2):
            with ExitStack() as c2:
                rows = HALF * P + (SR if half else 0)
                k.h_hi = c2.enter_context(nc.sbuf_tensor(f"h_hi{half}", [P, KD, rows], F32R))
                k.h_lo = c2.enter_context(nc.sbuf_tensor(f"h_lo{half}", [P, KD, rows], F32R))
                normalise(k, half)
                project(k, half)
        forget(k)
        maxima(k)
        attention_a(k)
        attention_b(k)
        recycle(k)
        sample(k)
        merge(k)


def tools(k, ctx, tag):
    nc = k.nc

    def sb(name, shape, dt=F32):
        return ctx.enter_context(nc.sbuf_tensor(f"{tag}_{name}", shape, dt))

    def ps(name, shape, dt=F32):
        return ctx.enter_context(nc.psum_tensor(f"{tag}_{name}", shape, dt))

    def sem(name):
        k.sems.append(nc.alloc_semaphore(f"{tag}_{name}"))
        return k.sems[-1]

    return sb, ps, sem


def recycle(k):
    with k.nc.Block() as block:
        @block.gpsimd
        def _(pool):
            k.nc.clear_and_free_semaphores(k.sems)
    k.sems = []


def persistent(k):
    k.sems = []
    nc = k.nc
    sb, _, _ = tools(k, k.ctx, "keep")

    def dram(name, shape, dt=F32):
        return nc.dram_tensor(f"scratch_{name}", shape, dt, kind="Internal").ap()

    k.q_hi, k.q_lo = dram("q_hi", [NU // 2, P, SEQ]), dram("q_lo", [NU // 2, P, SEQ])
    k.k_hi, k.k_lo = dram("k_hi", [NU // 2, P, SEQ]), dram("k_lo", [NU // 2, P, SEQ])
    k.gates = dram("gates", [SEQ + SR, 2 * W])
    k.mixes = dram("mixes", [SEQ + SR, 2 * D])
    k.ada_gate = dram("ada_gate", [SR + 1, D])
    k.bias_row = dram("bias_row", [2, NU * TILES, P])
    k.bias_col = dram("bias_col", [NU, P, TILES])
    k.neg_max = dram("neg_max", [2, NU * TILES, P])
    k.o_a, k.o_b = dram("o_a", [SEQ + SR, W]), dram("o_b", [SEQ + SR, W])

    k.pages = sb("pages", [1, NB * NPG], I32)
    k.lf = sb("lf", [P, NPG, NB, HB])
    k.ident = sb("ident", [P, P])
    k.ident_b = sb("ident_b", [P, P], BF16)
    k.mask_k = sb("mask_k", [P, P], BF16)
    k.mask_q = sb("mask_q", [P, P], BF16)
    k.neg_half = sb("neg_half", [P, 8])
    k.neg_lam = sb("neg_lam", [P, 1])
    k.shiftT = sb("shiftT", [P, KD, SR + 1])
    k.scaleT = sb("scaleT", [P, KD, SR + 1])
    k.logf = sb("logf", [P, TILES + 1, HB])
    k.max_shift = sb("max_shift", [P, NU, TILES])
    k.qT_s = sb("qT_s", [P, 2, 4, SR])
    k.kT_s = sb("kT_s", [P, 2, 4, SR])
    k.v_s = sb("v_s", [SR, 2, W])


def constants(k):
    nc, t = k.nc, k.t
    with ExitStack() as ctx:
        sb, ps, sem = tools(k, ctx, "const")
        lam_in = sb("lam_in", [P, 4, DH])
        prod = sb("prod", [P, 2, DH])
        dots = sb("dots", [P, 2])
        exps = sb("exps", [P, 2])
        loaded, filled, dots_done, exps_done = (sem(n) for n in ("loaded", "filled", "dots", "exps"))
        steps = sem("steps")
        with nc.Block() as block:
            @block.sync
            def _(sp):
                for n, name in enumerate(("lambda_q1", "lambda_k1", "lambda_q2", "lambda_k2")):
                    sp.dma_start(lam_in[:, n, :], t[name].to_broadcast([P, DH])).then_inc(loaded, 16)

            @block.gpsimd
            def _(pool):
                nc.gpsimd.memset(k.neg_half[:], -0.5)
                nc.gpsimd.memset(k.logf[:], 0.0)
                nc.gpsimd.memset(k.ident[:], 0.0).then_inc(filled, 1)
                nc.gpsimd.memset(k.ident_b[:], 0.0).then_inc(filled, 1)
                nc.gpsimd.memset(k.mask_k[:], 0.0).then_inc(filled, 1)
                nc.gpsimd.memset(k.mask_q[:], 0.0).then_inc(filled, 1)
                pool.wait_ge(filled, 4)
                for m in (k.ident, k.ident_b):
                    nc.gpsimd.affine_select(out=m[:], in_=m[:], compare_op=ALU.not_equal, fill=1.0,
                                            base=0, pattern=[[-1, P]], channel_multiplier=1)
                nc.gpsimd.affine_select(out=k.mask_k[:], in_=k.mask_k[:], compare_op=ALU.is_ge, fill=NEG,
                                        base=0, pattern=[[-1, P]], channel_multiplier=1)
                nc.gpsimd.affine_select(out=k.mask_q[:], in_=k.mask_q[:], compare_op=ALU.is_ge, fill=NEG,
                                        base=0, pattern=[[1, P]], channel_multiplier=-1)

            @block.vector
            def _(dve):
                step = Tally(steps)
                dve.wait_ge(loaded, 64)
                pairs = lam_in[:].rearrange("p (n two) d -> p n two d", two=2)
                step.inc(nc.vector.tensor_tensor(prod[:], pairs[:, :, 0, :], pairs[:, :, 1, :], ALU.mult))
                step.wait(dve)
                nc.vector.reduce_sum(dots[:], prod[:], AX.X).then_inc(dots_done, 1)
                dve.wait_ge(exps_done, 1)
                step.inc(nc.vector.tensor_tensor(k.neg_lam[:], exps[:, 1:2], exps[:, 0:1], ALU.subtract))
                step.wait(dve)
                nc.vector.tensor_scalar(k.neg_lam[:], k.neg_lam[:], -LAM_INIT, None, ALU.add)

            @block.scalar
            def _(act):
                act.wait_ge(dots_done, 1)
                nc.scalar.activation(exps[:], dots[:], ACT.Exp).then_inc(exps_done, 1)


def modulation(k):
    nc, t = k.nc, k.t
    RING = 3
    NC = 3 * D // 512
    R = SR + 1
    with ExitStack() as ctx:
        sb, ps, sem = tools(k, ctx, "ada")
        c_in = sb("c_in", [R, D])
        c_silu = sb("c_silu", [R, D])
        cT = sb("cT", [P, KD, R])
        w = sb("w", [P, RING, 3 * D])
        bias = sb("bias", [R, 3 * D])
        ada = sb("ada", [R, 3 * D])
        acc = ps("acc", [R, NC, 512])
        ps_t = ps("ps_t", [P, 2, 512])
        c_loaded, b_loaded, stored = sem("c_loaded"), sem("b_loaded"), sem("stored")
        w_loaded = [sem(f"w_loaded{i}") for i in range(RING)]
        sig_done, silu_done, cT_ready, cT_copied = (sem(n) for n in ("sig", "silu", "cT_ready", "cT_copied"))
        w_used, ada_done, turned = (sem(n) for n in ("w_used", "ada_done", "turned"))
        with nc.Block() as block:
            @block.sync
            def _(sp):
                for s in range(NT):
                    sp.dma_start(c_in[s:SR:NT, :], t["c_sample"]).then_inc(c_loaded, 16)
                sp.dma_start(c_in[SR:R, :], t["c_prompt"]).then_inc(c_loaded, 16)
                for kt in range(KD):
                    if kt >= RING:
                        sp.wait_ge(w_used, kt - RING + 1)
                    sp.dma_start(w[:, kt % RING, :], t["w_ada"][0, kt * P:(kt + 1) * P, :]).then_inc(w_loaded[kt % RING], 16)
                    if kt == 1:
                        sp.dma_start(bias[:], t["b_ada"].to_broadcast([R, 3 * D])).then_inc(b_loaded, 16)
                sp.wait_ge(ada_done, 2)
                sp.dma_start(k.ada_gate, ada[:, 2 * D:3 * D]).then_inc(stored, 16)
                sp.wait_ge(stored, 16)

            @block.scalar
            def _(act):
                act.wait_ge(c_loaded, 80)
                nc.scalar.activation(c_silu[:], c_in[:], ACT.Sigmoid).then_inc(sig_done, 1)

            @block.vector
            def _(dve):
                dve.wait_ge(sig_done, 1)
                nc.vector.tensor_tensor(c_silu[:], c_silu[:], c_in[:], ALU.mult).then_inc(silu_done, 1)
                dve.wait_ge(cT_ready, 1)
                nc.vector.tensor_copy(cT[:].rearrange("p a b -> p (a b)"), ps_t[:, 0, 0:KD * R]).then_inc(cT_copied, 1)
                dve.wait_ge(b_loaded, 16)
                dve.wait_ge(w_used, KD)
                nc.vector.tensor_tensor(ada[:], acc[:].rearrange("p a b -> p (a b)"), bias[:], ALU.add).then_inc(ada_done, 1)
                dve.wait_ge(ada_done, 1)
                nc.vector.tensor_scalar(ada[:, D:2 * D], ada[:, D:2 * D], 1.0, None, ALU.add).then_inc(ada_done, 1)
                for n, out in enumerate((k.shiftT, k.scaleT)):
                    dve.wait_ge(turned, n + 1)
                    nc.vector.tensor_copy(out[:].rearrange("p a b -> p (a b)"), ps_t[:, n, 0:KD * R])

            @block.tensor
            def _(pe):
                pe.wait_ge(silu_done, 1)
                for kt in range(KD):
                    last = nc.tensor.transpose(ps_t[:, 0, kt * R:(kt + 1) * R], c_silu[:, kt * P:(kt + 1) * P], k.ident[0:R, 0:R])
                last.then_inc(cT_ready, 1)
                pe.wait_ge(cT_copied, 1)
                for kt in range(KD):
                    pe.wait_ge(w_loaded[kt % RING], 16 * (kt // RING + 1))
                    for n in range(NC):
                        last = nc.tensor.matmul(acc[:, n, :], cT[:, kt, :], w[:, kt % RING, n * 512:(n + 1) * 512],
                                                start=(kt == 0), stop=(kt == KD - 1))
                    last.then_inc(w_used, 1)
                pe.wait_ge(ada_done, 2)
                for n in range(2):
                    for kt in range(KD):
                        c = n * D + kt * P
                        last = nc.tensor.transpose(ps_t[:, n, kt * R:(kt + 1) * R], ada[:, c:c + P], k.ident[0:R, 0:R])
                    last.then_inc(turned, 1)


def normalise(k, half):
    nc, t = k.nc, k.t
    NG = HALF // GROUP
    x_v = t["x_prompt"][0].rearrange("(g t p) d -> g p t d", t=GROUP, p=P)
    xs_v = t["x_sample"].rearrange("b t d -> (b t) d")
    groups = [(g, P, GROUP) for g in range(NG)] + ([(NG, SR, 1)] if half else [])
    with ExitStack() as ctx:
        sb, ps, sem = tools(k, ctx, f"norm{half}")
        x_in = sb("x_in", [P, 2, GROUP, D])
        xn = sb("xn", [P, GROUP, D])
        junk = sb("junk", [P, 2, D])
        ss = sb("ss", [P, 2, GROUP])
        rstd = sb("rstd", [P, 2, GROUP])
        hf = sb("hf", [P, 2, 512])
        ps_t = ps("ps_t", [P, 4, 512])
        loaded = [sem("loaded0"), sem("loaded1")]
        ss_done, rstd_done, xn_done, turned, hf_done, lo_done = (
            sem(n) for n in ("ss_done", "rstd_done", "xn_done", "turned", "hf_done", "lo_done"))
        with nc.Block() as block:
            @block.sync
            def _(sp):
                for g, pn, tn in groups:
                    if g >= 2:
                        sp.wait_ge(xn_done, g - 1)
                    src = x_v[half * NG + g] if tn == GROUP else xs_v
                    dst = x_in[0:pn, g % 2, :, :] if tn == GROUP else x_in[0:pn, g % 2, 0, :]
                    sp.dma_start(dst, src).then_inc(loaded[g % 2], 16)

            @block.gpsimd
            def _(pool):
                for g, pn, tn in groups:
                    pool.wait_ge(rstd_done, 2 * g + 1)
                    nc.gpsimd.tensor_tensor(rstd[0:pn, g % 2, 0:tn], rstd[0:pn, g % 2, 0:tn], k.neg_half[0:pn, 0:tn], ALU.pow).then_inc(rstd_done, 1)

            @block.scalar
            def _(act):
                n = 0
                for g, pn, tn in groups:
                    act.wait_ge(loaded[g % 2], 16 * (g // 2 + 1))
                    if g >= 2:
                        act.wait_ge(rstd_done, 2 * (g - 2) + 1)
                    for j in range(tn):
                        q = g * GROUP + j
                        if q >= 2:
                            act.wait_ge(ss_done, q - 1)
                        nc.scalar.activation(junk[0:pn, q % 2, :], x_in[0:pn, g % 2, j, :], ACT.Square,
                                             accum_out=ss[0:pn, g % 2, j:j + 1]).then_inc(ss_done, 1)
                    if tn == GROUP:
                        for kt in range(KD):
                            act.wait_ge(turned, n + 1)
                            if n >= 2:
                                act.wait_ge(lo_done, n - 1)
                            hi = k.h_hi[:, kt, g * 512:(g + 1) * 512]
                            src = ps_t[:, n % 4, :]
                            sc, sh = k.scaleT[:, kt, SR:SR + 1], k.shiftT[:, kt, SR:SR + 1]
                            nc.scalar.activation(hf[:, n % 2, :], src, ACT.Identity, scale=sc, bias=sh).then_inc(hf_done, 1)
                            nc.scalar.activation(hi, src, ACT.Identity, scale=sc, bias=sh).then_inc(hf_done, 1)
                            n += 1

            @block.vector
            def _(dve):
                n, m, seen = 0, 0, 0
                for g, pn, tn in groups:
                    seen += tn
                    dve.wait_ge(ss_done, seen)
                    nc.vector.tensor_scalar(rstd[0:pn, g % 2, 0:tn], ss[0:pn, g % 2, 0:tn], 1.0 / D, EPS, ALU.mult, ALU.add).then_inc(rstd_done, 1)
                    dve.wait_ge(rstd_done, 2 * g + 2)
                    if g >= 1:
                        dve.wait_ge(turned, n)
                    for j in range(tn):
                        last = nc.vector.tensor_scalar(xn[0:pn, j, :], x_in[0:pn, g % 2, j, :],
                                                       rstd[0:pn, g % 2, j:j + 1], None, ALU.mult)
                    last.then_inc(xn_done, 1)
                    for kt in range(KD):
                        cols = slice(g * 512, g * 512 + pn * tn)
                        if tn == GROUP:
                            m += 2
                            dve.wait_ge(hf_done, m)
                        else:
                            dve.wait_ge(turned, n + 1)
                            nc.vector.tensor_tensor(hf[:, n % 2, 0:SR], ps_t[:, n % 4, 0:SR], k.scaleT[:, kt, 0:SR], ALU.mult).then_inc(hf_done, 1)
                            m += 1
                            dve.wait_ge(hf_done, m)
                            nc.vector.tensor_tensor(hf[:, n % 2, 0:SR], hf[:, n % 2, 0:SR], k.shiftT[:, kt, 0:SR], ALU.add).then_inc(hf_done, 1)
                            m += 1
                            dve.wait_ge(hf_done, m)
                            nc.vector.tensor_copy(k.h_hi[:, kt, cols], hf[:, n % 2, 0:SR]).then_inc(hf_done, 1)
                            m += 1
                            dve.wait_ge(hf_done, m)
                        nc.vector.tensor_tensor(k.h_lo[:, kt, cols], hf[:, n % 2, 0:pn * tn],
                                                k.h_hi[:, kt, cols].bitcast(F32), ALU.subtract).then_inc(lo_done, 1)
                        n += 1

            @block.tensor
            def _(pe):
                n = 0
                for g, pn, tn in groups:
                    pe.wait_ge(xn_done, g + 1)
                    for kt in range(KD):
                        if n >= 4:
                            pe.wait_ge(lo_done, n - 3)
                        for j in range(tn):
                            last = nc.tensor.transpose(ps_t[:, n % 4, j * P:j * P + pn], xn[0:pn, j, kt * P:(kt + 1) * P],
                                                       k.ident[0:pn, 0:pn])
                        last.then_inc(turned, 1)
                        n += 1


def split_product(nc, out, left, right, terms, first=True, last=True):
    for n, (lt, rt) in enumerate(terms):
        ins = nc.tensor.matmul(out, left(*lt), right(*rt), start=first and n == 0, stop=last and n == len(terms) - 1)
    return ins


HI, LO = 0, 1


def three_terms(kts):
    return [((lp, kt), (rp, kt)) for kt in kts for lp, rp in ((HI, HI), (HI, LO), (LO, HI))]


def project(k, half):
    nc, t = k.nc, k.t
    T = HALF + half
    R = 4 if T % 2 == 0 else 3
    row0 = half * HALF * P
    w_in = t["w_in"][0]
    g_names = ("g_q_a", "g_k_a", "g_q_b", "g_k_b")
    chunks = [("gate", 0, C_GA), ("gate", 1, C_GB), ("v", 0, C_VA), ("v", 1, C_VB),
              ("k", 0, C_KA), ("k", 1, C_KB), ("q", 0, C_QA), ("q", 1, C_QB)]
    NM = 4
    tiles = [(c, j, kind, b) for c, (kind, b, _) in enumerate(chunks) for j in range(T)]
    M0 = NM * T

    def rows_of(j):
        return P if j < HALF else SR

    def dram_rows(ap, j):
        r = row0 + j * P if j < HALF else SEQ
        return ap[r:r + rows_of(j)]

    def out_rows(name, j):
        if j < HALF:
            r = row0 + j * P
            return t[f"{name}_prompt"][r:r + P, :]
        return t[f"{name}_sample"]

    turned_tiles = [n for n, (_, _, kind, _) in enumerate(tiles) if kind in "qk"]
    turn_index = {n: i for i, n in enumerate(turned_tiles)}
    parts_index = {n: i for i, n in enumerate(x for x in turned_tiles if tiles[x][1] < HALF)}
    dve_tiles = [n for n, (_, _, kind, _) in enumerate(tiles) if kind != "v"]
    dve_before = {n: sum(x <= n for x in dve_tiles) for n in range(-2, len(tiles))}
    stored_before, seen = [], [NM * T // R + 1] * R
    for n, (_, _, kind, _) in enumerate(tiles):
        stored_before.append(list(seen))
        if kind != "q":
            seen[n % R] += 1
    assert M0 % R == 0

    with ExitStack() as ctx:
        sb, ps, sem = tools(k, ctx, f"proj{half}")
        w_raw = sb("w_raw", [P, KD, 512])
        w_parts = [sb("w_hi", [P, 2, KD, 512], F32R), sb("w_lo", [P, 2, KD, 512], F32R)]
        wf_raw = sb("wf_raw", [P, KD, HB])
        wf_parts = [sb("wf_hi", [P, KD, HB], F32R), sb("wf_lo", [P, KD, HB], F32R)]
        gains = sb("gains", [P, 4, DH])
        z_sb = sb("z_sb", [P, 2, 512])
        sq = sb("sq", [P, 2, 512])
        ss = sb("ss", [P, 8])
        rstd = sb("rstd", [P, 8])
        out = sb("out", [P, R, 512])
        turned_parts = [sb("t_hi", [P, 2, 4, P], F32R), sb("t_lo", [P, 2, 4, P], F32R)]
        z = ps("z", [P, R, 512])
        ps_t = ps("ps_t", [P, 2, 4, P])
        ps_f = ps("ps_f", [P, 512])
        w_loaded = [sem(f"w_loaded{i}") for i in range(KD)]
        g_loaded, wf_loaded = sem("g_loaded"), sem("wf_loaded")
        stored = [sem(f"stored{i}") for i in range(R)]
        parts_stored = [sem("parts_stored0"), sem("parts_stored1")]
        (w_split, z_done, z_read, norm_done, norm_steps, turned, t_hi_done, t_done, wf_split, f_done,
         mean_done, rstd_done) = (sem(n) for n in (
             "w_split", "z_done", "z_read", "norm_done", "norm_steps", "turned",
                             "t_hi_done", "t_done", "wf_split", "f_done", "mean_done", "rstd_done"))
        h_parts = [k.h_hi, k.h_lo]

        def hT(part, kt, j):
            return h_parts[part][:, kt, j * P:j * P + rows_of(j)]

        with nc.Block() as block:
            def store_parts(sp, n):
                _, j, kind, b = tiles[n]
                i, r = parts_index[n], row0 + j * P
                sp.wait_ge(t_done, turn_index[n] + 1)
                for part, dst in zip(turned_parts, (k.q_hi, k.q_lo) if kind == "q" else (k.k_hi, k.k_lo)):
                    sp.dma_start(dst[4 * b:4 * b + 4, :, r:r + P].rearrange("u p r -> p u r"),
                                 part[:, i % 2, :, :].bitcast(F32)).then_inc(parts_stored[i % 2], 16)

            def turned_high(act, n):
                i = parts_index[n]
                act.wait_ge(turned, turn_index[n] + 1)
                if i >= 2:
                    act.wait_ge(parts_stored[i % 2], 32 * (i // 2))
                nc.scalar.activation(turned_parts[HI][:, i % 2, :, :], ps_t[:, turn_index[n] % 2, :, :],
                                     ACT.Copy).then_inc(t_hi_done, 1)

            def turned_low(dve, n):
                _, j, kind, b = tiles[n]
                q = turn_index[n]
                if n in parts_index:
                    i = parts_index[n]
                    dve.wait_ge(t_hi_done, i + 1)
                    nc.vector.tensor_tensor(turned_parts[LO][:, i % 2, :, :], ps_t[:, q % 2, :, :],
                                            turned_parts[HI][:, i % 2, :, :].bitcast(F32), ALU.subtract).then_inc(t_done, 1)
                else:
                    dve.wait_ge(turned, q + 1)
                    dst = (k.qT_s if kind == "q" else k.kT_s)[:, b, :, :]
                    nc.vector.tensor_copy(dst, ps_t[:, q % 2, :, 0:SR]).then_inc(t_done, 1)

            @block.gpsimd
            def _(pool):
                for i, n in enumerate(turned_tiles):
                    pn = rows_of(tiles[n][1])
                    pool.wait_ge(mean_done, i + 1)
                    nc.gpsimd.tensor_tensor(rstd[0:pn, :], rstd[0:pn, :], k.neg_half[0:pn, :], ALU.pow).then_inc(rstd_done, 1)

            @block.sync
            def _(sp):
                for s in range(R):
                    sp.sem_inc(stored[s], 16)
                sp.dma_start(wf_raw[:], w_in[:, C_F:C_F + HB].rearrange("(a p) n -> p a n", p=P)).then_inc(wf_loaded, 16)
                for n, name in enumerate(g_names):
                    sp.dma_start(gains[:, n, :], t[name].to_broadcast([P, DH])).then_inc(g_loaded, 16)
                def load_w(c, kt, col):
                    if not isinstance(c, int) or c > 0:
                        sp.wait_ge(w_split, (c - 1) * KD + (kt + 1))
                    sp.dma_start(w_raw[:, kt, :], w_in[kt * P:(kt + 1) * P, col]).then_inc(w_loaded[kt], 16)

                for c in range(2):
                    for kt in range(KD):
                        load_w(c, kt, slice(C_M + c * 512, C_M + (c + 1) * 512))
                with sp.Fori(0, NM // 2) as i:
                    for c in range(2):
                        first, then = C_M + (c + 2) * 512, chunks[c][2]
                        for kt in range(KD):
                            load_w(i * 2 + (c + 2), kt, ds(first + i * (then - first), 512))
                        for j in range(T):
                            n = c * T + j
                            sp.wait_ge(z_read, i * (2 * T) + (n + 1 + R))
                            sp.dma_start(dram_rows(k.mixes, j)[:, ds(i * 1024 + c * 512, 512)],
                                         out[0:rows_of(j), n % R, :]).then_inc(stored[n % R], 16)
                for n, (c, j, kind, b) in enumerate(tiles):
                    pn = rows_of(j)
                    src = out[0:pn, n % R, :]
                    if kind == "v":
                        sp.wait_ge(z_read, M0 + n + 1 + R)
                        sp.dma_start(out_rows("v_ab"[0:2] + "ab"[b], j), src).then_inc(stored[n % R], 16)
                    else:
                        sp.wait_ge(norm_done, dve_before[n])
                        if kind == "gate":
                            sp.dma_start(dram_rows(k.gates, j)[:, b * W:(b + 1) * W], src).then_inc(stored[n % R], 16)
                        elif kind == "k":
                            sp.dma_start(out_rows("k_" + "ab"[b], j), src).then_inc(stored[n % R], 16)
                    if n - 1 in parts_index:
                        store_parts(sp, n - 1)
                    if c + 2 < len(chunks) and j < KD:
                        col = chunks[c + 2][2]
                        load_w(NM + c + 2, j, slice(col, col + 512))
                if len(tiles) - 1 in parts_index:
                    store_parts(sp, len(tiles) - 1)
                for s in range(R):
                    sp.wait_ge(stored[s], 16 * seen[s])
                for s in range(2):
                    sp.wait_ge(parts_stored[s], 32 * len(range(s, len(parts_index), 2)))

            @block.scalar
            def _(act):
                act.sem_inc(z_read, R)
                with act.Fori(0, NM // 2) as i:
                    for n in range(2 * T):
                        pn = rows_of(n % T)
                        act.wait_ge(z_done, i * (2 * T) + (n + 1))
                        act.wait_ge(stored[n % R], 16 * (i * (2 * T // R) + (n // R + 1)))
                        nc.scalar.activation(out[0:pn, n % R, :], z[0:pn, n % R, :], ACT.Sigmoid).then_inc(z_read, 1)
                for n, (c, j, kind, b) in enumerate(tiles):
                    pn = rows_of(j)
                    src = z[0:pn, n % R, :]
                    act.wait_ge(z_done, M0 + n + 1)
                    if kind == "v":
                        act.wait_ge(stored[n % R], 16 * stored_before[n][n % R])
                        if n >= R and tiles[n - R][2] != "v":
                            act.wait_ge(norm_done, dve_before[n - R])
                        if j == HALF:
                            nc.scalar.activation(k.v_s[:, b, :], src, ACT.Copy)
                        nc.scalar.activation(out[0:pn, n % R, :], src, ACT.Copy).then_inc(z_read, 1)
                    else:
                        if n >= 2 and dve_before[n - 2]:
                            act.wait_ge(norm_done, dve_before[n - 2])
                        nc.scalar.activation(z_sb[0:pn, n % 2, :], src, ACT.Copy)
                        func = ACT.Sigmoid if kind == "gate" else ACT.Square
                        nc.scalar.activation(sq[0:pn, n % 2, :], src, func).then_inc(z_read, 1)
                    if n - 1 in parts_index:
                        turned_high(act, n - 1)
                if len(tiles) - 1 in parts_index:
                    turned_high(act, len(tiles) - 1)

            @block.vector
            def _(dve):
                step = Tally(norm_steps)
                dve.wait_ge(wf_loaded, 16)
                nc.vector.tensor_copy(wf_parts[HI][:], wf_raw[:]).then_inc(wf_split, 1)
                dve.wait_ge(wf_split, 1)
                nc.vector.tensor_tensor(wf_parts[LO][:], wf_raw[:], wf_parts[HI][:].bitcast(F32), ALU.subtract).then_inc(wf_split, 1)

                def split(c, par, kt):
                    dve.wait_ge(w_loaded[kt], 16 * (c + 1))
                    step.inc(nc.vector.tensor_copy(w_parts[HI][:, par, kt, :], w_raw[:, kt, :]))
                    step.wait(dve)
                    nc.vector.tensor_tensor(w_parts[LO][:, par, kt, :], w_raw[:, kt, :],
                                            w_parts[HI][:, par, kt, :].bitcast(F32), ALU.subtract).then_inc(w_split, 1)

                for c in range(2):
                    for kt in range(KD):
                        split(c, c, kt)
                with dve.Fori(1, NM // 2) as i:
                    step = Tally(norm_steps, 2 * KD * i)
                    for c in range(2):
                        dve.wait_ge(z_done, i * (2 * T) + (c - 1) * T)
                        for kt in range(KD):
                            split(i * 2 + c, c, kt)
                step = Tally(norm_steps, NM * KD)
                dve.wait_ge(f_done, 1)
                nc.vector.tensor_copy(k.logf[:, half * HALF:(half + 1) * HALF, :].rearrange("p a b -> p (a b)"), ps_f[:, 0:HALF * HB])
                if half:
                    nc.vector.tensor_copy(k.logf[0:SR, TILES, :], ps_f[0:SR, HALF * HB:(HALF + 1) * HB])
                dve.wait_ge(z_done, (NM - 1) * T)
                for kt in range(KD):
                    split(NM, NM % 2, kt)
                dve.wait_ge(g_loaded, 64)
                for n in (0, 2):
                    nc.vector.tensor_scalar(gains[:, n, :], gains[:, n, :], DH ** -0.5, None, ALU.mult)
                for n, (c, j, kind, b) in enumerate(tiles):
                    pn = rows_of(j)
                    if kind != "v":
                        dve.wait_ge(z_read, M0 + n + 1 + R)
                        dve.wait_ge(stored[n % R], 16 * stored_before[n][n % R])
                        if n - R in turn_index:
                            dve.wait_ge(turned, turn_index[n - R] + 1)
                        dst = out[0:pn, n % R, :]
                        zi, si = z_sb[0:pn, n % 2, :], sq[0:pn, n % 2, :]
                    if kind == "gate":
                        nc.vector.tensor_tensor(dst, zi, si, ALU.mult).then_inc(norm_done, 1)
                    elif kind != "v":
                        step.inc(nc.vector.reduce_sum(ss[0:pn, :], si.rearrange("p (u d) -> p u d", d=DH), AX.X))
                        step.wait(dve)
                        nc.vector.tensor_scalar(rstd[0:pn, :], ss[0:pn, :], 1.0 / DH, EPS, ALU.mult, ALU.add).then_inc(mean_done, 1)
                    if n - 1 in turn_index:
                        turned_low(dve, n - 1)
                    if c + 1 < len(chunks) and j < KD:
                        if j == 0:
                            dve.wait_ge(z_done, M0 + c * T)
                        split(NM + c + 1, (NM + c + 1) % 2, j)
                    if kind in "qk":
                        z3 = zi.rearrange("p (u d) -> p u d", d=DH)
                        dve.wait_ge(rstd_done, turn_index[n] + 1)
                        step.inc(nc.vector.tensor_tensor(z3, z3, rstd[0:pn, :].unsqueeze(2).to_broadcast([pn, 8, DH]), ALU.mult))
                        step.wait(dve)
                        gain = gains[0:pn, 2 * b + (kind == "k"), :].unsqueeze(1).to_broadcast([pn, 8, DH])
                        nc.vector.tensor_tensor(dst.rearrange("p (u d) -> p u d", d=DH), z3, gain, ALU.mult).then_inc(norm_done, 1)
                if len(tiles) - 1 in turn_index:
                    turned_low(dve, len(tiles) - 1)

            @block.tensor
            def _(pe):
                pe.wait_ge(wf_split, 2)
                for j in range(T):
                    last = split_product(nc, ps_f[0:rows_of(j), j * HB:(j + 1) * HB], lambda part, kt: hT(part, kt, j),
                                         lambda part, kt: wf_parts[part][:, kt, :], three_terms(range(KD)))
                last.then_inc(f_done, 1)

                def tile(par, j, bank):
                    split_product(nc, z[0:rows_of(j), bank, :], lambda part, kt: hT(part, kt, j),
                                  lambda part, kt: w_parts[part][:, par, kt, :],
                                  three_terms(range(KD))).then_inc(z_done, 1)

                def turn(n):
                    pn = rows_of(tiles[n][1])
                    q = turn_index[n]
                    pe.wait_ge(norm_done, dve_before[n])
                    if q >= 2:
                        pe.wait_ge(t_done, q - 1)
                    for p in range(4):
                        last = nc.tensor.transpose(ps_t[:, q % 2, p, 0:pn], out[0:pn, n % R, p * P:(p + 1) * P],
                                                   k.ident[0:pn, 0:pn])
                    last.then_inc(turned, 1)

                with pe.Fori(0, NM // 2) as i:
                    for c in range(2):
                        pe.wait_ge(w_split, i * (2 * KD) + (c + 1) * KD)
                        for j in range(T):
                            n = c * T + j
                            pe.wait_ge(z_read, i * (2 * T) + (n + 1))
                            tile(c, j, n % R)
                for n, (c, j, kind, b) in enumerate(tiles):
                    if j == 0:
                        pe.wait_ge(w_split, (NM + c + 1) * KD)
                    pe.wait_ge(z_read, M0 + n + 1)
                    tile((NM + c) % 2, j, n % R)
                    if n - 1 in turn_index:
                        turn(n - 1)
                if len(tiles) - 1 in turn_index:
                    turn(len(tiles) - 1)


def forget(k):
    nc, t = k.nc, k.t
    ALL = TILES + 1
    with ExitStack() as ctx:
        sb, ps, sem = tools(k, ctx, "forget")
        bf = sb("bf", [P, HB])
        x = sb("x", [P, ALL, HB])
        ab = sb("ab", [P, ALL, HB])
        tri = sb("tri", [P, P])
        ones = sb("ones", [P, P])
        pos = sb("pos", [P, TILES], I32)
        group_pos = sb("group_pos", [P, TILES], I32)
        incl = sb("incl", [P, HB, TILES])
        before = sb("before", [P, HB, TILES])
        bias = sb("bias", [P, NU, TILES])
        bias_c = sb("bias_c", [P, NU, TILES])
        rows_hi = sb("rows_hi", [P, 2, P], F32R)
        rows_lo = sb("rows_lo", [P, 2, P], F32R)
        sums = ps("sums", [P, 2, 512])
        ps_t = ps("ps_t", [P, 2, 512])
        loaded, made, filled, act_step, dve_step = (sem(n) for n in ("loaded", "made", "filled", "act_step", "dve_step"))
        logf_done, summed, bias_done, turned, hi_done, lo_done, stored = (
            sem(n) for n in ("logf_done", "summed", "bias_done", "turned", "hi_done", "lo_done", "stored"))
        x_done = sem("x_done")
        with nc.Block() as block:
            @block.gpsimd
            def _(pool):
                nc.gpsimd.memset(ones[:], 1.0)
                nc.gpsimd.memset(tri[:], 1.0).then_inc(filled, 1)
                pool.wait_ge(filled, 1)
                nc.gpsimd.affine_select(out=tri[:], in_=tri[:], compare_op=ALU.is_ge, fill=0.0, base=0,
                                        pattern=[[1, P]], channel_multiplier=-1)
                nc.gpsimd.iota(pos[:], pattern=[[P, TILES]], base=0, channel_multiplier=1)
                nc.gpsimd.iota(group_pos[:], pattern=[[512, TILES // GROUP], [0, GROUP]], base=0,
                               channel_multiplier=0).then_inc(made, 1)

            @block.sync
            def _(sp):
                sp.dma_start(bf[:], t["b_f"].to_broadcast([P, HB])).then_inc(loaded, 16)
                sp.wait_ge(logf_done, 1)
                sp.dma_start(t["logf_prompt"].rearrange("(t p) h -> p t h", p=P), k.logf[:, 0:TILES, :]).then_inc(stored, 16)
                sp.dma_start(t["logf_sample"], k.logf[0:SR, TILES, :]).then_inc(stored, 16)
                sp.wait_ge(bias_done, 2)
                sp.dma_start(k.bias_col.rearrange("u p t -> p u t"), bias_c[:]).then_inc(stored, 16)
                sp.wait_ge(lo_done, 1)
                for part, rows in ((HI, rows_hi), (LO, rows_lo)):
                    sp.dma_start(k.bias_row[part].rearrange("(g r) p -> r g p", g=2), rows[:].bitcast(F32)).then_inc(stored, 16)
                sp.wait_ge(stored, 80)

            @block.scalar
            def _(act):
                step = Tally(act_step)
                act.wait_ge(x_done, 1)
                step.inc(nc.scalar.activation(ab[:], x[:], ACT.Abs))
                step.wait(act)
                step.inc(nc.scalar.activation(ab[:], ab[:], ACT.Exp, scale=-1.0))
                step.wait(act)
                step.inc(nc.scalar.activation(ab[:], ab[:], ACT.Ln, bias=1.0))
                act.wait_ge(turned, 1)
                nc.scalar.activation(rows_hi[:], ps_t[:, :, 0:P], ACT.Copy).then_inc(hi_done, 1)

            @block.vector
            def _(dve):
                step = Tally(dve_step)
                dve.wait_ge(loaded, 16)
                nc.vector.tensor_tensor(x[:], k.logf[:], bf[:].unsqueeze(1).to_broadcast([P, ALL, HB]), ALU.add).then_inc(x_done, 1)
                dve.wait_ge(act_step, 3)
                step.inc(nc.vector.tensor_scalar(x[:], x[:], 0.0, None, ALU.min))
                step.wait(dve)
                nc.vector.tensor_tensor(k.logf[:], x[:], ab[:], ALU.subtract).then_inc(logf_done, 1)
                dve.wait_ge(made, 1)
                for u in range(2 * HA):
                    slope = SLOPES[u % HA]
                    step.inc(nc.vector.tensor_scalar(bias[:, u, :], pos[:], slope, None, ALU.mult))
                    nc.vector.tensor_scalar(k.max_shift[:, u, :], group_pos[:], slope, None, ALU.mult)
                step.inc(nc.vector.memset(k.max_shift[:, 2 * HA:NU, :], 0.0))
                step.wait(dve)
                for u in range(2 * HA):
                    nc.vector.tensor_scalar(bias_c[:, u, :], bias[:, u, :], -SLOPES[u % HA] * (SEQ - 512), None, ALU.add)
                dve.wait_ge(summed, 2)
                within = sums[:, 0, 0:TILES * HB].rearrange("p (t h) -> p h t", h=HB)
                total = sums[:, 1, 0:TILES * HB].rearrange("p (t h) -> p h t", h=HB)
                for h in range(HB):
                    last = nc.vector.tensor_tensor_scan(incl[:, h, :], ones[:, 0:TILES], total[:, h, :], 0.0, ALU.mult, ALU.add)
                step.inc(last)
                step.wait(dve)
                step.inc(nc.vector.tensor_tensor(before[:], total, incl[:], ALU.subtract))
                step.wait(dve)
                nc.vector.tensor_tensor(bias[:, 2 * HA:NU, :], before[:], within, ALU.subtract).then_inc(bias_done, 1)
                dve.wait_ge(bias_done, 1)
                nc.vector.tensor_copy(bias_c[:, 2 * HA:NU, :], bias[:, 2 * HA:NU, :]).then_inc(bias_done, 1)
                dve.wait_ge(hi_done, 1)
                nc.vector.tensor_tensor(rows_lo[:], ps_t[:, :, 0:P], rows_hi[:].bitcast(F32), ALU.subtract).then_inc(lo_done, 1)

            @block.tensor
            def _(pe):
                pe.wait_ge(made, 1)
                pe.wait_ge(logf_done, 1)
                rhs = k.logf[:, 0:TILES, :].rearrange("p t h -> p (t h)")
                for n, m in enumerate((tri, ones)):
                    nc.tensor.matmul(sums[:, n, 0:TILES * HB], m[:], rhs, start=True, stop=True).then_inc(summed, 1)
                pe.wait_ge(bias_done, 1)
                flat = bias[:].rearrange("p u t -> p (u t)")
                for g in range(2):
                    last = nc.tensor.transpose(ps_t[:, g, 0:P], flat[:, g * P:(g + 1) * P], k.ident[:])
                last.then_inc(turned, 1)


def maxima(k):
    nc, t = k.nc, k.t
    A = DH + 2
    q_u = k.q_hi.rearrange("a (b d) s -> (a b) d s", b=2)
    k_u = k.k_hi.rearrange("a (b d) s -> (a b) d s", b=2)
    bias_u = k.bias_row.rearrange("c (u t) p -> u c (t p)", t=TILES)
    N = 2 * TILES
    with ExitStack() as ctx:
        sb, ps, sem = tools(k, ctx, "max")
        q = [sb(f"q{s}", [A, SEQ], F32R) for s in range(2)]
        kb = [sb(f"kb{s}", [A, SEQ], F32R) for s in range(2)]
        ones = sb("ones", [A, SEQ])
        top = sb("top", [P, NU, TILES])
        neg = sb("neg", [P, NU, TILES])
        rows = [sb("rows_hi", [P, 2, P], F32R), sb("rows_lo", [P, 2, P], F32R)]
        s_ps = ps("s_ps", [P, 2, 4 * 512])
        loaded = [sem("loaded0"), sem("loaded1")]
        pages_in, lf_in = sem("pages_in"), sem("lf_in")
        ones_done, s_done, max_done, neg_done, turned, hi_done, lo_done, stored = (
            sem(n) for n in ("ones_done", "s_done", "max_done", "neg_done", "turned", "hi_done", "lo_done", "stored"))
        with nc.Block() as block:
            @block.sync
            def _(sp):
                def load(u, s):
                    sp.dma_start(q[s][0:DH, :].bitcast(F32).unsqueeze(1), q_u[ds(u, 1)].rearrange("u d s -> d u s")).then_inc(loaded[s], 16)
                    sp.dma_start(kb[s][0:DH, :].bitcast(F32).unsqueeze(1), k_u[ds(u, 1)].rearrange("u d s -> d u s")).then_inc(loaded[s], 16)
                    sp.dma_start(kb[s][DH:A, :].bitcast(F32).unsqueeze(1), bias_u[ds(u, 1)].rearrange("u c s -> c u s")).then_inc(loaded[s], 16)
                for s in range(2):
                    load(s, s)
                with sp.Fori(1, NU // 2) as i:
                    for s in range(2):
                        sp.wait_ge(s_done, i * N + ((s + 1) * TILES - N))
                        load(i * 2 + s, s)
                sp.wait_ge(lo_done, 1)
                for part in range(2):
                    sp.dma_start(k.neg_max[part].rearrange("(g r) p -> r g p", g=2), rows[part][:].bitcast(F32)).then_inc(stored, 16)
                sp.wait_ge(stored, 32)

            @block.gpsimd
            def _(pool):
                nc.gpsimd.memset(ones[DH:A, :], 1.0).then_inc(ones_done, 1)
                cache_f = t["cache_b_logf"].rearrange("z n r h -> (z n) r h")
                pool.dma_start(k.pages[:], t["page_table"].rearrange("b n -> (b n)").unsqueeze(0)).then_inc(pages_in, 16)
                pool.wait_ge(pages_in, 16)
                with pool.Fori(0, NB) as b:
                    for g in range(NPG):
                        pg = pool.value_load(k.pages[0:1, ds(b * NPG + g, 1)], min_val=0, max_val=cache_f.shape[0] - 1)
                        pool.dma_start(k.lf[:, g, ds(b, 1), :], cache_f[ds(pg, 1)].rearrange("n r h -> r n h")).then_inc(lf_in, 16)
                pool.wait_ge(lf_in, 16 * NB * NPG)

            @block.scalar
            def _(act):
                act.wait_ge(ones_done, 1)
                for s in range(2):
                    nc.scalar.activation(q[s][DH:A, :], ones[DH:A, :], ACT.Copy).then_inc(ones_done, 1)
                act.wait_ge(turned, 1)
                nc.scalar.activation(rows[HI][:], s_ps[:, 0, 0:2 * P].rearrange("p (g c) -> p g c", g=2), ACT.Copy).then_inc(hi_done, 1)

            @block.vector
            def _(dve):
                dve.sem_inc(max_done, 1)
                with dve.Fori(0, NU // 2) as i:
                    for n in range(N):
                        s, qt = n // TILES, n % TILES
                        dve.wait_ge(s_done, i * N + (n + 1))
                        nc.vector.reduce_max(top[:, ds(i * 2 + s, 1), qt], s_ps[:, n % 2, 0:(qt + 1) * P], AX.X).then_inc(max_done, 1)
                dve.wait_ge(max_done, NU * TILES + 1)
                nc.vector.tensor_tensor(neg[:], k.max_shift[:], top[:], ALU.subtract).then_inc(neg_done, 1)
                dve.wait_ge(hi_done, 1)
                nc.vector.tensor_tensor(rows[LO][:], s_ps[:, 0, 0:2 * P].rearrange("p (g c) -> p g c", g=2),
                                        rows[HI][:].bitcast(F32), ALU.subtract).then_inc(lo_done, 1)

            @block.tensor
            def _(pe):
                pe.wait_ge(ones_done, 3)
                with pe.Fori(0, NU // 2) as i:
                    for n in range(N):
                        s, qt = n // TILES, n % TILES
                        if qt == 0:
                            pe.wait_ge(loaded[s], i * 48 + 48)
                        pe.wait_ge(max_done, i * N + max(n, 1))
                        cols = (qt + 1) * P
                        for c0 in range(0, cols, 512):
                            w = min(512, cols - c0)
                            diag = c0 + w == cols
                            last = nc.tensor.matmul(s_ps[:, n % 2, c0:c0 + w], q[s][:, qt * P:(qt + 1) * P], kb[s][:, c0:c0 + w],
                                                    start=True, stop=not diag)
                        last = nc.tensor.matmul(s_ps[:, n % 2, cols - P:cols], k.ident_b[:], k.mask_k[:], start=False, stop=True)
                        last.then_inc(s_done, 1)
                pe.wait_ge(neg_done, 1)
                flat = neg[:].rearrange("p u t -> p (u t)")
                for g in range(2):
                    last = nc.tensor.transpose(s_ps[:, 0, g * P:(g + 1) * P], flat[:, g * P:(g + 1) * P], k.ident[:])
                last.then_inc(turned, 1)


def attention_a(k):
    nc, t = k.nc, k.t
    dv = DVA
    VW = 2 + 2 * dv
    LW = 2 + dv
    v_in = t["v_a_prompt"].rearrange("(t p) c -> p t c", p=P)
    o_out = k.o_a[0:SEQ].rearrange("(t p) c -> p t c", p=P)
    TURNS = HA
    unit = lambda ap: ap.rearrange("a (b d) s -> (a b) d s", b=2)
    q_hi, q_lo, k_hi, k_lo = (unit(x) for x in (k.q_hi, k.q_lo, k.k_hi, k.k_lo))
    nm_u = k.neg_max.rearrange("c (u t) p -> u c (t p)", t=TILES)
    NGR = TILES // GROUP
    steps = [(s, g, kt) for s in range(2) for g in range(NGR) for kt in range(4 * g + 4)]
    N, NS = len(steps), len(steps) // 2
    AHEAD = 3
    PR = 4
    AUG = DH + 2
    with ExitStack() as ctx:
        sb, ps, sem = tools(k, ctx, "att_a")
        q2 = [sb(f"q2_{s}", [P, SEQ], F32R) for s in range(2)]
        qm = [sb(f"qm_{s}", [AUG, SEQ], F32R) for s in range(2)]
        k2 = [sb(f"k2_{s}", [P, SEQ], F32R) for s in range(2)]
        km = [sb(f"km_{s}", [AUG, SEQ], F32R) for s in range(2)]
        ones = sb("ones", [P, SEQ // 2])
        zero = sb("zero", [P, TILES])
        bias = [sb(f"bias{s}", [P, TILES]) for s in range(2)]
        v_raw = [sb(f"v_raw{s}", [P, TILES, dv]) for s in range(2)]
        v = [sb(f"v{s}", [P, TILES, VW], F32R) for s in range(2)]
        pf = sb("pf", [P, PR, 512])
        parts = [sb("p_hi", [P, PR, 512], F32R), sb("p_lo", [P, PR, 512], F32R)]
        low = sb("low", [P, GROUP, dv])
        raw = sb("raw", [P, 2, GROUP, dv])
        recip = sb("recip", [P, 2, GROUP])
        o0 = sb("o0", [P, TILES, dv])
        o = sb("o", [P, 2, GROUP, dv])
        s_ps = ps("s_ps", [P, 4, 512])
        acc = ps("acc", [P, GROUP, 512])
        loaded = [sem("loaded0"), sem("loaded1")]
        ones_done, s_done, p_done, split_done, pv_done, v_done, dve_step, pool_step = (
            sem(n) for n in ("ones_done", "s_done", "p_done", "split_done", "pv_done", "v_done", "dve_step", "pool_step"))
        low_done, acc_read, o_done = sem("low_done"), sem("acc_read"), sem("o_done")
        stored = [sem("stored0"), sem("stored1")]
        LOADS = 9 * 16
        NG = 2 * NGR
        ends = [n for n in range(N) if n + 1 == N or steps[n + 1][1] != steps[n][1]]
        NQ = NG * GROUP

        def tile_of(m):
            s, g, kt = steps[m]
            return (s * NGR + g, kt - 4 * g) if kt >= 4 * g else None

        def due(n):
            e = n - 1 if n - 1 in ends else n if n == N - 1 else None
            return [] if e is None else range(e - GROUP + 1, e + 1)

        with nc.Block() as block:
            @block.sync
            def _(sp):
                def load(i, s):
                    u = i + s * HA
                    row = lambda ap: ap[ds(u, 1)].rearrange("u d s -> d u s")
                    to = lambda tile, a, b: tile[a:b, :].bitcast(F32).unsqueeze(1)
                    for dst, src in ((to(q2[s], 0, DH), row(q_hi)), (to(q2[s], DH, P), row(q_lo)),
                                     (to(qm[s], 0, DH), row(q_hi)), (to(qm[s], DH, AUG), row(nm_u)),
                                     (to(k2[s], 0, DH), row(k_hi)), (to(k2[s], DH, P), row(k_hi)),
                                     (to(km[s], 0, DH), row(k_lo)),
                                     (bias[s][:].unsqueeze(1), row(k.bias_col)),
                                     (v_raw[s][:], v_in[:, :, ds(i * dv, dv)])):
                        sp.dma_start(dst, src).then_inc(loaded[s], 16)
                def store(i):
                    for g in range(NGR):
                        sp.wait_ge(o_done, i * NGR + (g + 1))
                        sp.dma_start(o_out[:, g * GROUP:(g + 1) * GROUP, ds(i * dv, dv)], o[:, g % 2, :, :]).then_inc(stored[g % 2], 16)

                for s in range(2):
                    sp.sem_inc(stored[s], 16)
                    load(0, s)
                with sp.Fori(1, TURNS) as i:
                    for s in range(2):
                        if s == 1:
                            store(i - 1)
                        sp.wait_ge(pv_done, i * N + ((s + 1) * NS - N))
                        load(i, s)
                store(TURNS - 1)
                for s in range(2):
                    sp.wait_ge(stored[s], 16 * TURNS * NGR // 2 + 16)

            @block.gpsimd
            def _(pool):
                nc.gpsimd.memset(zero[:], 0.0)
                nc.gpsimd.memset(ones[:], 1.0).then_inc(ones_done, 1)
                pool.wait_ge(ones_done, 1)

                def split_v(i, s):
                    pool.wait_ge(loaded[s], i * LOADS + LOADS)
                    nc.gpsimd.tensor_tensor(v[s][:, :, 2:2 + dv], v_raw[s][:], zero[:].unsqueeze(2).to_broadcast([P, TILES, dv]),
                                            ALU.add).then_inc(pool_step, 1)
                    pool.wait_ge(pool_step, i * 2 + (s + 1))
                    nc.gpsimd.tensor_tensor(v[s][:, :, 2 + dv:VW], v_raw[s][:], v[s][:, :, 2:2 + dv].bitcast(F32),
                                            ALU.subtract).then_inc(v_done, 1)

                for s in range(2):
                    split_v(0, s)
                with pool.Fori(1, TURNS) as i:
                    for s in range(2):
                        split_v(i, s)

            @block.scalar
            def _(act):
                act.wait_ge(ones_done, 1)
                for s in range(2):
                    for c in range(2):
                        nc.scalar.activation(km[s][DH:AUG, c * (SEQ // 2):(c + 1) * (SEQ // 2)], ones[DH:AUG, :], ACT.Copy)
                    nc.scalar.activation(v[s][:, :, 0:2], ones[:, 0:2 * TILES].rearrange("p (t c) -> p t c", c=2), ACT.Copy).then_inc(ones_done, 1)
                with act.Fori(0, TURNS) as i:
                    def low_part(m):
                        if tile_of(m):
                            _, j = tile_of(m)
                            act.wait_ge(pv_done, i * N + (m + 1))
                            nc.scalar.activation(low[:, j, :], acc[:, j, 2 + dv:VW], ACT.Copy).then_inc(low_done, 1)

                    for n, (s, g, kt) in enumerate(steps):
                        if n % NS == 0:
                            act.wait_ge(loaded[s], i * LOADS + LOADS)
                        act.wait_ge(s_done, i * N + (n + 1))
                        if n >= PR:
                            act.wait_ge(split_done, i * N + (n - PR + 1))
                        w = 512 - P * max(0, kt - 4 * g)
                        col = 12 + kt - 4 * g
                        nc.scalar.activation(pf[:, n % PR, 0:w], s_ps[:, n % 4, 0:w], ACT.Exp,
                                             bias=bias[s][:, col:col + 1]).then_inc(p_done, 1)
                        for m in due(n):
                            low_part(m)

            @block.vector
            def _(dve):
                dve.sem_inc(acc_read, GROUP)
                with dve.Fori(0, TURNS) as i:
                    PER = N + NQ + NGR + NGR * 2
                    step = Tally(dve_step, i * PER)

                    def take(m):
                        if tile_of(m):
                            G, j = tile_of(m)
                            dve.wait_ge(pv_done, i * N + (m + 1))
                            dve.wait_ge(low_done, i * NQ + (G * GROUP + j + 1))
                            step.inc(nc.vector.reciprocal(recip[:, G % 2, j:j + 1], acc[:, j, 0:1]))
                            nc.vector.tensor_tensor(raw[:, G % 2, j, :], acc[:, j, 2:2 + dv], low[:, j, :], ALU.add).then_inc(acc_read, 1)

                    def finish(m):
                        s, g, kt = steps[m]
                        G = s * NGR + g
                        step.wait(dve)
                        if s == 1:
                            step.inc(nc.vector.tensor_scalar(recip[:, G % 2, :], recip[:, G % 2, :], k.neg_lam[:], None, ALU.mult))
                            step.wait(dve)
                        dve.wait_ge(acc_read, i * NQ + ((G + 2) * GROUP))
                        scale = recip[:, G % 2, :].unsqueeze(2).to_broadcast([P, GROUP, dv])
                        if s == 0:
                            step.inc(nc.vector.tensor_tensor(o0[:, g * GROUP:(g + 1) * GROUP, :], raw[:, G % 2, :, :], scale, ALU.mult))
                            return
                        dve.wait_ge(stored[g % 2], i * (8 * NGR) + 16 * (g // 2 + 1))
                        step.inc(nc.vector.tensor_tensor(raw[:, G % 2, :, :], raw[:, G % 2, :, :], scale, ALU.mult))
                        step.wait(dve)
                        nc.vector.tensor_tensor(o[:, g % 2, :, :], raw[:, G % 2, :, :], o0[:, g * GROUP:(g + 1) * GROUP, :],
                                                ALU.add).then_inc(o_done, 1)

                    for n, (s, g, kt) in enumerate(steps):
                        w = 512 - P * max(0, kt - 4 * g)
                        dve.wait_ge(p_done, i * N + (n + 1))
                        if n >= PR:
                            dve.wait_ge(pv_done, i * N + (n - PR + 1))
                        step.inc(nc.vector.tensor_copy(parts[HI][:, n % PR, 0:w], pf[:, n % PR, 0:w]))
                        step.wait(dve)
                        nc.vector.tensor_tensor(parts[LO][:, n % PR, 0:w], pf[:, n % PR, 0:w],
                                                parts[HI][:, n % PR, 0:w].bitcast(F32), ALU.subtract).then_inc(split_done, 1)
                        for m in due(n):
                            take(m)
                        if n - 3 in ends:
                            finish(n - 3)
                    finish(N - 1)
                    assert step.n == PER

            @block.tensor
            def _(pe):
                pe.wait_ge(ones_done, 3)
                with pe.Fori(0, TURNS) as i:
                    def scores(n):
                        s, g, kt = steps[n]
                        off = P * max(0, kt - 4 * g)
                        w = 512 - off
                        qs, ks = slice(g * 512 + off, (g + 1) * 512), slice(kt * P, (kt + 1) * P)
                        if n % NS == 0:
                            pe.wait_ge(loaded[s], i * LOADS + LOADS)
                        if n >= 4:
                            pe.wait_ge(p_done, i * N + (n - 3))
                        out = s_ps[:, n % 4, 0:w]
                        nc.tensor.matmul(out, k2[s][:, ks], q2[s][:, qs], start=True, stop=False)
                        last = nc.tensor.matmul(out, km[s][:, ks], qm[s][:, qs], start=False, stop=kt < 4 * g)
                        if kt >= 4 * g:
                            last = nc.tensor.matmul(s_ps[:, n % 4, 0:P], k.ident_b[:], k.mask_q[:], start=False, stop=True)
                        last.then_inc(s_done, 1)

                    for n in range(AHEAD):
                        scores(n)
                    for n, (s, g, kt) in enumerate(steps):
                        if n + AHEAD < N:
                            scores(n + AHEAD)
                        if n % NS == 0:
                            pe.wait_ge(v_done, i * 2 + (s + 1))
                        pe.wait_ge(split_done, i * N + (n + 1))
                        G = s * NGR + g
                        off = max(0, kt - 4 * g)
                        for j in range(off, GROUP):
                            stop = kt == 4 * g + j
                            if kt == 0:
                                pe.wait_ge(acc_read, i * NQ + (G * GROUP + j + 1))
                            lhs = slice((j - off) * P, (j - off + 1) * P)
                            nc.tensor.matmul(acc[:, j, 0:VW], parts[HI][:, n % PR, lhs], v[s][:, kt, :], start=kt == 0, stop=False)
                            last = nc.tensor.matmul(acc[:, j, 0:LW], parts[LO][:, n % PR, lhs], v[s][:, kt, 0:LW], start=False, stop=stop)
                        last.then_inc(pv_done, 1)



def attention_b(k):
    nc, t = k.nc, k.t
    dv = DH
    VW = P + dv
    v_in = t["v_b_prompt"].rearrange("(t p) c -> p t c", p=P)
    o_out = k.o_b[0:SEQ].rearrange("(t p) c -> p t c", p=P)
    TURNS = HB // 2
    unit = lambda ap: ap.rearrange("a (b d) s -> (a b) d s", b=2)
    q_hi, q_lo, k_hi, k_lo = (unit(x) for x in (k.q_hi, k.q_lo, k.k_hi, k.k_lo))
    nm_u = k.neg_max.rearrange("c (u t) p -> u c (t p)", t=TILES)
    NGR = TILES // GROUP
    steps = [(s, g, kt) for s in range(2) for g in range(NGR) for kt in range(4 * g + 4)]
    N, NS = len(steps), len(steps) // 2
    AHEAD = 3
    PR = 4
    AUG = DH + 2
    LATE = 2
    with ExitStack() as ctx:
        sb, ps, sem = tools(k, ctx, "att_b")
        q2 = [sb(f"q2_{s}", [P, SEQ], F32R) for s in range(2)]
        qm = [sb(f"qm_{s}", [AUG, SEQ], F32R) for s in range(2)]
        k2 = [sb(f"k2_{s}", [P, SEQ], F32R) for s in range(2)]
        km = [sb(f"km_{s}", [AUG, SEQ], F32R) for s in range(2)]
        ones = sb("ones", [P, SEQ // 2])
        zero = sb("zero", [P, TILES])
        bias = [sb(f"bias{s}", [P, TILES]) for s in range(2)]
        v_raw = [sb(f"v_raw{s}", [P, TILES, dv]) for s in range(2)]
        v = [sb(f"v{s}", [P, TILES, VW], F32R) for s in range(2)]
        pf = sb("pf", [P, PR, 512])
        parts = [sb("p_hi", [P, PR, 512], F32R), sb("p_lo", [P, PR, 512], F32R)]
        o_t = sb("o_t", [P, 2, 512])
        recip = sb("recip", [P, 2, GROUP])
        o = sb("o", [P, 2, GROUP, dv])
        s_ps = ps("s_ps", [P, 4, 512])
        acc = ps("acc", [P, 2, 512])
        turned = ps("turned", [P, 2, GROUP, P])
        loaded = [sem("loaded0"), sem("loaded1")]
        ones_done, s_done, p_done, split_done, pv_done, v_done, dve_step, pool_step = (
            sem(n) for n in ("ones_done", "s_done", "p_done", "split_done", "pv_done", "v_done", "dve_step", "pool_step"))
        acc_read, turned_done, o_done = sem("acc_read"), sem("turned_done"), sem("o_done")
        stored = [sem("stored0"), sem("stored1")]
        LOADS = 9 * 16
        NG = 2 * NGR
        ends = [n for n in range(N) if n + 1 == N or steps[n + 1][1] != steps[n][1]]
        group_of = lambda n: steps[n][0] * NGR + steps[n][1]

        with nc.Block() as block:
            @block.sync
            def _(sp):
                def load(i, s):
                    u = i * 2 + (2 * HA + s)
                    row = lambda ap: ap[ds(u, 1)].rearrange("u d s -> d u s")
                    to = lambda tile, a, b: tile[a:b, :].bitcast(F32).unsqueeze(1)
                    for dst, src in ((to(q2[s], 0, DH), row(q_hi)), (to(q2[s], DH, P), row(q_lo)),
                                     (to(qm[s], 0, DH), row(q_hi)), (to(qm[s], DH, AUG), row(nm_u)),
                                     (to(k2[s], 0, DH), row(k_hi)), (to(k2[s], DH, P), row(k_hi)),
                                     (to(km[s], 0, DH), row(k_lo)),
                                     (bias[s][:].unsqueeze(1), row(k.bias_col)),
                                     (v_raw[s][:], v_in[:, :, ds(i * 2 * DH + s * DH, dv)])):
                        sp.dma_start(dst, src).then_inc(loaded[s], 16)
                def store(i, s):
                    for g in range(NGR):
                        G = s * NGR + g
                        sp.wait_ge(o_done, i * NG + (G + 1))
                        sp.dma_start(o_out[:, g * GROUP:(g + 1) * GROUP, ds(i * 2 * DH + s * DH, dv)],
                                     o[:, G % 2, :, :]).then_inc(stored[G % 2], 16)

                for s in range(2):
                    sp.sem_inc(stored[s], 16)
                    load(0, s)
                with sp.Fori(1, TURNS) as i:
                    for s in range(2):
                        store(i - 1, s)
                        sp.wait_ge(pv_done, i * N + ((s + 1) * NS - N))
                        load(i, s)
                for s in range(2):
                    store(TURNS - 1, s)
                for s in range(2):
                    sp.wait_ge(stored[s], 16 * TURNS * NG // 2 + 16)

            @block.gpsimd
            def _(pool):
                nc.gpsimd.memset(zero[:], 0.0)
                nc.gpsimd.memset(ones[:], 1.0).then_inc(ones_done, 1)
                pool.wait_ge(ones_done, 1)

                def split_v(i, s):
                    pool.wait_ge(loaded[s], i * LOADS + LOADS)
                    nc.gpsimd.tensor_tensor(v[s][:, :, 0:dv], v_raw[s][:], zero[:].unsqueeze(2).to_broadcast([P, TILES, dv]),
                                            ALU.add).then_inc(pool_step, 1)
                    pool.wait_ge(pool_step, i * 2 + (s + 1))
                    nc.gpsimd.tensor_tensor(v[s][:, :, P:VW], v_raw[s][:], v[s][:, :, 0:dv].bitcast(F32),
                                            ALU.subtract).then_inc(v_done, 1)

                for s in range(2):
                    split_v(0, s)
                with pool.Fori(1, TURNS) as i:
                    for s in range(2):
                        split_v(i, s)

            @block.scalar
            def _(act):
                act.wait_ge(ones_done, 1)
                for s in range(2):
                    for c in range(2):
                        nc.scalar.activation(km[s][DH:AUG, c * (SEQ // 2):(c + 1) * (SEQ // 2)], ones[DH:AUG, :], ACT.Copy)
                    nc.scalar.activation(v[s][:, :, dv:P], ones[:, 0:TILES * DH].rearrange("p (t c) -> p t c", c=DH), ACT.Copy).then_inc(ones_done, 1)
                with act.Fori(0, TURNS) as i:
                    def take(m):
                        G = group_of(m)
                        act.wait_ge(pv_done, i * N + (m + 1))
                        act.wait_ge(turned_done, i * NG + (G + 1))
                        nc.scalar.activation(o_t[:, G % 2, :], acc[:, G % 2, :], ACT.Copy).then_inc(acc_read, 1)

                    for n, (s, g, kt) in enumerate(steps):
                        if n % NS == 0:
                            act.wait_ge(loaded[s], i * LOADS + LOADS)
                        act.wait_ge(s_done, i * N + (n + 1))
                        if n >= PR:
                            act.wait_ge(split_done, i * N + (n - PR + 1))
                        w = 512 - P * max(0, kt - 4 * g)
                        nc.scalar.activation(pf[:, n % PR, 0:w], s_ps[:, n % 4, 0:w], ACT.Exp,
                                             bias=bias[s][:, kt:kt + 1]).then_inc(p_done, 1)
                        if n - LATE in ends:
                            take(n - LATE)
                    take(N - 1)

            @block.vector
            def _(dve):
                with dve.Fori(0, TURNS) as i:
                    step = Tally(dve_step, i * (N + NG))

                    def finish(m):
                        G = group_of(m)
                        dve.wait_ge(turned_done, i * NG + (G + 3))
                        step.inc(nc.vector.reciprocal(recip[:, G % 2, :], turned[:, G % 2, :, dv]))
                        step.wait(dve)
                        dve.wait_ge(stored[G % 2], i * (8 * NG) + 16 * (G // 2 + 1))
                        nc.vector.tensor_tensor(o[:, G % 2, :, :], turned[:, G % 2, :, 0:dv],
                                                recip[:, G % 2, :].unsqueeze(2).to_broadcast([P, GROUP, dv]), ALU.mult).then_inc(o_done, 1)

                    for n, (s, g, kt) in enumerate(steps):
                        w = 512 - P * max(0, kt - 4 * g)
                        dve.wait_ge(p_done, i * N + (n + 1))
                        if n >= PR:
                            dve.wait_ge(pv_done, i * N + (n - PR + 1))
                        step.inc(nc.vector.tensor_copy(parts[HI][:, n % PR, 0:w], pf[:, n % PR, 0:w]))
                        step.wait(dve)
                        nc.vector.tensor_tensor(parts[LO][:, n % PR, 0:w], pf[:, n % PR, 0:w],
                                                parts[HI][:, n % PR, 0:w].bitcast(F32), ALU.subtract).then_inc(split_done, 1)
                        if n - LATE - 2 in ends:
                            finish(n - LATE - 2)
                    finish(N - 1)
                    assert step.n == N + NG

            @block.tensor
            def _(pe):
                pe.wait_ge(ones_done, 3)
                pe.sem_inc(turned_done, 2)
                with pe.Fori(0, TURNS) as i:
                    def scores(n):
                        s, g, kt = steps[n]
                        off = P * max(0, kt - 4 * g)
                        w = 512 - off
                        qs, ks = slice(g * 512 + off, (g + 1) * 512), slice(kt * P, (kt + 1) * P)
                        if n % NS == 0:
                            pe.wait_ge(loaded[s], i * LOADS + LOADS)
                        if n >= 4:
                            pe.wait_ge(p_done, i * N + (n - 3))
                        out = s_ps[:, n % 4, 0:w]
                        nc.tensor.matmul(out, k2[s][:, ks], q2[s][:, qs], start=True, stop=False)
                        last = nc.tensor.matmul(out, km[s][:, ks], qm[s][:, qs], start=False, stop=kt < 4 * g)
                        if kt >= 4 * g:
                            last = nc.tensor.matmul(s_ps[:, n % 4, 0:P], k.ident_b[:], k.mask_q[:], start=False, stop=True)
                        last.then_inc(s_done, 1)

                    def turn(m):
                        G = group_of(m)
                        pe.wait_ge(acc_read, i * NG + (G + 1))
                        if G >= 2:
                            pe.wait_ge(o_done, i * NG + (G - 1))
                        for j in range(GROUP):
                            last = nc.tensor.transpose(turned[:, G % 2, j, :], o_t[:, G % 2, j * P:(j + 1) * P], k.ident[:])
                        last.then_inc(turned_done, 1)

                    for n in range(AHEAD):
                        scores(n)
                    for n, (s, g, kt) in enumerate(steps):
                        if n + AHEAD < N:
                            scores(n + AHEAD)
                        if n - LATE - 1 in ends:
                            turn(n - LATE - 1)
                        if n % NS == 0:
                            pe.wait_ge(v_done, i * 2 + (s + 1))
                        pe.wait_ge(split_done, i * N + (n + 1))
                        G = group_of(n)
                        if kt == 0 and G >= 2:
                            pe.wait_ge(acc_read, i * NG + (G - 1))
                        off = P * max(0, kt - 4 * g)
                        w = 512 - off
                        out = acc[:, G % 2, off:512]
                        p_hi, p_lo = (parts[part][:, n % PR, 0:w] for part in (HI, LO))
                        nc.tensor.matmul(out, v[s][:, kt, 0:P], p_hi, start=kt == 0, stop=False, skip_group_check=True)
                        nc.tensor.matmul(out, v[s][:, kt, 0:P], p_lo, start=False, stop=False, skip_group_check=True)
                        last = nc.tensor.matmul(acc[0:dv, G % 2, off:512], v[s][:, kt, P:VW], p_hi, start=False, stop=False,
                                                skip_group_check=True)
                        last.then_inc(pv_done, 1)
                    turn(N - 1)


def sample(k):
    nc, t = k.nc, k.t
    ROWS = 4 * HB
    KEYS = PAST + SR
    caches = [t[n].rearrange(f"z n r {x} -> (z n) r ({x})") for n, x in (
        ("cache_a_k", "m h d"), ("cache_b_k", "h d"), ("cache_a_v", "h d"), ("cache_b_v", "h d"))]
    NPOOL = caches[0].shape[0]
    TURNS = NB // 2
    with ExitStack() as ctx:
        sb, ps, sem = tools(k, ctx, "smp")
        kv = [[sb(f"{n}{s}", [P, NPG, W]) for n in ("k_a", "k_b", "v_a", "v_b")] for s in range(2)]
        row_i, col_i, t_i = sb("row_i", [ROWS, 4], I32), sb("col_i", [ROWS, PAST], I32), sb("t_i", [ROWS, NB, NT], I32)
        row_q, map_i = sb("row_q", [ROWS, 1], I32), sb("map_i", [ROWS, 1], I32)
        row_qf, weight, slope = sb("row_qf", [ROWS, 1]), sb("weight", [ROWS, 1]), sb("slope", [ROWS, 1])
        past_bias = sb("past_bias", [ROWS, PAST])
        causal, causal_a = sb("causal", [ROWS, SR]), sb("causal_a", [ROWS, SR])
        new_bias = sb("new_bias", [ROWS, 2, NB, SR])
        own = sb("own", [ROWS, 2, W])
        match = sb("match", [ROWS, 2, SR])
        select = sb("select", [ROWS, 2, NB, SR])
        pick_f = sb("pick_f", [NB * HB, NB, ROWS])
        pick_h = sb("pick_h", [HB, ROWS])
        tri = sb("tri", [SR, SR])
        ones = sb("ones", [NB * HB, PAST])
        f_past = sb("f_past", [NB * HB, PAST])
        f_rel = sb("f_rel", [NB * HB, PAST])
        f_new = sb("f_new", [HB, SR])
        q_all = sb("q_all", [P, NB, 2, 4, ROWS])
        fence = sb("fence", [1, 2])
        q_blk = [sb(f"q_blk{s}", [P, 2, 4, ROWS]) for s in range(2)]
        sel_b = [sb(f"sel_b{s}", [ROWS, 2, SR]) for s in range(2)]
        pick_b = [sb(f"pick_b{s}", [NB * HB, ROWS]) for s in range(2)]
        kT = sb("kT", [P, 2, 4, PAST])
        sc = sb("sc", [ROWS, 2, KEYS])
        pr = sb("pr", [ROWS, 2, KEYS])
        neg_max, sums, recip = sb("neg_max", [ROWS, 2]), sb("sums", [ROWS, 2]), sb("recip", [ROWS, 2])
        pT = sb("pT", [P, 2, NPG, ROWS])
        pT_new = sb("pT_new", [SR, 2, ROWS])
        o_own = sb("o_own", [ROWS, 2, W])
        o_sum = sb("o_sum", [SR, 2, W])
        ps_t = ps("ps_t", [P, 2, 512])
        ps_s = ps("ps_s", [ROWS, 2, 512])
        ps_n = ps("ps_n", [ROWS, 512])
        ps_p = ps("ps_p", [P, 512])
        ps_f = ps_p[0:NB * HB, :]
        ps_o = ps("ps_o", [ROWS, 2, 512])
        stored = sem("stored")
        kv_in = [[sem(f"kv_in{s}_{n}") for n in range(4)] for s in range(2)]
        names = ("pool_step", "filled", "made", "small", "consts", "dve_step", "lf_turned", "f_scanned", "f_ready",
                 "fn_ready", "fn_copied", "prepared", "turned", "kt_act", "kt_dve", "s_done", "past_b", "max_done",
                 "p_done", "pt_ready", "pt_copied", "pv_done", "own_done", "dve_recip", "picked", "added")
        S = {n: sem(n) for n in names}
        with nc.Block() as block:
            @block.sync
            def _(sp):
                def page(b, g):
                    return sp.value_load(k.pages[0:1, ds(b * NPG + g, 1)], min_val=0, max_val=NPOOL - 1)

                def load(b, s, what):
                    at = [page(b, g) for g in range(NPG)]
                    for n in (2 * what, 2 * what + 1):
                        for g in range(NPG):
                            sp.dma_start(kv[s][n][:, g:g + 1, :], caches[n][ds(at[g], 1)].rearrange("n r c -> r n c")).then_inc(kv_in[s][n], 16)

                def next_k(b, s):
                    sp.wait_ge(S["made"], 1)
                    sp.wait_ge(S["turned"], b * 8 - 8)
                    load(b, s, 0)

                def next_v(b, s):
                    sp.wait_ge(S["made"], 1)
                    sp.wait_ge(S["pv_done"], b - 1)
                    load(b, s, 1)

                for what in range(2):
                    load(0, 0, what)
                    load(1, 1, what)
                next_k(2, 0)
                with sp.Fori(1, TURNS - 1) as i:
                    next_k(i * 2 + 1, 1)
                    next_v(i * 2, 0)
                    next_k(i * 2 + 2, 0)
                    next_v(i * 2 + 1, 1)
                next_k(NB - 1, 1)
                next_v(NB - 2, 0)
                next_v(NB - 1, 1)
                sp.wait_ge(S["added"], NB + 1)
                sp.dma_start(k.o_a[SEQ:SEQ + SR], o_sum[:, 0, :]).then_inc(stored, 16)
                sp.dma_start(k.o_b[SEQ:SEQ + SR], o_sum[:, 1, :]).then_inc(stored, 16)
                sp.wait_ge(stored, 32)

            @block.gpsimd
            def _(pool):
                g = nc.gpsimd
                g.iota(row_i[:], pattern=[[0, 4]], base=0, channel_multiplier=1)
                g.iota(col_i[:], pattern=[[1, PAST]], base=-PAST, channel_multiplier=0)
                g.iota(t_i[:], pattern=[[0, NB], [1, NT]], base=0, channel_multiplier=0)
                g.memset(slope[:], SLOPES[HA - 1])
                g.memset(own[:], 1.0)
                g.memset(pick_f[:], -1.0)
                g.memset(pick_h[:], -1.0)
                g.memset(tri[:], 1.0)
                g.memset(ones[:], 1.0)
                g.memset(q_all[:], 0.0).then_inc(S["filled"], 1)
                pool.wait_ge(S["filled"], 1)
                step = Tally(S["pool_step"])

                def select_(ap, pattern, cm, base, fill, op=ALU.is_ge):
                    step.inc(g.affine_select(out=ap, in_=ap, compare_op=op, fill=fill, base=base, pattern=pattern, channel_multiplier=cm))
                    step.wait(pool)
                for h in range(HA - 2, -1, -1):
                    select_(slope[:], [[0, 1]], 1, -8 * (h + 1), SLOPES[h])
                for b, (n, w, r) in enumerate(((HA, DVA, 2 * NT), (HB, DH, NT))):
                    select_(own[:, b, :], [[-r, n], [0, w]], 1, 0, 0.0)
                    select_(own[:, b, :], [[r, n], [0, w]], -1, r - 1, 0.0)
                select_(pick_f[:], [[-HB, NB], [-1, HB], [0, NT]], 1, 0, 0.0, ALU.is_equal)
                select_(pick_h[:], [[-1, HB], [0, NT]], 1, 0, 0.0, ALU.is_equal)
                select_(tri[:], [[NT, NB], [1, NT]], -1, 0, 0.0)
                select_(tri[:], [[-NT, NB], [0, NT]], 1, 0, 0.0)
                g.memset(fence[:], 0.0).then_inc(S["made"], 1)
                pool.wait_ge(S["small"], 1)
                for b in range(2):
                    select_(new_bias[:, b, :, :], [[-1, NB], [1, NB], [0, NT]], 0, 0, NEG, ALU.is_equal)
                    select_(select[:, b, :, :], [[-1, NB], [1, NB], [0, NT]], 0, 0, 0.0, ALU.is_equal)
                g.memset(fence[:], 0.0).then_inc(S["consts"], 1)

            def iterate(eng, body):
                body(0, 0, True, False)
                body(0, 1, False, False)
                with eng.Fori(1, TURNS - 1) as i:
                    for s in range(2):
                        body(i, s, False, False)
                body(TURNS - 1, 0, False, False)
                body(TURNS - 1, 1, False, True)

            @block.vector
            def _(dve):
                v = nc.vector
                step = Tally(S["dve_step"])

                def go(ins):
                    step.inc(ins)
                    step.wait(dve)
                dve.wait_ge(S["made"], 1)
                go(v.tensor_scalar(row_q[:], row_i[:, 0:1], 3, None, ALU.bitwise_and))
                go(v.tensor_scalar(map_i[:], row_i[:, 0:1], 4, None, ALU.bitwise_and))
                go(v.tensor_copy(row_qf[:], row_q[:]))
                go(v.tensor_scalar(weight[:], map_i[:], 0.25, None, ALU.mult))
                go(v.tensor_scalar(sums[:, 0:1], k.neg_lam[0:ROWS, :], -1.0, None, ALU.add))
                go(v.tensor_tensor(weight[:], weight[:], sums[:, 0:1], ALU.mult))
                go(v.tensor_scalar(weight[:], weight[:], 1.0, None, ALU.add))
                go(v.tensor_scalar(past_bias[:], col_i[:], slope[:], None, ALU.mult))
                tf = t_i[:].rearrange("p b t -> p (b t)")
                go(v.tensor_scalar(causal[:], tf, row_qf[:], NEG, ALU.is_gt, ALU.mult))
                go(v.tensor_scalar(causal_a[:], tf, slope[:], None, ALU.mult))
                go(v.tensor_tensor(causal_a[:], causal_a[:], causal[:], ALU.add))
                go(v.tensor_scalar(match[:, 1, :], tf, row_qf[:], None, ALU.is_equal))
                go(v.tensor_scalar(match[:, 0, :], match[:, 1, :], weight[:], None, ALU.mult))
                over = lambda ap: ap.unsqueeze(1).to_broadcast([ROWS, NB, SR])
                v.tensor_copy(new_bias[:, 0, :, :], over(causal_a[:]))
                v.tensor_copy(new_bias[:, 1, :, :], over(causal[:]))
                v.tensor_copy(select[:, 0, :, :], over(match[:, 0, :]))
                v.tensor_copy(select[:, 1, :, :], over(match[:, 1, :])).then_inc(S["small"], 1)
                for b in range(2):
                    for u in range(8):
                        p, half = u // 2, u % 2
                        c = 8 * (u % HA) + 4 * (u // HA) if b == 0 else 4 * u
                        r = slice(half * DH, (half + 1) * DH)
                        last = v.tensor_copy(q_all[r, :, b, p, c:c + NT], k.qT_s[r, b, p, :].rearrange("p (b t) -> p b t", t=NT))
                step.inc(last)

                def k_turned(b):
                    for n in range(0, 8, 2):
                        dve.wait_ge(S["turned"], b * 8 + (n + 1))
                        v.tensor_copy(kT[:, n // 4, n % 4, :], ps_t[:, 0, :]).then_inc(S["kt_dve"], 1)

                k_turned(0)
                dve.wait_ge(S["lf_turned"], 1)
                go(v.tensor_tensor_scan(f_past[:], ones[:], ps_f, 0.0, ALU.mult, ALU.add))
                v.tensor_scalar(f_rel[:], f_past[:], f_past[:, PAST - 1:PAST], None, ALU.subtract).then_inc(S["f_ready"], 1)
                dve.wait_ge(S["fn_ready"], 1)
                v.tensor_copy(f_new[:], ps_n[0:HB, 0:SR]).then_inc(S["fn_copied"], 1)
                go(v.memset(o_sum[:], 0.0))
                dve.wait_ge(S["consts"], 1)

                def prepare(b, s):
                    v.tensor_copy(q_blk[s][:].unsqueeze(1), q_all[:, ds(b, 1)])
                    v.tensor_copy(sel_b[s][:].unsqueeze(2), select[:, :, ds(b, 1), :])
                    v.tensor_copy(pick_b[s][:].unsqueeze(1), pick_f[:, ds(b, 1), :]).then_inc(S["prepared"], 1)

                dve.sem_inc(S["added"], 1)
                prepare(0, 0)
                prepare(1, 1)

                def biased(b):
                    dve.wait_ge(S["s_done"], b + 1)
                    v.tensor_tensor(sc[:, 0, 0:PAST], ps_s[:, 0, :], past_bias[:], ALU.add)
                    v.tensor_tensor(sc[:, :, PAST:KEYS].unsqueeze(2), ps_n[:, 0:2 * SR].rearrange("p (c k) -> p c k", c=2).unsqueeze(2),
                                    new_bias[:, :, ds(b, 1), :], ALU.add).then_inc(S["max_done"], 1)
                    dve.wait_ge(S["past_b"], b + 1)
                    dve.wait_ge(S["max_done"], b * 2 + 1)
                    v.tensor_reduce(neg_max[:], sc[:], AX.X, ALU.max, negate=True).then_inc(S["max_done"], 1)

                def own_columns(b):
                    dve.wait_ge(S["pv_done"], b + 1)
                    dve.wait_ge(S["dve_recip"], b + 1)
                    for c in range(2):
                        last = v.scalar_tensor_tensor(o_own[:, c, :], ps_o[:, c, :], recip[:, c:c + 1], own[:, c, :], ALU.mult, ALU.mult)
                    last.then_inc(S["own_done"], 1)

                def add(b):
                    dve.wait_ge(S["picked"], b + 1)
                    v.tensor_tensor(o_sum[:], ps_o[0:SR, :, :], o_sum[:], ALU.add).then_inc(S["added"], 1)
                    dve.wait_ge(S["added"], b + 2)

                biased(0)

                def body(i, s, first, last):
                    b = i * 2 + s
                    if not first:
                        own_columns(b - 1)
                    if not last:
                        k_turned(b + 1)
                    if not first:
                        add(b - 1)
                        if not last:
                            prepare(b + 1, 1 - s)
                    dve.wait_ge(S["p_done"], b * 2 + 2)
                    v.reciprocal(recip[:], sums[:]).then_inc(S["dve_recip"], 1)
                    dve.wait_ge(S["pt_ready"], b + 1)
                    v.tensor_copy(pT[:], ps_p[:, 0:2 * NPG * ROWS].rearrange("p (c g r) -> p c g r", c=2, g=NPG))
                    v.tensor_copy(pT_new[:], ps_p[0:SR, 2 * NPG * ROWS:2 * (NPG + 1) * ROWS].rearrange("p (c r) -> p c r", c=2)).then_inc(S["pt_copied"], 1)
                    if not last:
                        biased(b + 1)

                iterate(dve, body)
                own_columns(NB - 1)
                add(NB - 1)

            @block.scalar
            def _(act):
                a = nc.scalar

                def k_turned(b):
                    for n in range(1, 8, 2):
                        act.wait_ge(S["turned"], b * 8 + (n + 1))
                        a.activation(kT[:, n // 4, n % 4, :], ps_t[:, 1, :], ACT.Copy).then_inc(S["kt_act"], 1)

                def probabilities(b, first=False):
                    act.wait_ge(S["s_done"], b + 1)
                    a.activation(sc[:, 1, 0:PAST], ps_s[:, 1, :], ACT.Copy).then_inc(S["past_b"], 1)
                    if not first:
                        act.wait_ge(S["pt_ready"], b)
                        act.wait_ge(S["dve_recip"], b)
                    act.wait_ge(S["max_done"], b * 2 + 2)
                    for c in range(2):
                        a.activation(pr[:, c, :], sc[:, c, :], ACT.Exp, bias=neg_max[:, c:c + 1],
                                     accum_out=sums[:, c:c + 1]).then_inc(S["p_done"], 1)

                def body(i, s, first, last):
                    b = i * 2 + s
                    if not last:
                        k_turned(b + 1)
                        probabilities(b + 1)

                k_turned(0)
                probabilities(0, first=True)
                iterate(act, body)

            @block.tensor
            def _(pe):
                mm, tr = nc.tensor.matmul, nc.tensor.transpose

                def turn_k(i, s, first=0, end=8):
                    b = i * 2 + s
                    for n in range(first, end):
                        c, p = n // 4, n % 4
                        if p == 0:
                            pe.wait_ge(kv_in[s][c], i * (16 * NPG) + 16 * NPG)
                        if n >= 2:
                            pe.wait_ge((S["kt_dve"], S["kt_act"])[n % 2], b * 4 + n // 2)
                        for g in range(NPG):
                            last = tr(ps_t[:, n % 2, g * PG:(g + 1) * PG], kv[s][c][:, g, p * P:(p + 1) * P], k.ident[:])
                        last.then_inc(S["turned"], 1)

                def scores(i, s):
                    b = i * 2 + s
                    pe.wait_ge(S["prepared"], b + 1)
                    pe.wait_ge(S["kt_dve"], b * 4 + 4)
                    pe.wait_ge(S["kt_act"], b * 4 + 4)
                    for c in range(2):
                        for p in range(4):
                            mm(ps_s[:, c, :], q_blk[s][:, c, p, :], kT[:, c, p, :], start=p == 0, stop=p == 3 and c == 0)
                    mm(ps_s[:, 1, :], pick_b[s][:], f_rel[:], start=False, stop=True)
                    for c in range(2):
                        for p in range(4):
                            mm(ps_n[:, c * SR:(c + 1) * SR], q_blk[s][:, c, p, :], k.kT_s[:, c, p, :], start=p == 0, stop=p == 3 and c == 0)
                    mm(ps_n[:, SR:2 * SR], pick_h[:], f_new[:], start=False, stop=True).then_inc(S["s_done"], 1)

                turn_k(0, 0)
                for g in range(NPG):
                    last = tr(ps_f[:, g * PG:(g + 1) * PG], k.lf[:, g, :, :].rearrange("p b h -> p (b h)"), k.ident[:])
                last.then_inc(S["lf_turned"], 1)
                pe.wait_ge(S["made"], 1)
                mm(ps_n[0:HB, 0:SR], k.logf[0:SR, TILES, :], tri[:], start=True, stop=True).then_inc(S["fn_ready"], 1)
                pe.wait_ge(S["fn_copied"], 1)
                pe.wait_ge(S["f_ready"], 1)
                scores(0, 0)

                def pick(s):
                    for c in range(2):
                        last = mm(ps_o[:, c, :], sel_b[s][:, c, :], o_own[:, c, :], start=True, stop=True)
                    last.then_inc(S["picked"], 1)

                def body(i, s, first, last):
                    b = i * 2 + s
                    following = (i, 1) if s == 0 else (i + 1, 0)
                    if not last:
                        turn_k(*following, 0, 6)
                    if not first:
                        pe.wait_ge(S["own_done"], b)
                    pe.wait_ge(S["p_done"], b * 2 + 2)
                    if not last:
                        turn_k(*following, 6, 8)
                    if not first:
                        pick(1 - s)
                    for c in range(2):
                        for g in range(NPG):
                            n = c * NPG + g
                            tr(ps_p[:, n * ROWS:(n + 1) * ROWS], pr[:, c, g * PG:(g + 1) * PG], k.ident[0:ROWS, 0:ROWS])
                    for c in range(2):
                        n = 2 * NPG + c
                        done = tr(ps_p[0:SR, n * ROWS:(n + 1) * ROWS], pr[:, c, PAST:KEYS], k.ident[0:ROWS, 0:ROWS])
                    done.then_inc(S["pt_ready"], 1)
                    if not last:
                        pe.wait_ge(S["max_done"], b * 2 + 2)
                        scores(*following)
                    pe.wait_ge(S["pt_copied"], b + 1)
                    pe.wait_ge(S["added"], b + 1)
                    for c in range(2):
                        pe.wait_ge(kv_in[s][2 + c], i * (16 * NPG) + 16 * NPG)
                        for g in range(NPG):
                            mm(ps_o[:, c, :], pT[:, c, g, :], kv[s][2 + c][:, g, :], start=g == 0, stop=False)
                        done = mm(ps_o[:, c, :], pT_new[:, c, :], k.v_s[:, c, :], start=False, stop=True)
                    done.then_inc(S["pv_done"], 1)

                iterate(pe, body)
                pe.wait_ge(S["own_done"], NB)
                pick(1)


def merge(k):
    nc, t = k.nc, k.t
    KW = W // P
    KT = 2 * KW + KD
    weights = [t["w_out_a"][0]] * KW + [t["w_out_b"][0]] * KW + [t["w_o"][0]] * KD
    w_row = [kt % KW if kt < 2 * KW else kt - 2 * KW for kt in range(KT)]
    x_in = {P: t["x_prompt"][0], SR: t["x_sample"].rearrange("b t d -> (b t) d")}
    with ExitStack() as ctx:
        sb, ps, sem = tools(k, ctx, "mrg")
        w_raw = sb("w_raw", [P, 2, D])
        w = [sb("w_hi", [P, KT, D], F32R), sb("w_lo", [P, KT, D], F32R)]
        gain = sb("gain", [P, DVA])
        res = sb("res", [P, D])
        ob = sb("ob", [P, 2 * W])
        gates = sb("gates", [P, 2 * W])
        mix = sb("mix", [P, 2 * D])
        x = sb("x", [P, D])
        ms, rstd = sb("ms", [P, HA]), sb("rstd", [P, HA])
        u = sb("u", [P, 2 * W])
        uT = [sb("uT_hi", [P, 2 * KW, P], F32R), sb("uT_lo", [P, 2 * KW, P], F32R)]
        y, y2 = sb("y", [P, D]), sb("y2", [P, D])
        yT = [sb("yT_hi", [P, KD, P], F32R), sb("yT_lo", [P, KD, P], F32R)]
        out = sb("out", [P, D])
        ps_y = ps("ps_y", [P, 4, 512])
        ps_o = ps("ps_o", [P, 2, 512])
        ps_t = ps("ps_t", [P, 2, 512])
        names = ("gain_in", "gain_done", "res_in", "w_split", "w_hi_done", "o_in", "g_in", "m_in", "x_in", "sq_done", "mean_done",
                 "rstd_done", "u_step", "u_done", "u_turned", "uT_hi_done", "uT_done", "y_ready", "y_step", "y_done",
                 "y_turned", "yT_hi_done", "yT_done", "o_ready", "scaled", "out_done", "stored")
        S = {n: sem(n) for n in names}
        w_slots = [w_raw[:, 0, :], w_raw[:, 1, :], x[:], out[:]]
        NW = len(w_slots)
        w_in = [sem(f"w_in{i}") for i in range(NW)]

        def where(tile, pn, ap):
            return ap[ds(tile * P, P)] if pn == P else ap[SEQ:SEQ + SR]

        with nc.Block() as block:
            @block.sync
            def _(sp):
                def load_o(tile, pn):
                    for n, src in enumerate((k.o_a, k.o_b)):
                        sp.dma_start(ob[0:pn, n * W:(n + 1) * W], where(tile, pn, src)).then_inc(S["o_in"], 16)
                    sp.dma_start(gates[0:pn, :], where(tile, pn, k.gates)).then_inc(S["g_in"], 16)

                def load_m(tile, pn):
                    sp.dma_start(mix[0:pn, :], where(tile, pn, k.mixes)).then_inc(S["m_in"], 16)

                def load_x(tile, pn):
                    src = x_in[P][ds(tile * P, P)] if pn == P else x_in[SR]
                    sp.dma_start(x[0:pn, :], src).then_inc(S["x_in"], 16)

                def store(tile, pn):
                    sp.wait_ge(S["out_done"], tile + 1)
                    dst = t["y_prompt"][ds(tile * P, P)] if pn == P else t["y_sample"]
                    sp.dma_start(dst, out[0:pn, :]).then_inc(S["stored"], 16)

                sp.sem_inc(S["stored"], 16)
                sp.dma_start(gain[:], t["g_sub_a"].to_broadcast([P, DVA])).then_inc(S["gain_in"], 16)
                load_o(0, P)
                for kt in range(KT):
                    if kt >= NW:
                        sp.wait_ge(S["w_split"], kt - NW + 1)
                    r = w_row[kt] * P
                    sp.dma_start(w_slots[kt % NW], weights[kt][r:r + P, :]).then_inc(w_in[kt % NW], 16)
                    if kt == 2 * KW - 1:
                        load_m(0, P)
                        sp.wait_ge(S["u_done"], 1)
                        load_o(1, P)
                sp.wait_ge(S["w_split"], KT)
                load_x(0, P)
                sp.dma_start(res[:], k.ada_gate[SR:SR + 1, :].to_broadcast([P, D])).then_inc(S["res_in"], 16)

                def turn(n, pn_next, first=False):
                    if not first:
                        sp.wait_ge(S["u_done"], n + 1)
                        load_o(n + 1, pn_next)
                    sp.wait_ge(S["y_done"], n + 1)
                    load_m(n + 1, pn_next)
                    if not first:
                        sp.wait_ge(S["out_done"], n)
                        load_x(n, P)
                        store(n - 1, P)
                turn(0, P, first=True)
                with sp.Fori(1, TILES - 1) as n:
                    turn(n, P)
                turn(TILES - 1, SR)
                sp.wait_ge(S["out_done"], TILES)
                load_x(TILES, SR)
                store(TILES - 1, P)
                sp.wait_ge(S["scaled"], TILES + 1)
                sp.dma_start(res[0:SR, :], k.ada_gate[0:SR, :]).then_inc(S["res_in"], 16)
                store(TILES, SR)
                sp.wait_ge(S["stored"], 16 * (TILES + 2))

            @block.gpsimd
            def _(pool):
                def gate(n, pn):
                    pool.wait_ge(S["mean_done"], n + 1)
                    nc.gpsimd.tensor_tensor(rstd[0:pn, :], ms[0:pn, :], k.neg_half[0:pn, 0:HA], ALU.pow).then_inc(S["rstd_done"], 1)
                with pool.Fori(0, TILES) as n:
                    gate(n, P)
                gate(TILES, SR)

            @block.scalar
            def _(act):
                a = nc.scalar

                def square(n, pn, first=False):
                    act.wait_ge(S["o_in"], n * 32 + 32)
                    if not first:
                        act.wait_ge(S["u_turned"], n)
                    a.activation(u[0:pn, 0:W], ob[0:pn, 0:W], ACT.Square).then_inc(S["sq_done"], 1)

                def turn(n, pn, nxt):
                    if nxt:
                        square(n + 1, nxt)
                        act.wait_ge(S["u_turned"], n + 2)
                        act.wait_ge(S["y_ready"], n + 1)
                        evacuate(n + 1, nxt, uT[HI], S["uT_hi_done"])
                    act.wait_ge(S["y_turned"], n + 1)
                    act.wait_ge(S["o_ready"], n + 1)
                    evacuate(n, pn, yT[HI], S["yT_hi_done"])

                def evacuate(n, pn, hi, done):
                    for c in range(2):
                        last = a.activation(hi[:, 4 * c:4 * c + 4, 0:pn], ps_t[:, c, :].rearrange("p (a r) -> p a r", a=4)[:, :, 0:pn], ACT.Copy)
                    last.then_inc(done, 1)

                square(0, P, first=True)
                act.wait_ge(S["u_turned"], 1)
                evacuate(0, P, uT[HI], S["uT_hi_done"])

                def w_high(kts):
                    for kt in kts:
                        act.wait_ge(w_in[kt % NW], 16 * (kt // NW + 1))
                        a.activation(w[HI][:, kt, :], w_slots[kt % NW], ACT.Copy).then_inc(S["w_hi_done"], 1)

                w_high(range(2 * KW))
                square(1, P)
                w_high(range(2 * KW, KT - 4))
                act.wait_ge(S["u_turned"], 2)
                act.wait_ge(S["y_ready"], 1)
                evacuate(1, P, uT[HI], S["uT_hi_done"])
                w_high(range(KT - 4, KT))
                act.wait_ge(S["y_turned"], 1)
                evacuate(0, P, yT[HI], S["yT_hi_done"])
                with act.Fori(1, TILES - 1) as n:
                    turn(n, P, P)
                turn(TILES - 1, P, SR)
                turn(TILES, SR, 0)

            @block.vector
            def _(dve):
                v = nc.vector
                halves = lambda ap: ap.rearrange("p a b -> p (a b)")

                def gated(n, pn):
                    step = Tally(S["u_step"], n * 2)
                    heads = lambda ap: ap.rearrange("p (h d) -> p h d", h=HA)
                    dve.wait_ge(S["sq_done"], n + 1)
                    step.inc(v.reduce_sum(ms[0:pn, :], heads(u[0:pn, 0:W]), AX.X))
                    step.wait(dve)
                    v.tensor_scalar(ms[0:pn, :], ms[0:pn, :], 1.0 / DVA, EPS, ALU.mult, ALU.add).then_inc(S["mean_done"], 1)
                    dve.wait_ge(S["g_in"], n * 16 + 16)
                    step.inc(v.tensor_tensor(heads(gates[0:pn, 0:W]), heads(gates[0:pn, 0:W]),
                                             gain[0:pn, :].unsqueeze(1).to_broadcast([pn, HA, DVA]), ALU.mult))
                    v.tensor_tensor(u[0:pn, W:2 * W], ob[0:pn, W:2 * W], gates[0:pn, W:2 * W], ALU.mult)
                    step.wait(dve)
                    dve.wait_ge(S["rstd_done"], n + 1)
                    for h in range(HA):
                        c = slice(h * DVA, (h + 1) * DVA)
                        last = v.scalar_tensor_tensor(u[0:pn, c], ob[0:pn, c], rstd[0:pn, h:h + 1], gates[0:pn, c], ALU.mult, ALU.mult)
                    last.then_inc(S["u_done"], 1)

                def low(n, pn, hi_done, parts, done):
                    dve.wait_ge(hi_done, n + 1)
                    for c in range(2):
                        last = v.tensor_tensor(parts[LO][:, 4 * c:4 * c + 4, 0:pn], ps_t[:, c, :].rearrange("p (a r) -> p a r", a=4)[:, :, 0:pn],
                                               parts[HI][:, 4 * c:4 * c + 4, 0:pn].bitcast(F32), ALU.subtract)
                    last.then_inc(done, 1)

                def combine(n, pn, first):
                    dve.wait_ge(S["m_in"], n * 16 + 16)
                    dve.wait_ge(S["y_ready"], n + 1)
                    if not first:
                        dve.wait_ge(S["y_turned"], n)
                    v.tensor_tensor(y[0:pn, :], halves(ps_y[0:pn, 0:2, :]), mix[0:pn, 0:D], ALU.mult)
                    v.tensor_tensor(y2[0:pn, :], halves(ps_y[0:pn, 2:4, :]), mix[0:pn, D:2 * D], ALU.mult).then_inc(S["y_step"], 1)
                    dve.wait_ge(S["y_step"], n + 1)
                    v.tensor_tensor(y[0:pn, :], y[0:pn, :], y2[0:pn, :], ALU.add).then_inc(S["y_done"], 1)

                def finish(n, pn):
                    dve.wait_ge(S["o_ready"], n + 2)
                    dve.wait_ge(S["res_in"], 16 if pn == P else 32)
                    dve.wait_ge(S["x_in"], n * 16 + 16)
                    dve.wait_ge(S["stored"], n * 16 + 16)
                    v.tensor_tensor(out[0:pn, :], halves(ps_o[0:pn, :, :]), res[0:pn, :], ALU.mult).then_inc(S["scaled"], 1)
                    dve.wait_ge(S["scaled"], n + 2)
                    v.tensor_tensor(out[0:pn, :], out[0:pn, :], x[0:pn, :], ALU.add).then_inc(S["out_done"], 1)

                def turn(n, pn, nxt, first=False):
                    if nxt:
                        gated(n + 1, nxt)
                    combine(n, pn, first)
                    if nxt:
                        low(n + 1, nxt, S["uT_hi_done"], uT, S["uT_done"])
                    if not first:
                        finish(n - 1, P)
                    low(n, pn, S["yT_hi_done"], yT, S["yT_done"])

                dve.sem_inc(S["scaled"], 1)
                dve.wait_ge(S["gain_in"], 16)
                v.tensor_scalar(gain[:], gain[:], 1.0 - LAM_INIT, None, ALU.mult).then_inc(S["gain_done"], 1)
                dve.wait_ge(S["gain_done"], 1)
                gated(0, P)
                low(0, P, S["uT_hi_done"], uT, S["uT_done"])

                def w_low(kts):
                    for kt in kts:
                        dve.wait_ge(S["w_hi_done"], kt + 1)
                        v.tensor_tensor(w[LO][:, kt, :], w_slots[kt % NW], w[HI][:, kt, :].bitcast(F32), ALU.subtract).then_inc(S["w_split"], 1)

                w_low(range(2 * KW))
                gated(1, P)
                w_low(range(2 * KW, KT - 4))
                combine(0, P, True)
                low(1, P, S["uT_hi_done"], uT, S["uT_done"])
                w_low(range(KT - 4, KT))
                low(0, P, S["yT_hi_done"], yT, S["yT_done"])
                with dve.Fori(1, TILES - 1) as n:
                    turn(n, P, P)
                turn(TILES - 1, P, SR)
                turn(TILES, SR, 0)
                finish(TILES, SR)

            @block.tensor
            def _(pe):
                def turn_u(n, pn):
                    pe.wait_ge(S["u_done"], n + 1)
                    transpose(u, pn).then_inc(S["u_turned"], 1)

                def transpose(src, pn):
                    for c in range(8):
                        at = (c % 4) * P
                        last = nc.tensor.transpose(ps_t[:, c // 4, at:at + pn], src[0:pn, c * P:(c + 1) * P], k.ident[0:pn, 0:pn])
                    return last

                def products(n, pn, first=False):
                    pe.wait_ge(S["uT_done"], n + 1)
                    if not first:
                        pe.wait_ge(S["y_done"], n)
                    for b in range(2):
                        if first:
                            pe.wait_ge(S["w_split"], (b + 1) * KW)
                        for h in range(2):
                            last = split_product(nc, ps_y[0:pn, 2 * b + h, :], lambda part, kt: uT[part][:, kt, 0:pn],
                                                 lambda part, kt: w[part][:, kt, h * 512:(h + 1) * 512],
                                                 three_terms(range(b * KW, (b + 1) * KW)))
                    last.then_inc(S["y_ready"], 1)

                def project_out(n, pn):
                    pe.wait_ge(S["yT_done"], n + 1)
                    pe.wait_ge(S["scaled"], n + 1)
                    for h in range(2):
                        last = split_product(nc, ps_o[0:pn, h, :], lambda part, kt: yT[part][:, kt, 0:pn],
                                             lambda part, kt: w[part][:, 2 * KW + kt, h * 512:(h + 1) * 512],
                                             three_terms(range(KD)))
                    last.then_inc(S["o_ready"], 1)

                def turn(n, pn, nxt, first=False):
                    products(n, pn, first)
                    if nxt:
                        if not first:
                            pe.wait_ge(S["yT_done"], n)
                        turn_u(n + 1, nxt)
                    if not first:
                        project_out(n - 1, P)
                    if nxt:
                        pe.wait_ge(S["uT_done"], n + 2)
                    pe.wait_ge(S["y_done"], n + 1)
                    transpose(y, pn).then_inc(S["y_turned"], 1)

                pe.sem_inc(S["o_ready"], 1)
                turn_u(0, P)
                turn(0, P, P, first=True)
                pe.wait_ge(S["w_split"], KT)
                with pe.Fori(1, TILES - 1) as n:
                    turn(n, P, P)
                turn(TILES - 1, P, SR)
                turn(TILES, SR, 0)
                project_out(TILES, SR)


INPUTS = ["x_prompt", "x_sample", "cache_a_k", "cache_a_v", "cache_b_k", "cache_b_v", "cache_b_logf", "page_table",
          "c_prompt", "c_sample", "w_ada", "b_ada", "w_in", "b_f", "g_q_a", "g_k_a", "g_q_b", "g_k_b",
          "lambda_q1", "lambda_k1", "lambda_q2", "lambda_k2", "g_sub_a", "w_out_a", "w_out_b", "w_o"]
OUTPUTS = [("y_prompt", (1, SEQ, D)), ("y_sample", (NB, NT, D)),
           ("k_a_prompt", (1, 1, SEQ, 2, HA, DH)), ("v_a_prompt", (1, 1, SEQ, HA, DVA)),
           ("k_b_prompt", (1, 1, SEQ, HB, DH)), ("v_b_prompt", (1, 1, SEQ, HB, DH)),
           ("logf_prompt", (1, 1, SEQ, HB)),
           ("k_a_sample", (1, NB, NT, 2, HA, DH)), ("v_a_sample", (1, NB, NT, HA, DVA)),
           ("k_b_sample", (1, NB, NT, HB, DH)), ("v_b_sample", (1, NB, NT, HB, DH)),
           ("logf_sample", (1, NB, NT, HB))]


def declare(nc, arrays):
    t = {n: nc.dram_tensor(f"in_{n}", a.shape, mybir.dt.from_np(a.dtype), kind="ExternalInput").ap()
         for n, a in arrays.items()}
    for name, shape in OUTPUTS:
        ap = nc.dram_tensor(f"out_{name}", shape, F32, kind="ExternalOutput").ap()
        rows = SEQ if name.endswith("prompt") else SR
        letters = "abcdef"[:len(shape)]
        lead = 2 if name[0] == "y" else 3
        t[name] = ap.rearrange(f"{' '.join(letters)} -> ({' '.join(letters[:lead])}) ({' '.join(letters[lead:])})")
        assert t[name].shape[0] == rows
    return t


def kernel(**inputs):
    import concourse.bacc as bacc
    from concourse.bass_utils import run_bass_kernel_spmd

    nc = bacc.Bacc("TRN2", target_bir_lowering=False, num_devices=1)
    arrays = {n: np.ascontiguousarray(inputs[n]) for n in INPUTS}
    program(nc, declare(nc, arrays))
    r = run_bass_kernel_spmd(nc, [{f"in_{n}": a for n, a in arrays.items()}], core_ids=[0])
    return tuple(r.results[0][f"out_{n}"] for n, _ in OUTPUTS)
```
